# Optimizing a Trainium2 kernel written in Bass

```python
import math
import jax
import jax.numpy as jnp
from jax import lax
import numpy as np

D_MODEL = 1024
BATCH = 1
SEQ = 128
DEPTH = 1
DEC_BATCH = 1
DEC_SEQ = 512
PAST_LEN = 128

GRID_W = 64
H_A = D_MODEL // 128
DK_A = 64
DV_A = 64
H_B = D_MODEL // 256
DQK_B = 64
DV_B = 128
A_QK = H_A * DK_A
A_V = H_A * DV_A
B_QK = H_B * 2 * DQK_B
B_V = H_B * DV_B
MIX_WIDTH = A_V + B_V
IN_SIZES = (A_QK, A_QK, A_V, A_V, 2 * H_A, 2 * H_A, B_QK, B_QK, B_V)
IN_COLS = 2 * A_QK + 2 * A_V + 4 * H_A + 2 * B_QK + B_V
CONV_K = 5
CHUNK = 64
Q_BLOCK = 128
D_FF = ((8 * D_MODEL // 3 + 127) // 128) * 128
N_MOD = 9
ROPE_THETA = 10000.0
ROPE_AXIS_DIM = DQK_B // 2
ROPE_PAIRS = ROPE_AXIS_DIM // 2
EPS = 1e-6

kernel_name = 'hybrid_deltanet_diffattn_prefix_dit_step'

def rmsnorm(x, gain):
    xf = x.astype(jnp.float32)
    y = xf * lax.rsqrt(jnp.mean(xf * xf, axis=-1, keepdims=True) + EPS)
    return (y * gain.astype(jnp.float32)).astype(x.dtype)

def l2norm(x):
    xf = x.astype(jnp.float32)
    return xf * lax.rsqrt(jnp.sum(xf * xf, axis=-1, keepdims=True) + EPS)

def adaln(cond, w_ada, b_ada):
    m = jax.nn.silu(cond) @ w_ada + b_ada
    return m.reshape(cond.shape[:-1] + (1, N_MOD, D_MODEL))

def modulated_norm(x, gain, shift, scale):
    return rmsnorm(x, gain) * (1 + scale) + shift

def swiglu(h, w_in, w_out):
    gate, up = jnp.split(h @ w_in, 2, axis=-1)
    return (jax.nn.silu(gate) * up) @ w_out

def split_cols(z, sizes):
    out, start = [], 0
    for s in sizes:
        out.append(z[..., start:start + s])
        start += s
    return out

def centred_dwconv(x, w):
    return lax.conv_general_dilated(
        x, w[:, None, :].astype(x.dtype), window_strides=(1,),
        padding=[(CONV_K // 2, CONV_K // 2)],
        dimension_numbers=('NWC', 'WIO', 'NWC'), feature_group_count=x.shape[-1])

def axial_rope(x):
    length = x.shape[1]
    n_rows = length // GRID_W
    pos_row = jnp.repeat(jnp.arange(n_rows), GRID_W).astype(jnp.float32)
    pos_col = jnp.tile(jnp.arange(GRID_W), n_rows).astype(jnp.float32)
    inv = ROPE_THETA ** (-jnp.arange(ROPE_PAIRS, dtype=jnp.float32) / ROPE_PAIRS)

    def rot(v, pos):
        ang = pos[:, None] * inv
        cos = jnp.cos(ang)[None, :, None, None, :]
        sin = jnp.sin(ang)[None, :, None, None, :]
        v1, v2 = v[..., :ROPE_PAIRS], v[..., ROPE_PAIRS:]
        return jnp.concatenate([v1 * cos - v2 * sin, v2 * cos + v1 * sin], axis=-1)

    xf = x.astype(jnp.float32)
    out = jnp.concatenate([rot(xf[..., :ROPE_AXIS_DIM], pos_row), rot(xf[..., ROPE_AXIS_DIM:], pos_col)], axis=-1)
    return out.astype(x.dtype)

def diff_attention(q, k, v, lam):
    bsz, lq = q.shape[0], q.shape[1]
    nb = lq // Q_BLOCK
    qb = jnp.moveaxis(q.reshape((bsz, nb, Q_BLOCK) + q.shape[2:]), 1, 0)
    scale = DQK_B ** -0.5

    def one_block(qblk):
        s = jnp.einsum('bqhmd,bkhmd->bhmqk', qblk, k).astype(jnp.float32) * scale
        p = jax.nn.softmax(s, axis=-1)
        a = p[:, :, 0] - lam * p[:, :, 1]
        return jnp.einsum('bhqk,bkhe->bqhe', a.astype(v.dtype), v)

    o = lax.map(one_block, qb)
    return jnp.moveaxis(o, 0, 1).reshape((bsz, lq) + o.shape[3:])

def gated_delta_chunked(q, k, v, g, beta, s0):
    bsz, length, nh, dk = q.shape
    dv = v.shape[-1]
    n = length // CHUNK

    def blocks(t):
        t = t.reshape((bsz, n, CHUNK, nh) + t.shape[3:])
        return jnp.moveaxis(t, 3, 1)

    qc = blocks(q) * (dk ** -0.5)
    kc = blocks(k)
    vc = blocks(v)
    gc = jnp.cumsum(blocks(g), axis=-1)
    bc = blocks(beta)
    idx = jnp.arange(CHUNK)
    incl = idx[:, None] >= idx[None, :]
    strict = idx[:, None] > idx[None, :]
    decay = jnp.exp(jnp.where(incl, gc[..., :, None] - gc[..., None, :], -jnp.inf))
    kk = jnp.einsum('bhncd,bhnsd->bhncs', kc, kc)
    a_mat = jnp.where(strict, bc[..., :, None] * kk * decay, 0.0) + jnp.eye(CHUNK, dtype=jnp.float32)
    rhs = jnp.concatenate([bc[..., None] * vc, (bc * jnp.exp(gc))[..., None] * kc], axis=-1)
    sol = lax.linalg.triangular_solve(a_mat, rhs, left_side=True, lower=True, unit_diagonal=True)
    u0, w = sol[..., :dv], sol[..., dv:]
    qk = jnp.where(incl, jnp.einsum('bhncd,bhnsd->bhncs', qc, kc) * decay, 0.0)
    qg = qc * jnp.exp(gc)[..., None]
    kg = kc * jnp.exp(gc[..., -1:] - gc)[..., None]
    glast = jnp.exp(gc[..., -1])
    xs = (jnp.moveaxis(qg, 2, 0), jnp.moveaxis(kg, 2, 0), jnp.moveaxis(u0, 2, 0),
          jnp.moveaxis(w, 2, 0), jnp.moveaxis(qk, 2, 0), jnp.moveaxis(glast, 2, 0))

    def step(state, inp):
        qg_n, kg_n, u0_n, w_n, qk_n, gl_n = inp
        u = u0_n - jnp.einsum('bhcd,bhde->bhce', w_n, state)
        o = jnp.einsum('bhcd,bhde->bhce', qg_n, state) + jnp.einsum('bhcs,bhse->bhce', qk_n, u)
        state = state * gl_n[..., None, None] + jnp.einsum('bhcd,bhce->bhde', kg_n, u)
        return state, o

    s_final, o = lax.scan(step, s0, xs)
    o = jnp.moveaxis(jnp.moveaxis(o, 0, 2), 1, 3).reshape(bsz, length, nh, dv)
    return o, s_final

def mixer(h, lp, lam_init, ctx_k, ctx_v, s0):
    bsz, length, _ = h.shape
    aq, ak, av, az, a_dec, a_beta, bq, bk, bv = split_cols(h @ lp['w_in'], IN_SIZES)

    qkv = jax.nn.silu(centred_dwconv(jnp.concatenate([aq, ak, av], axis=-1), lp['conv_w']))
    aq, ak, av = jnp.split(qkv, [A_QK, 2 * A_QK], axis=-1)
    qa = l2norm(aq.reshape(bsz, length, H_A, DK_A))
    ka = l2norm(ak.reshape(bsz, length, H_A, DK_A))
    va = av.reshape(bsz, length, H_A, DV_A).astype(jnp.float32)
    a_dec = a_dec.reshape(bsz, length, 2, H_A).astype(jnp.float32)
    g = -jnp.exp(lp['a_log'].astype(jnp.float32)) * jax.nn.softplus(a_dec + lp['dt_bias'].astype(jnp.float32))
    beta = jax.nn.sigmoid(a_beta.reshape(bsz, length, 2, H_A).astype(jnp.float32))
    if s0 is None:
        s0 = jnp.zeros((bsz, 2, H_A, DK_A, DV_A), jnp.float32)
    s0 = s0.astype(jnp.float32)
    o_f, s_f = gated_delta_chunked(qa, ka, va, g[:, :, 0], beta[:, :, 0], s0[:, 0])
    o_b, s_b = gated_delta_chunked(qa[:, ::-1], ka[:, ::-1], va[:, ::-1],
                                   g[:, ::-1, 1], beta[:, ::-1, 1], s0[:, 1])
    o_a = rmsnorm(o_f + o_b[:, ::-1], lp['delta_norm'])
    o_a = (o_a * jax.nn.silu(az.reshape(bsz, length, H_A, DV_A).astype(jnp.float32))).astype(h.dtype)
    state = jnp.stack([s_f, s_b], axis=1).astype(h.dtype)

    qb = bq.reshape(bsz, length, H_B, 2, DQK_B)
    kb = bk.reshape(bsz, length, H_B, 2, DQK_B)
    vb = bv.reshape(bsz, length, H_B, DV_B)
    f32 = jnp.float32
    lam = (jnp.exp(jnp.sum(lp['lambda_q1'].astype(f32) * lp['lambda_k1'].astype(f32)))
           - jnp.exp(jnp.sum(lp['lambda_q2'].astype(f32) * lp['lambda_k2'].astype(f32))) + lam_init)
    if ctx_k is None:
        o_b_att = diff_attention(qb, kb, vb, lam)
    else:
        keys = jnp.concatenate([ctx_k.astype(kb.dtype), axial_rope(kb)], axis=1)
        vals = jnp.concatenate([ctx_v.astype(vb.dtype), vb], axis=1)
        o_b_att = diff_attention(axial_rope(qb), keys, vals, lam)
    o_b_att = rmsnorm(o_b_att, lp['diff_norm']) * (1 - lam_init)

    y = jnp.concatenate([o_a.reshape(bsz, length, A_V), o_b_att.reshape(bsz, length, B_V)], axis=-1) @ lp['w_out']
    return y, (kb, vb, state)

def trunk_layer(x, mod, lp, lam_init, ctx_k, ctx_v, s0):
    x = x + 0.5 * mod[..., 2, :] * swiglu(modulated_norm(x, lp['norm_ffn1'], mod[..., 0, :], mod[..., 1, :]),
                                          lp['w_ffn1_in'], lp['w_ffn1_out'])
    h = modulated_norm(x, lp['norm_mix'], mod[..., 3, :], mod[..., 4, :])
    y, ctx_tensors = mixer(h, lp, lam_init, ctx_k, ctx_v, s0)
    x = x + mod[..., 5, :] * y
    x = x + 0.5 * mod[..., 8, :] * swiglu(modulated_norm(x, lp['norm_ffn2'], mod[..., 6, :], mod[..., 7, :]),
                                          lp['w_ffn2_in'], lp['w_ffn2_out'])
    return x, ctx_tensors

def setup_inputs(seed: int = 0) -> dict:
    key = jax.random.key(seed)
    ks = jax.random.split(key, 28)
    f32 = jnp.float32

    def nrm(k, shape, scale=1.0):
        return jax.random.normal(k, shape, f32) * scale

    def gain(k, shape):
        return 1.0 + 0.02 * jax.random.normal(k, shape, f32)

    dt = jnp.exp(jax.random.uniform(ks[16], (DEPTH, 2, H_A), f32, math.log(1e-3), math.log(1e-1)))
    return {
        'x_prompt': nrm(ks[0], (BATCH, SEQ, D_MODEL)),
        'x_sample': nrm(ks[1], (DEC_BATCH, DEC_SEQ, D_MODEL)),
        'cache_diff_k': nrm(ks[2], (DEC_BATCH, DEPTH, PAST_LEN, H_B, 2, DQK_B)),
        'cache_diff_v': nrm(ks[3], (DEC_BATCH, DEPTH, PAST_LEN, H_B, DV_B)),
        'state_delta': nrm(ks[4], (DEC_BATCH, DEPTH, 2, H_A, DK_A, DV_A), 0.1),
        'c': nrm(ks[5], (DEC_BATCH, D_MODEL)),
        'c_ctx': nrm(ks[6], (D_MODEL,)),
        'w_ada': nrm(ks[7], (DEPTH, D_MODEL, N_MOD * D_MODEL), 0.5 * D_MODEL ** -0.5),
        'b_ada': nrm(ks[8], (DEPTH, N_MOD * D_MODEL), 0.02),
        'norm_ffn1': gain(ks[9], (DEPTH, D_MODEL)),
        'w_ffn1_in': nrm(ks[10], (DEPTH, D_MODEL, 2 * D_FF), D_MODEL ** -0.5),
        'w_ffn1_out': nrm(ks[11], (DEPTH, D_FF, D_MODEL), D_FF ** -0.5),
        'norm_mix': gain(ks[12], (DEPTH, D_MODEL)),
        'w_in': nrm(ks[13], (DEPTH, D_MODEL, IN_COLS), D_MODEL ** -0.5),
        'conv_w': nrm(ks[14], (DEPTH, CONV_K, 2 * A_QK + A_V), CONV_K ** -0.5),
        'a_log': jnp.log(jax.random.uniform(ks[15], (DEPTH, 2, H_A), f32, 1.0, 16.0)),
        'dt_bias': dt + jnp.log(-jnp.expm1(-dt)),
        'delta_norm': gain(ks[17], (DEPTH, DV_A)),
        'lambda_q1': nrm(ks[18], (DEPTH, DQK_B), 0.1),
        'lambda_k1': nrm(ks[19], (DEPTH, DQK_B), 0.1),
        'lambda_q2': nrm(ks[20], (DEPTH, DQK_B), 0.1),
        'lambda_k2': nrm(ks[21], (DEPTH, DQK_B), 0.1),
        'diff_norm': gain(ks[22], (DEPTH, DV_B)),
        'w_out': nrm(ks[23], (DEPTH, MIX_WIDTH, D_MODEL), MIX_WIDTH ** -0.5),
        'norm_ffn2': gain(ks[24], (DEPTH, D_MODEL)),
        'w_ffn2_in': nrm(ks[25], (DEPTH, D_MODEL, 2 * D_FF), D_MODEL ** -0.5),
        'w_ffn2_out': nrm(ks[26], (DEPTH, D_FF, D_MODEL), D_FF ** -0.5),
        'norm_final': gain(ks[27], (D_MODEL,)),
    }

def reference(x_prompt, x_sample, cache_diff_k, cache_diff_v, state_delta, c, c_ctx,
              w_ada, b_ada, norm_ffn1, w_ffn1_in, w_ffn1_out, norm_mix, w_in, conv_w,
              a_log, dt_bias, delta_norm, lambda_q1, lambda_k1, lambda_q2, lambda_k2,
              diff_norm, w_out, norm_ffn2, w_ffn2_in, w_ffn2_out, norm_final):
    xp = x_prompt
    xs = x_sample
    new_k, new_v, new_s = [], [], []
    for l in range(DEPTH):
        lam_init = 0.8 - 0.6 * math.exp(-0.3 * l)
        lp = {
            'norm_ffn1': norm_ffn1[l], 'w_ffn1_in': w_ffn1_in[l], 'w_ffn1_out': w_ffn1_out[l],
            'norm_mix': norm_mix[l], 'w_in': w_in[l], 'conv_w': conv_w[l],
            'a_log': a_log[l], 'dt_bias': dt_bias[l], 'delta_norm': delta_norm[l],
            'lambda_q1': lambda_q1[l], 'lambda_k1': lambda_k1[l],
            'lambda_q2': lambda_q2[l], 'lambda_k2': lambda_k2[l],
            'diff_norm': diff_norm[l], 'w_out': w_out[l],
            'norm_ffn2': norm_ffn2[l], 'w_ffn2_in': w_ffn2_in[l], 'w_ffn2_out': w_ffn2_out[l],
        }
        xp, (k_ctx, v_ctx, s_ctx) = trunk_layer(xp, adaln(c_ctx, w_ada[l], b_ada[l]), lp, lam_init,
                                                None, None, None)
        new_k.append(k_ctx)
        new_v.append(v_ctx)
        new_s.append(s_ctx)
        xs, _ = trunk_layer(xs, adaln(c, w_ada[l], b_ada[l]), lp, lam_init,
                            cache_diff_k[:, l], cache_diff_v[:, l], state_delta[:, l])
    y_prompt = rmsnorm(xp, norm_final)
    y_sample = rmsnorm(xs, norm_final)
    new_diff_k = jnp.stack(new_k, axis=1)
    new_diff_v = jnp.stack(new_v, axis=1)
    new_state_delta = jnp.stack(new_s, axis=1)
    return (y_prompt, y_sample, new_diff_k, new_diff_v, new_state_delta)


_drawn_inputs = setup_inputs


def setup_inputs(seed=0):
    import zlib

    import numpy as np

    out = dict(_drawn_inputs(seed))
    spreads = {}
    factors = {'state_delta': 4.348,
     'norm_ffn1': 8.0,
     'delta_norm': 64.0,
     'lambda_q1': 2.699,
     'lambda_q2': 8.0,
     'lambda_k2': 7.551,
     'diff_norm': 64.0,
     'norm_ffn2': 23.309,
     'norm_final': 9.684}
    for name, (base, spread) in spreads.items():
        noise = np.random.default_rng([zlib.crc32(name.encode()), seed]).standard_normal(out[name].shape)
        drawn = base * np.exp(spread * noise) if base else spread * noise
        out[name] = jnp.asarray(drawn.astype(out[name].dtype))
    for name, factor in factors.items():
        out[name] = (out[name] * factor).astype(out[name].dtype)
    return out
```

```python
import math
from contextlib import ExitStack

import numpy as np
import concourse.bass as bass
from concourse import mybir

F32 = mybir.dt.float32
F32R = mybir.dt.float32r
ALU = mybir.AluOpType
ACT = mybir.ActivationFunctionType
AX = mybir.AxisListType

P = 128
D = 1024
KD = D // P
TC, TS = 128, 512
T = TC + TS
NT = T // P
HT = T // 2
DFF = 2816
NJ = DFF // P
HA, DK = 8, 64
HB = 4
NMOD = 9
CONV = 5
EPS = 1e-6
LAM_INIT = 0.8 - 0.6 * math.exp(-0.3 * 0)
LEVELS = [1, 2, 4, 8, 16, 32, 64]
COL_DEC = 2048
NDB = 4 * HA
COL_B = COL_DEC + NDB
SEGS = [(0, 0, 0, 0, TC), (1, 0, TC, TC, HT - TC), (1, 1, 0, HT, HT)]
ATT_UNITS = [(hb, 0, TC) for hb in range(HB)] + [(hb, q, P + TS) for hb in range(HB) for q in range(TC, T, P)]
NU = len(ATT_UNITS)
PE_T, DVE_T, ACT_T, POOL_T = 23, 15, 7, 3
PE_C, DVE_C = 3, 5


def tile_of(step, d):
    return step if d == 0 else (0 if step == 0 else NT - step)


def pick(x, j, *rest):
    if isinstance(j, int):
        return x[(slice(None), j) + rest]
    return x[(slice(None), bass.ds(j, 1)) + (rest or (slice(None),))].rearrange("p a b -> p (a b)")


def halves(x):
    return x.rearrange("p (a b) -> p a b", a=2)


def heads4(x, n):
    return x.rearrange("p (h n) -> p h n", n=n)


def spread(x, n):
    return x[:, :, None].broadcast_to([x.shape[0], x.shape[1], n])


N_IN, N_OUT = 2 * NJ, NJ
FFN_TILES = N_IN + N_OUT
TILE_FFN = [0, FFN_TILES + 28 + 8]
TILE_WIN = FFN_TILES
TILE_WBV = TILE_WIN + 24
TILE_WOUT = TILE_WIN + 28
N_TILES = TILE_FFN[1] + FFN_TILES

CONST_NAMES = ["ident", "perm", "headones", "tri_f", "tri_b"]


def shape_constants():
    i = np.arange(P)
    ident = np.eye(P)
    perm = np.zeros((P, P))
    perm[i ^ 16, i] = 1.0
    headones = (i[:, None] // DK == i[None, :] // DK) * 1.0
    tri_f = (i[:, None] <= i[None, :]) * 1.0
    tri_b = (i[:, None] >= i[None, :]) * 1.0
    low, up = [], []
    for b in LEVELS:
        same = i[:, None] // (2 * b) == i[None, :] // (2 * b)
        second = (i // b) % 2 == 1
        low.append((same & second[:, None] & ~second[None, :]) * 1.0)
        up.append((same & ~second[:, None] & second[None, :]) * 1.0)
    n = np.arange(TS)
    d = i % DK
    pos = np.where((d // 32)[:, None] == 0, (n // 64)[None, :], (n % 64)[None, :]).astype(np.float32)
    inv = (np.float32(10000.0) ** (-(d % 16).astype(np.float32) / np.float32(16))).astype(np.float32)
    ang = (pos * inv[:, None]).astype(np.float32)
    sign = np.where(d % 32 < 16, -1.0, 1.0)[:, None]
    small = np.concatenate([ident, perm, headones, tri_f, tri_b] + low + up, 1).astype(np.float32)
    rope = np.concatenate([np.cos(ang), np.sin(ang) * sign], 1).astype(np.float32)
    return small, rope


N_SMALL = (5 + 2 * len(LEVELS)) * P


class Chain:

    def __init__(self, eng, sem):
        self.eng, self.sem, self.n, self.reg, self.m = eng, sem, 0, None, 0

    def link(self, ins):
        ins.then_inc(self.sem, 1)
        self.m += 1
        at = self.n + self.m
        self.eng.wait_ge(self.sem, at if self.reg is None else self.reg + at)

    def loop(self, i, per):
        self.n, self.m = self.n + self.m, 0
        self.reg, self.per = i * per, per

    def done(self, iters):
        assert self.m == self.per, (self.m, self.per)
        self.n, self.m, self.reg = self.n + iters * self.per, 0, None


def hybrid_step(nc, x_prompt, x_sample, cache_diff_k, cache_diff_v, state_delta, c, c_ctx, w_ada, b_ada,
                norm_ffn1, w_ffn1_in, w_ffn1_out, norm_mix, w_in, conv_w, a_log, dt_bias, delta_norm,
                lambda_q1, lambda_k1, lambda_q2, lambda_k2, diff_norm, w_out, norm_ffn2, w_ffn2_in,
                w_ffn2_out, norm_final, consts, rope, y_prompt, y_sample, new_k, new_v, new_state):
    ctx = ExitStack()
    with ctx:
        def sem(name):
            return ctx.enter_context(nc.semaphore(name))

        def holder(stack):
            return lambda name, shape, dt=F32: stack.enter_context(nc.sbuf_tensor(name, shape, dt))

        sb = holder(ctx)
        x_t = sb("x_t", [P, KD, T])
        w_raw = [sb(f"w_raw{i}", [P, D]) for i in range(2)]
        w_hi = [sb(f"w_hi{i}", [P, D], F32R) for i in range(2)]
        w_lo = [sb(f"w_lo{i}", [P, D], F32R) for i in range(2)]
        h_hi = sb("h_hi", [P, KD, T], F32R)
        h_lo = sb("h_lo", [P, KD, T], F32R)
        ident = sb("ident", [P, P])
        ones_d = sb("ones_d", [P, P])
        cols_a = sb("cols_a", [P, 120])
        cols_b = sb("cols_b", [P, 62])
        mods = sb("mods", [P, NMOD * KD, 2])
        scales = sb("scales", [P, 3, KD, 2])
        rstd = sb("rstd", [P, T])
        sumsq = sb("sumsq", [P, T])
        square = [sb(f"square{i}", [P, T]) for i in range(2)]
        scratch = [sb(f"scratch{i}", [P, T]) for i in range(2)]
        silu_g, act_f = square, scratch

        with ExitStack() as s:
            tb = holder(s)
            x_tok = tb("x_tok", [P, NT, D])
            ada_ring = [tb(f"ada_ring{i}", [P, D]) for i in range(8)]
            rows_a = tb("rows_a", [120, P])
            rows_b = tb("rows_b", [62, P])
            cond = tb("cond", [P, KD, 2])
        with ExitStack() as s:
            tb = holder(s)
            act_hi = tb("act_hi", [P, NJ, T], F32R)
            act_lo = tb("act_lo", [P, NJ, T], F32R)
        with ExitStack() as s:
            y_tok = holder(s)("y_tok", [P, NT, D])
        mb = holder(ctx.enter_context(ExitStack()))
        cst = mb("cst", [P, N_SMALL])
        pre = mb("pre", [P, 12, T + 6])
        z_t = mb("z_t", [P, HB, T])
        vecs = mb("vecs", [P, 3, 16])
        ones_1 = mb("ones_1", [P, P])
        g_t, beta, gc, egc, ekg, gl, sp_a, sp_b = [
            mb(n, [P, NT, 16]) for n in ("g_t", "beta", "gc", "egc", "ekg", "gl", "sp_a", "sp_b")]
        dn_col = mb("dn_col", [P, 1])
        with ExitStack() as s:
            tb = holder(s)
            rope_sb = tb("rope_sb", [P, 2 * TS])
            gate_w = tb("gate_w", [P, KD * NDB])
            gate_hi = tb("gate_hi", [P, KD * NDB], F32R)
            gate_lo = tb("gate_lo", [P, KD * NDB], F32R)
            conv_acc = [tb(f"conv_acc{i}", [P, T + 2]) for i in range(2)]
            q_b = tb("q_b", [P, HB, T])
            k_b = tb("k_b", [P, HB, T])
            k_all = tb("k_all", [P, HB, T])
            v_b = tb("v_b", [P, NT, HB * P])
            ck_tok = tb("ck_tok", [P, HB * P])
            cv_tok = tb("cv_tok", [P, HB * P])
            lam_in = tb("lam_in", [P, 4, DK])
            lam_t = tb("lam_t", [P, 8])
            att_s = tb("att_s", [P, 2, 8])
            att_v = tb("att_v", [P, T])
            att_wt = tb("att_wt", [P, T])
            nk_tok = tb("nk_tok", [P, HB * P])
            att_p = conv_acc
            att_w = sumsq
            att_q = q_b
        with ExitStack() as s:
            tb = holder(s)
            k_tok = tb("k_tok", [P, NT, HA * DK])
            v_tok = tb("v_tok", [P, NT, HA * DK])
            o_acc = pre[:, 8:12, :].rearrange("p a b -> p (a b)")[:, 0:NT * HA * DK].rearrange("p (t n) -> p t n", t=NT)
            st = [tb(f"st{i}", [P, 2, 4, P]) for i in range(2)]
            e_x = [tb(f"e_x{i}", [P, 4, P]) for i in range(4)]
            m_t = [tb(f"m_t{i}", [P, 4, P]) for i in range(4)]
            t_t = [tb(f"t_t{i}", [P, 4, P]) for i in range(4)]
            t_n = [tb(f"t_n{i}", [P, 4, P]) for i in range(4)]
            p_t = [tb(f"p_t{i}", [P, 4, P]) for i in range(4)]
            kg = [square[i // 2][:, (i % 2) * 256:(i % 2) * 256 + 256] for i in range(4)]
            r_s = [t_n[i][:, 0:2, :].rearrange("p a b -> p (a b)") for i in range(4)]
            u_s = [t_n[i][:, 2:4, :].rearrange("p a b -> p (a b)") for i in range(4)]
            oq = [e_x[i][:, 0:2, :].rearrange("p a b -> p (a b)") for i in range(4)]
            o_sum = tb("o_sum", [P, NT, HA])
        ps = ctx.enter_context(nc.psum_tensor("ps", [P, 8, 512], F32))

        def const(name):
            i = CONST_NAMES.index(name)
            return cst[:, i * P:(i + 1) * P]

        def mask(d, n, transposed):
            i = 5 + n + (len(LEVELS) if (d == 0) == transposed else 0)
            return cst[:, i * P:(i + 1) * P]

        def over4(x):
            return x[:, None, :].broadcast_to([P, 4, P])

        w_landed = [sem(f"w_landed{i}") for i in range(2)]
        w_hi_ready, w_lo_ready, tile_done = sem("w_hi_ready"), sem("w_lo_ready"), sem("tile_done")
        small_in, x_in = sem("small_in"), sem("x_in")
        ada_landed = [sem(f"ada_landed{i}") for i in range(8)]
        ada_used, mods_ready, ones_set = sem("ada_used"), sem("mods_ready"), sem("ones_set")
        cols_turned, cols_ready, cond_ready = sem("cols_turned"), sem("cols_ready"), sem("cond_ready")
        x_turned, x_copied = sem("x_turned"), sem("x_copied")
        dve_own, act_own, pool_own = sem("dve_own"), sem("act_own"), sem("pool_own")
        sq_ready, sq_added, x_updated = sem("sq_ready"), sem("sq_added"), sem("x_updated")
        mean_mm, var_ready, sd_ready = sem("mean_mm"), sem("var_ready"), sem("sd_ready")
        hn_ready, hhi_ready, h_ready = sem("hn_ready"), sem("hhi_ready"), sem("h_ready")
        silu_ready, act_ready, acthi_ready, actlo_ready = (sem("silu_ready"), sem("act_ready"),
                                                           sem("acthi_ready"), sem("actlo_ready"))
        mix_in, proj_out, conv_ready, conv_silu = sem("mix_in"), sem("proj_out"), sem("conv_ready"), sem("conv_silu")
        pads_set, gate_split, gate_mm, vb_ready = sem("pads_set"), sem("gate_split"), sem("gate_mm"), sem("vb_ready")
        sc_pe, sc_act, sc_dve = sem("scalars_pe"), sem("scalars_act"), sem("scalars_dve")
        l2_sq, l2_mm, l2_var, l2_sd, l2_done = [sem("l2_" + n) for n in ("sq", "mm", "var", "sd", "done")]
        rot_mm, rot_cos, rot_done = sem("rot_mm"), sem("rot_cos"), sem("rot_done")
        kt_turned, kt_copied = sem("kt_turned"), sem("kt_copied")
        s_mm, s_max, s_exp, s_wts, s_turn, s_turned, s_pv, s_out = [
            sem("att_" + n) for n in ("scores", "max", "exp", "weights", "turn", "turned", "pv", "out")]
        an_sq, an_mm, an_var, an_sd, an_tmp, an_hi, an_done = [
            sem("att_norm_" + n) for n in ("sq", "mm", "var", "sd", "tmp", "hi", "done")]
        kv_out, st_out, st_in, st_clear, y_out = sem("kv_out"), sem("st_out"), sem("st_in"), sem("st_clear"), sem("y_out")
        kv_turned, kv_copied = sem("kv_turned"), sem("kv_copied")
        t_pe, t_dve, t_act, t_pool, c_pe, c_dve = [
            [sem(f"{n}{b}") for b in range(4)]
            for n in ("make_t_pe", "make_t_dve", "make_t_act", "make_t_pool", "scan_pe", "scan_dve")]
        o_pe, o_dve, o_act = sem("delta_out_pe"), sem("delta_out_dve"), sem("delta_out_act")
        y_scaled, y_turned, y_copied = sem("y_scaled"), sem("y_turned"), sem("y_copied")

        block = ctx.enter_context(nc.Block())
        X_BASE = [0, 16]
        SEQ = [1, 3]
        ffn_w = [(w_ffn1_in, w_ffn1_out), (w_ffn2_in, w_ffn2_out)]
        win = w_in[0].rearrange("(k p) n -> p k n", p=P)

        @block.sync
        def _(sp):
            rows = [(0, b_ada[0].rearrange("(m p) -> m p", p=P)), (72, c.rearrange("a (m p) -> (a m) p", p=P)),
                    (80, c_ctx.rearrange("(m p) -> m p", p=P)), (88, norm_ffn1[0].rearrange("(m p) -> m p", p=P)),
                    (96, norm_mix[0].rearrange("(m p) -> m p", p=P)),
                    (104, norm_ffn2[0].rearrange("(m p) -> m p", p=P)),
                    (112, norm_final.rearrange("(m p) -> m p", p=P))]
            sp.dma_start(ident[:], consts[:, 0:P]).then_inc(small_in, 16)
            for at, src in rows:
                sp.dma_start(rows_a[at:at + src.shape[0], :], src).then_inc(small_in, 16)
            sp.dma_start(rows_b[0:60, :], conv_w[0].rearrange("t (m p) -> (t m) p", p=P)).then_inc(small_in, 16)
            for k in range(2):
                sp.dma_start(rows_b[60:61, k * DK:(k + 1) * DK], delta_norm).then_inc(small_in, 16)
            sp.dma_start(rows_b[61:62, :], diff_norm).then_inc(small_in, 16)
            sp.dma_start(x_tok[:, 0, :], x_prompt[0]).then_inc(x_in, 16)
            sp.dma_start(x_tok[:, 1:NT, :], x_sample[0].rearrange("(t p) d -> p t d", p=P)).then_inc(x_in, 16)
            ada_v = w_ada[0].rearrange("(k p) n -> p k n", p=P)

            def ada_load(m, k):
                col = (m * D + k * P) if not isinstance(m, int) else m * D + k * P
                src = ada_v[:, :, col:col + P] if isinstance(col, int) else ada_v[:, :, bass.ds(col, P)]
                sp.dma_start(ada_ring[k][:].rearrange("p (k n) -> p k n", k=KD), src).then_inc(ada_landed[k], 16)

            for k in range(8):
                ada_load(0, k)
            with sp.Fori(0, NMOD - 1) as m:
                for k in range(8):
                    sp.wait_ge(ada_used, m * 8 + (k + 1))
                    ada_load(m + 1, k)

            def w_load(n, s, src, first=False):
                if not first:
                    sp.wait_ge(w_lo_ready, n - 1)
                sp.dma_start(w_raw[s][:].rearrange("p (a b) -> p a b", a=src.shape[1]), src)\
                    .then_inc(w_landed[s], 16)

            def ffn_loads(f):
                base = TILE_FFN[f]
                wi = ffn_w[f][0][0].rearrange("(k p) n -> p k n", p=P)
                wo = ffn_w[f][1][0].rearrange("(j p) n -> p j n", p=P)
                for k in range(2):
                    w_load(base + k, k, wi[:, :, k * DFF:k * DFF + P], first=(f == 0))
                with sp.Fori(0, NJ - 1) as j:
                    for k in range(2):
                        w_load(j * 2 + (base + 2 + k), k, wi[:, :, bass.ds(j * P + (k * DFF + P), P)])
                for hf in range(2):
                    n = base + N_IN + 11 * hf
                    cols = slice(hf * 512, hf * 512 + 512)
                    w_load(n, n % 2, wo[:, 0:2, cols])
                    with sp.Fori(0, 5) as i:
                        for k in range(2):
                            w_load(i * 2 + (n + 1 + k), (n + 1 + k) % 2, wo[:, bass.ds(i * 4 + (2 + 2 * k), 2), cols])

            ffn_loads(0)
            sp.wait_ge(tile_done, FFN_TILES)
            sp.dma_start(cst[:], consts).then_inc(mix_in, 16)
            sp.dma_start(rope_sb[:], rope).then_inc(mix_in, 16)
            sp.dma_start(gate_w[:].rearrange("p (k n) -> p k n", k=KD), win[:, :, COL_DEC:COL_DEC + NDB]).then_inc(mix_in, 16)
            sp.dma_start(vecs[:, 0, :], a_log.rearrange("a d h -> a (d h)").broadcast_to([P, 16])).then_inc(mix_in, 16)
            sp.dma_start(vecs[:, 1, :], dt_bias.rearrange("a d h -> a (d h)").broadcast_to([P, 16])).then_inc(mix_in, 16)
            for i, v in enumerate((lambda_q1, lambda_k1, lambda_q2, lambda_k2)):
                sp.dma_start(lam_in[:, i, :], v.broadcast_to([P, DK])).then_inc(mix_in, 16)
            sp.dma_start(ck_tok[:], cache_diff_k[0, 0].rearrange("t h m d -> t (h m d)")).then_inc(mix_in, 16)
            sp.dma_start(cv_tok[:], cache_diff_v[0, 0].rearrange("t h e -> t (h e)")).then_inc(mix_in, 16)
            for i0, iters, col in ((0, 8, 0), (16, 4, COL_B)):
                with sp.Fori(0, iters) as i:
                    for k in range(2):
                        w_load(i * 2 + (TILE_WIN + i0 + k), k, win[:, :, bass.ds(i * (2 * P) + (col + k * P), P)])
            for q in range(4):
                w_load(TILE_WBV + q, q % 2, win[:, 2 * q:2 * q + 2, COL_B + 1024:COL_B + 1536])
            wo = w_out[0].rearrange("(k p) n -> p k n", p=P)
            for m in range(2):
                w_load(TILE_WOUT + m, m % 2, wo[:, :, m * P:(m + 1) * P])
            sp.wait_ge(vb_ready, 1)
            sp.dma_start(new_v, v_b[:, 0, :]).then_inc(kv_out, 16)
            sp.wait_ge(kt_copied, 1)
            sp.dma_start(new_k, nk_tok[:]).then_inc(kv_out, 16)
            sp.wait_ge(st_clear, 3)
            for d in range(2):
                for e in range(2):
                    sp.dma_start(st[1][e * DK:(e + 1) * DK, d, :, e * DK:(e + 1) * DK],
                                 state_delta[0, 0, d].rearrange("(c e) k v -> e k c v", e=2)[e]).then_inc(st_in, 16)
            for b in range(4):
                sp.wait_ge(c_dve[b], DVE_C)
            for d in range(2):
                for e in range(2):
                    sp.dma_start(new_state[d].rearrange("(c e) k v -> e k c v", e=2)[e],
                                 st[0][e * DK:(e + 1) * DK, d, :, e * DK:(e + 1) * DK]).then_inc(st_out, 16)
            with sp.Fori(0, 3) as i:
                for k in range(2):
                    w_load(i * 2 + (TILE_WOUT + 2 + k), k, wo[:, :, bass.ds(i * (2 * P) + (2 + k) * P, P)])
            ffn_loads(1)
            for t in range(NT):
                sp.wait_ge(y_copied, 2 * (t + 1))
                dst = y_prompt[0] if t == 0 else y_sample[0, (t - 1) * P:t * P, :]
                sp.dma_start(dst, y_tok[:, t, :]).then_inc(y_out, 16)
            sp.wait_ge(y_out, 16 * NT)
            sp.wait_ge(kv_out, 32)
            sp.wait_ge(st_out, 64)

        @block.scalar
        def _(act):
            own = Chain(act, act_own)

            def w_high(n, s, first=False):
                act.wait_ge(w_landed[s], n * 8 + (16 - 8 * s))
                if not first:
                    act.wait_ge(tile_done, n - 1)
                nc.scalar.copy(w_hi[s][:], w_raw[s][:]).then_inc(w_hi_ready, 1)

            def square_of(k, seq, after):
                if after is not None:
                    act.wait_ge(x_updated, after + k + 1)
                if seq * 8 + k >= 2:
                    act.wait_ge(sq_added, seq * 8 + k - 1)
                nc.scalar.activation(square[k % 2][:], x_t[:, k, :], ACT.Square).then_inc(sq_ready, 1)

            def norm(seq):
                act.wait_ge(var_ready, seq + 1)
                nc.scalar.activation(rstd[:], rstd[:], ACT.Sqrt).then_inc(sd_ready, 1)

            def modulate(nth):
                for k in range(KD):
                    act.wait_ge(hn_ready, nth * 8 + k + 1)
                    nc.scalar.activation(h_hi[:, k, 0:TC], scratch[k % 2][:, 0:TC], ACT.Identity,
                                         bias=mods[:, 24 * nth + k, 0:1])
                    nc.scalar.activation(h_hi[:, k, TC:T], scratch[k % 2][:, TC:T], ACT.Identity,
                                         bias=mods[:, 24 * nth + k, 1:2]).then_inc(hhi_ready, 1)

            def ffn(f):
                base, J = TILE_FFN[f], NJ * f

                def hidden(j, par, first):
                    w_high(j * 2 + (base + 1), 1, first=(f == 0 and first and par == 0))
                    act.wait_ge(tile_done, j * 2 + (base + 1))
                    if not first:
                        act.wait_ge(act_ready, j + (J - 1))
                    nc.scalar.activation(halves(silu_g[par][:]), ps[:, 4 * par:4 * par + 2, 0:HT],
                                         ACT.Silu).then_inc(silu_ready, 1)
                    w_high(j * 2 + (base + 2), 0)
                    act.wait_ge(act_ready, j + (J + 1))
                    nc.scalar.copy(pick(act_hi, j), act_f[par][:]).then_inc(acthi_ready, 1)

                hidden(0, 0, True)
                hidden(1, 1, True)
                with act.Fori(0, NJ // 2 - 1) as i:
                    for k in range(2):
                        hidden(i * 2 + (2 + k), k, False)
                for hf in range(2):
                    n = base + N_IN + 11 * hf
                    with act.Fori(0, 5) as i:
                        for k in range(2):
                            w_high(i * 2 + (n + 1 + k), (n + 1 + k) % 2)
                    if n + 11 < N_TILES:
                        w_high(n + 11, (n + 11) % 2)
                    for k in range(4 * hf, 4 * hf + 4):
                        square_of(k, SEQ[f], X_BASE[f])

            act.wait_ge(cols_turned, 2)
            nc.scalar.copy(cols_a[:], ps[:, 0, 0:120]).then_inc(cols_ready, 1)
            nc.scalar.copy(cols_b[:], ps[:, 1, 0:62]).then_inc(cols_ready, 1)
            act.wait_ge(cols_ready, 2)
            nc.scalar.activation(cond[:, :, 1], cols_a[:, 72:80], ACT.Silu).then_inc(cond_ready, 1)
            nc.scalar.activation(cond[:, :, 0], cols_a[:, 80:88], ACT.Silu).then_inc(cond_ready, 1)
            for i in range(2 * NT):
                t, q = i // 2, i % 2
                act.wait_ge(x_turned, i + 1)
                nc.scalar.copy(x_t[:, 4 * q:4 * q + 4, t * P:(t + 1) * P], heads4(ps[:, 2 + i % 4, :], P)).then_inc(x_copied, 1)
            w_high(0, 0, first=True)
            act.wait_ge(x_copied, 2 * NT)
            for k in range(KD):
                square_of(k, 0, None)
            norm(0)
            modulate(0)
            ffn(0)
            norm(1)
            modulate(1)

            def to_conv(m, k):
                w_high(m + (TILE_WIN + 1), 1 - k)
                act.wait_ge(tile_done, m + (TILE_WIN + 1))
                for grp, half, col, tok, ln in SEGS:
                    a = 2 + tok + 2 * grp
                    ins = nc.scalar.copy(pick(pre, m, slice(a, a + ln)), ps[:, 2 * k + half, col:col + ln])
                ins.then_inc(proj_out, 1)

            def from_conv(m, k):
                act.wait_ge(conv_ready, m + 1)
                nc.scalar.activation(pick(pre, m, slice(0, TC)), conv_acc[k][:, 0:TC], ACT.Silu)
                nc.scalar.activation(pick(pre, m, slice(TC, T)), conv_acc[k][:, TC + 2:T + 2], ACT.Silu)\
                    .then_inc(conv_silu, 1)

            act.wait_ge(pads_set, 3)
            to_conv(0, 0)
            to_conv(1, 1)
            from_conv(0, 0)
            with act.Fori(0, 5) as i:
                for k in range(2):
                    to_conv(i * 2 + (2 + k), k)
                    from_conv(i * 2 + (1 + k), 1 - k)
            for m in range(12, 24):
                w_high(TILE_WIN + m + 1, (m + 1) % 2)
                if m == 12:
                    from_conv(11, 1)
                act.wait_ge(tile_done, TILE_WIN + m + 1)
                src = ps[:, 2 * (m % 2):2 * (m % 2) + 2, 0:HT]
                if m < 16:
                    nc.scalar.activation(halves(z_t[:, m - 12, :]), src, ACT.Silu).then_inc(proj_out, 1)
                else:
                    dst = q_b[:, m - 16, :] if m < 20 else k_b[:, m - 20, :]
                    nc.scalar.copy(halves(dst), src).then_inc(proj_out, 1)
            act.wait_ge(mix_in, 16 * 11)
            nc.scalar.copy(gate_hi[:], gate_w[:]).then_inc(gate_split, 1)
            for q in range(1, 5):
                w_high(TILE_WBV + q, q % 2)
            act.wait_ge(tile_done, TILE_WBV + 4)
            for t in range(NT):
                ins = nc.scalar.copy(v_b[:, t, :], ps[:, t, :])
            ins.then_inc(vb_ready, 1)

            act.wait_ge(sc_dve, 1)
            nc.scalar.activation(sp_a[:], sp_a[:], ACT.Exp, scale=-1.0).then_inc(sc_act, 1)
            nc.scalar.activation(beta[:], beta[:], ACT.Exp, scale=-1.0).then_inc(sc_act, 1)
            nc.scalar.activation(vecs[:, 2, :], vecs[:, 0, :], ACT.Exp).then_inc(sc_act, 1)
            nc.scalar.activation(lam_t[:, 2:4], lam_t[:, 0:2], ACT.Exp).then_inc(sc_act, 1)
            act.wait_ge(sc_dve, 2)
            nc.scalar.activation(sp_a[:], sp_a[:], ACT.Ln).then_inc(sc_act, 1)
            act.wait_ge(sc_dve, 4)
            nc.scalar.activation(egc[:], gc[:], ACT.Exp).then_inc(sc_act, 1)
            nc.scalar.activation(ekg[:], ekg[:], ACT.Exp).then_inc(sc_act, 1)
            nc.scalar.activation(gl[:], gl[:], ACT.Exp).then_inc(sc_act, 1)

            def l2_root(m):
                act.wait_ge(l2_var, m + 1)
                nc.scalar.activation(scratch[m % 2][:], scratch[m % 2][:], ACT.Sqrt).then_inc(l2_sd, 1)

            act.wait_ge(conv_silu, 12)
            for m in range(8):
                if m >= 2:
                    act.wait_ge(l2_mm, m - 1)
                nc.scalar.activation(square[m % 2][:], pre[:, m, 0:T], ACT.Square).then_inc(l2_sq, 1)
                if m >= 1:
                    l2_root(m - 1)
            l2_root(7)
            act.wait_ge(kt_turned, 2)
            nc.scalar.copy(nk_tok[:], ps[:, 6, :]).then_inc(kt_copied, 1)
            nc.scalar.copy(k_all[:, :, 0:P], heads4(ps[:, 7, :], P)).then_inc(kt_copied, 1)

            for v, (hb, q0, nk) in enumerate(ATT_UNITS):
                for m in range(2):
                    act.wait_ge(s_max, 2 * v + m + 1)
                    if m == 0 and v >= 1:
                        act.wait_ge(s_wts, v)
                    if m == 0 and v == 0:
                        act.wait_ge(rot_done, 8)
                    if nk == P:
                        src, dst = ps[:, 2 * m, 0:P], att_p[m][:, 0:P]
                    else:
                        src, dst = ps[:, 2 * m:2 * m + 2, 0:HT], halves(att_p[m][:, 0:T])
                    nc.scalar.activation(dst, src, ACT.Exp, bias=att_s[:, v % 2, m:m + 1], scale=DK ** -0.5,
                                         accum_out=att_s[:, v % 2, 2 + m:3 + m]).then_inc(s_exp, 1)
                act.wait_ge(s_turn, v + 1)
                if v >= 1:
                    act.wait_ge(s_pv, v)
                if nk == P:
                    nc.scalar.copy(att_wt[:, 0:P], ps[:, 4, 0:P]).then_inc(s_turned, 1)
                else:
                    nc.scalar.copy(att_wt[:, 0:512], ps[:, 4, :])
                    nc.scalar.copy(att_wt[:, 512:T], ps[:, 5, 0:P]).then_inc(s_turned, 1)
            act.wait_ge(s_out, NU)
            for hb in range(HB):
                if hb >= 1:
                    act.wait_ge(an_mm, hb)
                nc.scalar.activation(square[0][:], att_q[:, hb, :], ACT.Square).then_inc(an_sq, 1)
                act.wait_ge(an_var, hb + 1)
                nc.scalar.activation(rstd[:], rstd[:], ACT.Sqrt).then_inc(an_sd, 1)
                act.wait_ge(an_tmp, hb + 1)
                nc.scalar.copy(h_hi[:, 4 + hb, :], scratch[0][:]).then_inc(an_hi, 1)

            act.wait_ge(an_done, 4)
            act.wait_ge(kv_out, 32)
            for i in range(2 * NT):
                act.wait_ge(kv_turned, i + 1)
                nc.scalar.copy((k_tok, v_tok)[i % 2][:, i // 2, :], ps[:, 4 + i % 4, :]).then_inc(kv_copied, 1)
            for s in range(NT):
                for b in range(4):
                    act.wait_ge(t_dve[b], s * DVE_T + 1)
                    nc.scalar.activation(e_x[b][:], e_x[b][:], ACT.Exp).then_inc(t_act[b], 1)
                for n in range(6):
                    for b in range(4):
                        act.wait_ge(t_pe[b], s * PE_T + 6 + 3 * n)
                        nc.scalar.copy(t_n[b][:].rearrange("p a b -> p (a b)"), ps[:, b, :]).then_inc(t_act[b], 1)
            for t in range(NT):
                act.wait_ge(o_dve, 4 * t + 1)
                nc.scalar.activation(o_sum[:, t, :], o_sum[:, t, :], ACT.Sqrt).then_inc(o_act, 1)
                act.wait_ge(o_dve, 4 * t + 3)
                nc.scalar.copy(h_hi[:, 0:4, t * P:(t + 1) * P], heads4(scratch[0][:, 0:512], P)).then_inc(o_act, 1)
            for m in range(8):
                w_high(TILE_WOUT + m + 1, (m + 1) % 2)
                square_of(m, 2, 8)
            norm(2)
            modulate(2)
            act.wait_ge(st_out, 64)
            ffn(1)
            norm(3)
            for i in range(2 * NT):
                act.wait_ge(y_turned, i + 1)
                nc.scalar.copy(y_tok[:, i // 2, (i % 2) * 512:(i % 2) * 512 + 512], ps[:, i % 4, :]).then_inc(y_copied, 1)

        @block.vector
        def _(dve):
            own = Chain(dve, dve_own)

            def w_low(n, s):
                dve.wait_ge(w_hi_ready, n + 1)
                nc.vector.tensor_tensor(w_lo[s][:], w_raw[s][:], w_hi[s][:].bitcast(F32), ALU.subtract)\
                    .then_inc(w_lo_ready, 1)

            def norm(seq):
                dve.wait_ge(mean_mm, seq + 1)
                nc.vector.tensor_scalar(halves(rstd[:]), ps[:, 0:2, 0:HT], EPS, None, ALU.add).then_inc(var_ready, 1)
                dve.wait_ge(sd_ready, seq + 1)
                own.link(nc.vector.reciprocal(rstd[:], rstd[:]))

            def modulate(nth):
                def high(k):
                    if k >= 2:
                        dve.wait_ge(h_ready, nth * 8 + k - 1)
                    for grp, a, b in ((0, 0, TC), (1, TC, T)):
                        ins = nc.vector.scalar_tensor_tensor(scratch[k % 2][:, a:b], x_t[:, k, a:b],
                                                             scales[:, nth, k, grp:grp + 1], rstd[:, a:b],
                                                             op0=ALU.mult, op1=ALU.mult)
                    ins.then_inc(hn_ready, 1)

                def rest(k):
                    dve.wait_ge(hhi_ready, nth * 8 + k + 1)
                    for grp, a, b in ((0, 0, TC), (1, TC, T)):
                        ins = nc.vector.scalar_tensor_tensor(h_lo[:, k, a:b], scratch[k % 2][:, a:b],
                                                             mods[:, 24 * nth + k, grp:grp + 1],
                                                             h_hi[:, k, a:b].bitcast(F32),
                                                             op0=ALU.add, op1=ALU.subtract)
                    ins.then_inc(h_ready, 1)

                high(0)
                for k in range(KD):
                    if k + 1 < KD:
                        high(k + 1)
                    rest(k)

            def update_x(m, banks, gate):
                for grp, half, col, tok, ln in SEGS:
                    ins = nc.vector.scalar_tensor_tensor(x_t[:, m, tok:tok + ln], ps[:, banks + half, col:col + ln],
                                                         mods[:, gate * KD + m, grp:grp + 1], x_t[:, m, tok:tok + ln],
                                                         op0=ALU.mult, op1=ALU.add)
                ins.then_inc(x_updated, 1)

            def ffn(f):
                base, J = TILE_FFN[f], NJ * f

                def hidden(j, par):
                    w_low(j * 2 + (base + 1), 1)
                    w_low(j * 2 + (base + 2), 0)
                    dve.wait_ge(tile_done, j * 2 + (base + 2))
                    dve.wait_ge(silu_ready, j + (J + 1))
                    nc.vector.tensor_tensor(halves(act_f[par][:]), halves(silu_g[par][:]),
                                            ps[:, 4 * par + 2:4 * par + 4, 0:HT], ALU.mult).then_inc(act_ready, 1)
                    dve.wait_ge(acthi_ready, j + (J + 1))
                    nc.vector.tensor_tensor(pick(act_lo, j), act_f[par][:], pick(act_hi, j).bitcast(F32),
                                            ALU.subtract).then_inc(actlo_ready, 1)

                with dve.Fori(0, NJ // 2) as i:
                    for k in range(2):
                        hidden(i * 2 + k, k)
                for hf in range(2):
                    n = base + N_IN + 11 * hf
                    with dve.Fori(0, 5) as i:
                        for k in range(2):
                            w_low(i * 2 + (n + 1 + k), (n + 1 + k) % 2)
                    if n + 11 < N_TILES:
                        w_low(n + 11, (n + 11) % 2)
                    dve.wait_ge(tile_done, n + 11)
                    for mm in range(4):
                        update_x(4 * hf + mm, 2 * mm, 2 + 6 * f)

            nc.vector.memset(ones_d[:], 1.0 / D).then_inc(ones_set, 1)
            w_low(0, 0)
            dve.wait_ge(cols_ready, 2)
            dve.wait_ge(ada_used, NMOD * KD)
            own.link(nc.vector.tensor_tensor(mods[:], ps[:, 7, 0:2 * NMOD * KD].rearrange("p (m a) -> p m a", a=2),
                                             spread(cols_a[:, 0:72], 2), ALU.add))
            for nth in range(3):
                own.link(nc.vector.scalar_tensor_tensor(scales[:, nth], mods[:, 24 * nth + 8:24 * nth + 16, :], 1.0,
                                                        spread(cols_a[:, 88 + 8 * nth:96 + 8 * nth], 2),
                                                        op0=ALU.add, op1=ALU.mult))
            for gate in (2, 8):
                own.link(nc.vector.tensor_scalar(mods[:, gate * KD:gate * KD + 8, :], mods[:, gate * KD:gate * KD + 8, :],
                                                 0.5, None, ALU.mult))
            dve.wait_ge(x_copied, 2 * NT)
            norm(0)
            modulate(0)
            ffn(0)
            norm(1)
            modulate(1)

            def conv(m, k):
                w_low(m + (TILE_WIN + 1), 1 - k)
                dve.wait_ge(proj_out, m + 1)
                if not isinstance(m, int) or m >= 2:
                    dve.wait_ge(conv_silu, m - 1)
                tap = lambda t: cols_b[:, bass.ds(m + 12 * t, 1)] if not isinstance(m, int) else cols_b[:, m + 12 * t:m + 12 * t + 1]
                own.link(nc.vector.tensor_scalar(conv_acc[k][:], pick(pre, m, slice(0, T + 2)), tap(0), None, ALU.mult))
                for t in range(1, CONV):
                    ins = nc.vector.scalar_tensor_tensor(conv_acc[k][:], pick(pre, m, slice(t, t + T + 2)), tap(t),
                                                         conv_acc[k][:], op0=ALU.mult, op1=ALU.add)
                    if t < CONV - 1:
                        own.link(ins)
                ins.then_inc(conv_ready, 1)

            conv(0, 0)
            conv(1, 1)
            with dve.Fori(0, 5) as i:
                own.loop(i, 2 * (CONV - 1))
                for k in range(2):
                    conv(i * 2 + (2 + k), k)
                own.done(5)
            for m in range(12, 24):
                w_low(TILE_WIN + m + 1, (m + 1) % 2)
            dve.wait_ge(gate_split, 1)
            nc.vector.tensor_tensor(gate_lo[:], gate_w[:], gate_hi[:].bitcast(F32), ALU.subtract).then_inc(gate_split, 1)
            for q in range(1, 5):
                w_low(TILE_WBV + q, q % 2)

            dve.wait_ge(gate_mm, 1)
            raw = ps[:, 5, 0:NT * NDB].rearrange("p (t n) -> p t n", t=NT)
            own.link(nc.vector.tensor_tensor(sp_b[:], raw[:, :, 0:16], vecs[:, 1:2, :].broadcast_to([P, NT, 16]), ALU.add))
            own.link(nc.vector.scalar_tensor_tensor(sp_a[:], sp_b[:], -1.0, sp_b[:], op0=ALU.mult, op1=ALU.max))
            own.link(nc.vector.tensor_copy(beta[:], raw[:, :, 16:32]))
            own.link(nc.vector.tensor_tensor(lam_in[:, 0:2, :], lam_in[:, 0:4:2, :], lam_in[:, 1:4:2, :], ALU.mult))
            nc.vector.tensor_reduce(lam_t[:, 0:2], lam_in[:, 0:2, :], AX.X, ALU.add).then_inc(sc_dve, 1)
            dve.wait_ge(sc_act, 4)
            nc.vector.tensor_scalar(sp_a[:], sp_a[:], 1.0, None, ALU.add).then_inc(sc_dve, 1)
            own.link(nc.vector.tensor_scalar(beta[:], beta[:], 1.0, None, ALU.add))
            own.link(nc.vector.reciprocal(beta[:], beta[:]))
            own.link(nc.vector.tensor_tensor(lam_t[:, 4:5], lam_t[:, 2:3], lam_t[:, 3:4], ALU.subtract))
            own.link(nc.vector.tensor_scalar(lam_t[:, 4:5], lam_t[:, 4:5], LAM_INIT, None, ALU.add))
            nc.vector.tensor_scalar(dn_col[:], cols_b[:, 61:62], 1.0 - LAM_INIT, None, ALU.mult)
            dve.wait_ge(sc_act, 5)
            own.link(nc.vector.scalar_tensor_tensor(sp_a[:], sp_b[:], 0.0, sp_a[:], op0=ALU.max, op1=ALU.add))
            nc.vector.scalar_tensor_tensor(g_t[:], sp_a[:], -1.0, vecs[:, 2:3, :].broadcast_to([P, NT, 16]),
                                           op0=ALU.mult, op1=ALU.mult).then_inc(sc_dve, 1)
            dve.wait_ge(sc_pe, 1)
            sums = ps[:, 6, 0:240]
            for d in range(2):
                own.link(nc.vector.tensor_copy(gc[:, :, 8 * d:8 * d + 8],
                                               sums[:, 40 * d:40 * d + 40].rearrange("p (t n) -> p t n", t=NT)))
            total = sums[:, 80:160].rearrange("p (t n) -> p t n", t=NT)
            own.link(nc.vector.tensor_copy(gl[:], total))
            nc.vector.tensor_tensor(ekg[:], total, gc[:], ALU.subtract).then_inc(sc_dve, 1)

            def l2_mean(m):
                dve.wait_ge(l2_mm, m + 1)
                if m >= 2:
                    dve.wait_ge(l2_done, m - 1)
                nc.vector.tensor_scalar(halves(scratch[m % 2][:]), ps[:, 2 * (m % 2):2 * (m % 2) + 2, 0:HT], EPS, None,
                                        ALU.add).then_inc(l2_var, 1)

            l2_mean(0)
            for m in range(8):
                if m < 7:
                    l2_mean(m + 1)
                dve.wait_ge(l2_sd, m + 1)
                own.link(nc.vector.reciprocal(scratch[m % 2][:], scratch[m % 2][:]))
                nc.vector.scalar_tensor_tensor(pre[:, m, 0:T], pre[:, m, 0:T], DK ** -0.5 if m < 4 else 1.0,
                                               scratch[m % 2][:], op0=ALU.mult, op1=ALU.mult).then_inc(l2_done, 1)
            for r in range(8):
                hb = r % 4
                dst = q_b[:, hb, TC:T] if r < 4 else k_all[:, hb, TC:T]
                dve.wait_ge(rot_mm, r + 1)
                own.link(nc.vector.tensor_tensor(scratch[r % 2][:, 0:TS], ps[:, 4 + r % 2, :], rope_sb[:, TS:2 * TS], ALU.mult))
                dve.wait_ge(rot_cos, r + 1)
                nc.vector.tensor_tensor(dst, scratch[r % 2][:, 0:TS], conv_acc[r % 2][:, 0:TS], ALU.add).then_inc(rot_done, 1)

            def att_max(v):
                nk = ATT_UNITS[v][2]
                for m in range(2):
                    dve.wait_ge(s_mm, 2 * v + m + 1)
                    src = ps[:, 2 * m, 0:P] if nk == P else ps[:, 2 * m:2 * m + 2, 0:HT]
                    own.link(nc.vector.tensor_reduce(att_s[:, v % 2, 6 + m:7 + m], src, AX.X if nk == P else AX.XY, ALU.max))
                    nc.vector.tensor_scalar(att_s[:, v % 2, m:m + 1], att_s[:, v % 2, 6 + m:7 + m], -DK ** -0.5, None,
                                            ALU.mult).then_inc(s_max, 1)

            att_max(0)
            for v, (hb, q0, nk) in enumerate(ATT_UNITS):
                a = att_s[:, v % 2, :]
                dve.wait_ge(s_exp, 2 * v + 2)
                own.link(nc.vector.reciprocal(a[:, 4:6], a[:, 2:4]))
                own.link(nc.vector.tensor_tensor(a[:, 5:6], a[:, 5:6], lam_t[:, 4:5], ALU.mult))
                own.link(nc.vector.tensor_scalar(att_v[:, 0:nk], att_p[1][:, 0:nk], a[:, 5:6], None, ALU.mult))
                if v >= 1:
                    dve.wait_ge(s_turn, v)
                nc.vector.scalar_tensor_tensor(att_w[:, 0:nk], att_p[0][:, 0:nk], a[:, 4:5], att_v[:, 0:nk],
                                               op0=ALU.mult, op1=ALU.subtract).then_inc(s_wts, 1)
                if v + 1 < NU:
                    att_max(v + 1)
                dve.wait_ge(s_pv, v + 1)
                nc.vector.tensor_copy(att_q[:, hb, q0:q0 + P], ps[:, 6, 0:P]).then_inc(s_out, 1)
            for hb in range(HB):
                dve.wait_ge(an_mm, hb + 1)
                nc.vector.tensor_scalar(halves(rstd[:]), ps[:, 0:2, 0:HT], D / P, EPS, ALU.mult, ALU.add).then_inc(an_var, 1)
                dve.wait_ge(an_sd, hb + 1)
                own.link(nc.vector.reciprocal(rstd[:], rstd[:]))
                nc.vector.scalar_tensor_tensor(scratch[0][:], att_q[:, hb, :], dn_col[:], rstd[:],
                                               op0=ALU.mult, op1=ALU.mult).then_inc(an_tmp, 1)
                dve.wait_ge(an_hi, hb + 1)
                nc.vector.tensor_tensor(h_lo[:, 4 + hb, :], scratch[0][:], h_hi[:, 4 + hb, :].bitcast(F32),
                                        ALU.subtract).then_inc(an_done, 1)

            dve.wait_ge(sc_act, 8)
            dve.wait_ge(st_clear, 3)
            for s in range(NT):
                T0, C0 = s * DVE_T, s * DVE_C

                def decay(b):
                    d, g = b // 2, b % 2
                    t, q = tile_of(s, d), 8 * d + 4 * g
                    dve.wait_ge(t_pe[b], s * PE_T + 1)
                    if s >= 1:
                        dve.wait_ge(c_dve[b], s * DVE_C)
                    for h in range(4):
                        ins = nc.vector.tensor_scalar(e_x[b][:, h, :], ps[:, b, h * P:(h + 1) * P], gc[:, t, q + h:q + h + 1],
                                                      0.0, ALU.subtract, ALU.min)
                    ins.then_inc(t_dve[b], 1)

                def make_m(b):
                    d, g = b // 2, b % 2
                    t, q = tile_of(s, d), 8 * d + 4 * g
                    dve.wait_ge(t_act[b], s * ACT_T + 1)
                    dve.wait_ge(t_pe[b], s * PE_T + 3)
                    for h in range(4):
                        ins = nc.vector.scalar_tensor_tensor(m_t[b][:, h, :], ps[:, b, h * P:(h + 1) * P],
                                                             beta[:, t, q + h:q + h + 1], e_x[b][:, h, :],
                                                             op0=ALU.mult, op1=ALU.mult)
                    ins.then_inc(t_dve[b], 1)

                def make_p(b):
                    dve.wait_ge(t_pe[b], s * PE_T + 5)
                    if s >= 1:
                        dve.wait_ge(c_pe[b], s * PE_C)
                    nc.vector.tensor_tensor(p_t[b][:], heads4(ps[:, b, :], P), e_x[b][:], ALU.mult).then_inc(t_dve[b], 1)

                def x_out(b, n):
                    dve.wait_ge(t_pe[b], s * PE_T + 7 + 3 * (n - 1))
                    nc.vector.tensor_tensor(e_x[b][:], heads4(ps[:, b, :], P), over4(mask(b // 2, n, False)),
                                            ALU.mult).then_inc(t_dve[b], 1)

                def t_out(b, n):
                    dve.wait_ge(t_pe[b], s * PE_T + 8 + 3 * (n - 1))
                    nc.vector.tensor_tensor(t_t[b][:], t_t[b][:], heads4(ps[:, b, :], P), ALU.subtract).then_inc(t_dve[b], 1)

                for b in range(4):
                    decay(b)
                for b in range(4):
                    make_m(b)
                for b in range(4):
                    make_p(b)
                for n in range(1, 7):
                    for b in range(4):
                        x_out(b, n)
                    for b in range(4):
                        t_out(b, n)

                def where(b):
                    d, g = b // 2, b % 2
                    return d, g, tile_of(s, d), slice(8 * d + 4 * g, 8 * d + 4 * g + 4)

                for b in range(4):
                    d, g, t, q = where(b)
                    dve.wait_ge(c_pe[b], s * PE_C + 1)
                    own.link(nc.vector.tensor_tensor(heads4(r_s[b], DK), heads4(ps[:, 4 + b, 0:256], DK),
                                                     spread(egc[:, t, q], DK), ALU.mult))
                    nc.vector.tensor_tensor(r_s[b], v_tok[:, t, g * 256:g * 256 + 256], r_s[b],
                                            ALU.subtract).then_inc(c_dve[b], 1)
                    nc.vector.tensor_tensor(heads4(oq[b], DK), heads4(ps[:, 4 + b, 256:512], DK),
                                            spread(egc[:, t, q], DK), ALU.mult).then_inc(c_dve[b], 1)
                for b in range(4):
                    d, g, t, q = where(b)
                    dve.wait_ge(c_pe[b], s * PE_C + 2)
                    nc.vector.tensor_tensor(heads4(u_s[b], DK), heads4(ps[:, 4 + b, 0:256], DK),
                                            spread(beta[:, t, q], DK), ALU.mult).then_inc(c_dve[b], 1)
                for b in range(4):
                    d, g, t, q = where(b)
                    S = st[0 if s == 0 else 1]
                    if s == 1:
                        dve.wait_ge(st_in, 64)
                    dve.wait_ge(c_pe[b], s * PE_C + 3)
                    for h in range(4):
                        cc, e = h // 2, h % 2
                        rows, cols = slice(e * DK, e * DK + DK), slice(e * DK, e * DK + DK)
                        ins = nc.vector.scalar_tensor_tensor(
                            S[rows, d, 2 * g + cc, cols], S[rows, d, 2 * g + cc, cols],
                            gl[rows, t, 8 * d + 4 * g + h:8 * d + 4 * g + h + 1],
                            ps[rows, 4 + b, cc * P + e * DK:cc * P + e * DK + DK], op0=ALU.mult, op1=ALU.add)
                    ins.then_inc(c_dve[b], 1)
                    own.link(nc.vector.tensor_tensor(oq[b], oq[b], ps[:, 4 + b, 256:512], ALU.add))
                    nc.vector.tensor_tensor(o_acc[:, t, g * 256:g * 256 + 256], o_acc[:, t, g * 256:g * 256 + 256],
                                            oq[b], ALU.add).then_inc(c_dve[b], 1)
            for b in range(4):
                dve.wait_ge(c_dve[b], NT * DVE_C)
            for t in range(NT):
                sq = scratch[1][:, 0:512]
                own.link(nc.vector.tensor_tensor(sq, o_acc[:, t, :], o_acc[:, t, :], ALU.mult))
                own.link(nc.vector.tensor_reduce(o_sum[:, t, :], heads4(sq, DK), AX.X, ALU.add))
                nc.vector.tensor_scalar(o_sum[:, t, :], o_sum[:, t, :], 1.0 / DK, EPS, ALU.mult, ALU.add).then_inc(o_dve, 1)
                dve.wait_ge(o_act, 2 * t + 1)
                own.link(nc.vector.reciprocal(o_sum[:, t, :], o_sum[:, t, :]))
                nc.vector.tensor_tensor(heads4(o_acc[:, t, :], DK), heads4(o_acc[:, t, :], DK),
                                        spread(o_sum[:, t, :], DK), ALU.mult).then_inc(o_dve, 1)
                dve.wait_ge(o_pe, t + 1)
                nc.vector.scalar_tensor_tensor(heads4(scratch[0][:, 0:512], P), heads4(ps[:, t % 4, :], P),
                                               cols_b[:, 60:61], z_t[:, :, t * P:(t + 1) * P],
                                               op0=ALU.mult, op1=ALU.mult).then_inc(o_dve, 1)
                dve.wait_ge(o_act, 2 * t + 2)
                nc.vector.tensor_tensor(h_lo[:, 0:4, t * P:(t + 1) * P], heads4(scratch[0][:, 0:512], P),
                                        h_hi[:, 0:4, t * P:(t + 1) * P].bitcast(F32), ALU.subtract).then_inc(o_dve, 1)
            for m in range(8):
                w_low(TILE_WOUT + m + 1, (m + 1) % 2)
                dve.wait_ge(tile_done, TILE_WOUT + m + 1)
                update_x(m, 2 * (m % 2), 5)
            norm(2)
            modulate(2)
            ffn(1)
            norm(3)
            for k in range(KD):
                nc.vector.scalar_tensor_tensor(x_t[:, k, :], x_t[:, k, :], cols_a[:, 112 + k:113 + k], rstd[:],
                                               op0=ALU.mult, op1=ALU.mult).then_inc(y_scaled, 1)

        @block.gpsimd
        def _(pool):
            own = Chain(pool, pool_own)

            def add_squares(seq):
                for k in range(KD):
                    pool.wait_ge(sq_ready, seq * 8 + k + 1)
                    if k == 0:
                        if seq >= 1:
                            pool.wait_ge(mean_mm, seq)
                        nc.gpsimd.tensor_copy(sumsq[:], square[0][:]).then_inc(sq_added, 1)
                    else:
                        pool.wait_ge(sq_added, seq * 8 + k)
                        nc.gpsimd.tensor_tensor(sumsq[:], sumsq[:], square[k % 2][:], ALU.add).then_inc(sq_added, 1)

            add_squares(0)
            add_squares(1)
            pool.wait_ge(tile_done, FFN_TILES)
            for a in (0, TC + 2, T + 4):
                nc.gpsimd.memset(pre[:, :, a:a + 2], 0.0).then_inc(pads_set, 1)
            nc.gpsimd.memset(ones_1[:], 1.0).then_inc(pads_set, 1)
            pool.wait_ge(mix_in, 16 * 11)
            pool.wait_ge(proj_out, 24)
            pool.wait_ge(conv_silu, 12)
            for r in range(8):
                src = q_b[:, r % 4, TC:T] if r < 4 else k_b[:, r % 4, TC:T]
                if r >= 2:
                    pool.wait_ge(rot_done, r - 1)
                nc.gpsimd.tensor_tensor(conv_acc[r % 2][:, 0:TS], src, rope_sb[:, 0:TS], ALU.mult).then_inc(rot_cos, 1)
            pool.wait_ge(an_done, 4)
            pool.wait_ge(kv_out, 32)
            nc.gpsimd.memset(st[0][:], 0.0).then_inc(st_clear, 1)
            nc.gpsimd.memset(st[1][:], 0.0).then_inc(st_clear, 1)
            pool.wait_ge(kv_copied, 2 * NT)
            nc.gpsimd.memset(o_acc, 0.0).then_inc(st_clear, 1)
            for s in range(NT):
                for b in range(4):
                    pool.wait_ge(t_dve[b], s * DVE_T + 2)
                    if s >= 1:
                        pool.wait_ge(c_pe[b], s * PE_C)
                    own.link(nc.gpsimd.tensor_tensor(t_t[b][:], m_t[b][:], over4(mask(b // 2, 0, True)), ALU.mult))
                    nc.gpsimd.tensor_tensor(t_t[b][:], over4(const("ident")), t_t[b][:], ALU.subtract).then_inc(t_pool[b], 1)
                for b in range(4):
                    d, g = b // 2, b % 2
                    pool.wait_ge(t_dve[b], s * DVE_T + 3)
                    nc.gpsimd.tensor_tensor(p_t[b][:], p_t[b][:], over4(const(("tri_f", "tri_b")[d])), ALU.mult)\
                        .then_inc(t_pool[b], 1)
                    t = tile_of(s, d)
                    nc.gpsimd.tensor_tensor(heads4(kg[b], DK), heads4(k_tok[:, t, g * 256:g * 256 + 256], DK),
                                            spread(ekg[:, t, 8 * d + 4 * g:8 * d + 4 * g + 4], DK), ALU.mult)\
                        .then_inc(t_pool[b], 1)
            add_squares(2)
            add_squares(3)

        @block.tensor
        def _(pe):
            def product(out, k0, weights, x_parts, start, stop):
                hi, lo = weights
                xh, xl = x_parts
                nc.tensor.matmul(out, lo, xh, start=start, stop=False)
                nc.tensor.matmul(out, hi, xl, start=False, stop=False)
                return nc.tensor.matmul(out, hi, xh, start=False, stop=stop)

            def dense(s, banks, per_k=None):
                for k in range(KD):
                    if per_k is not None:
                        pe.wait_ge(h_ready, per_k + k + 1)
                    w = (w_hi[s][:, k * P:(k + 1) * P], w_lo[s][:, k * P:(k + 1) * P])
                    for half in range(2):
                        x = [h[:, k, half * HT:half * HT + HT] for h in (h_hi, h_lo)]
                        ins = product(ps[:, banks + half, 0:HT], k, w, x, k == 0, k == KD - 1)
                return ins

            def mean(seq):
                pe.wait_ge(sq_added, 8 * (seq + 1))
                for half in range(2):
                    ins = nc.tensor.matmul(ps[:, half, 0:HT], ones_d[:], sumsq[:, half * HT:half * HT + HT],
                                           start=True, stop=True)
                ins.then_inc(mean_mm, 1)

            def ffn(f):
                base, J = TILE_FFN[f], NJ * f

                def hidden(j, par, first):
                    pe.wait_ge(w_lo_ready, j * 2 + (base + 1))
                    if not first:
                        pe.wait_ge(silu_ready, j + (J - 1))
                    dense(0, 4 * par, 16 * f if first and par == 0 else None).then_inc(tile_done, 1)
                    pe.wait_ge(w_lo_ready, j * 2 + (base + 2))
                    if not first:
                        pe.wait_ge(act_ready, j + (J - 1))
                    dense(1, 4 * par + 2).then_inc(tile_done, 1)

                def down(n, s, j, mm_wait, start, stop):
                    pe.wait_ge(w_lo_ready, n + 1)
                    for jj in range(2):
                        for mm in range(4):
                            if mm_wait is not None and jj == 0:
                                pe.wait_ge(x_updated, mm_wait + mm + 1)
                            at = jj * 512 + mm * P
                            w = (w_hi[s][:, at:at + P], w_lo[s][:, at:at + P])
                            for half in range(2):
                                x = [pick(a, j + jj, slice(half * HT, half * HT + HT)) for a in (act_hi, act_lo)]
                                ins = product(ps[:, 2 * mm + half, 0:HT], None, w, x, start and jj == 0, stop and jj == 1)
                    ins.then_inc(tile_done, 1)

                hidden(0, 0, True)
                hidden(1, 1, True)
                with pe.Fori(0, NJ // 2 - 1) as i:
                    for k in range(2):
                        hidden(i * 2 + (2 + k), k, False)
                pe.wait_ge(actlo_ready, NJ * (f + 1))
                for hf in range(2):
                    n = base + N_IN + 11 * hf
                    down(n, n % 2, 0, X_BASE[f] if hf else None, True, False)
                    with pe.Fori(0, 4) as i:
                        for k in range(2):
                            down(i * 2 + (n + 1 + k), (n + 1 + k) % 2, i * 4 + (2 + 2 * k), None, False, False)
                    down(n + 9, (n + 9) % 2, 18, None, False, False)
                    down(n + 10, (n + 10) % 2, 20, None, False, True)

            pe.wait_ge(small_in, 16 * 12)
            nc.tensor.transpose(ps[:, 0, 0:120], rows_a[:], ident[0:120, 0:120]).then_inc(cols_turned, 1)
            nc.tensor.transpose(ps[:, 1, 0:62], rows_b[:], ident[0:62, 0:62]).then_inc(cols_turned, 1)
            pe.wait_ge(x_in, 32)
            for i in range(2 * NT):
                t, q = i // 2, i % 2
                if i >= 4:
                    pe.wait_ge(x_copied, i - 3)
                for a in range(4):
                    ins = nc.tensor.transpose(ps[:, 2 + i % 4, a * P:(a + 1) * P], x_tok[:, t, (4 * q + a) * P:(4 * q + a + 1) * P],
                                              ident[:])
                ins.then_inc(x_turned, 1)
            pe.wait_ge(cond_ready, 2)
            with pe.Fori(0, NMOD) as m:
                for k in range(8):
                    pe.wait_ge(ada_landed[k], m * 16 + 16)
                    for a in range(KD):
                        ins = nc.tensor.matmul(ps[:, 7, bass.ds(m * 16 + 2 * k, 2)], ada_ring[k][:, a * P:(a + 1) * P],
                                               cond[:, a, :], start=(a == 0), stop=(a == KD - 1))
                    ins.then_inc(ada_used, 1)
            pe.wait_ge(ones_set, 1)
            mean(0)
            ffn(0)
            mean(1)
            for m in range(2):
                pe.wait_ge(w_lo_ready, TILE_WIN + m + 1)
                dense(m, 2 * m, 8 if m == 0 else None).then_inc(tile_done, 1)
            with pe.Fori(0, 11) as i:
                for k in range(2):
                    pe.wait_ge(w_lo_ready, i * 2 + (TILE_WIN + 3 + k))
                    pe.wait_ge(proj_out, i * 2 + (1 + k))
                    dense(k, 2 * k).then_inc(tile_done, 1)
            pe.wait_ge(proj_out, 24)
            for q in range(4):
                pe.wait_ge(w_lo_ready, TILE_WBV + q + 1)
                s = q % 2
                for kk in range(2):
                    k = 2 * q + kk
                    w = [x[s][:, kk * 512:kk * 512 + 512] for x in (w_hi, w_lo)]
                    for t in range(NT):
                        hh, hl = [h[:, k, t * P:(t + 1) * P] for h in (h_hi, h_lo)]
                        out = ps[:, t, :]
                        nc.tensor.matmul(out, hl, w[0], start=(k == 0), stop=False)
                        nc.tensor.matmul(out, hh, w[1], start=False, stop=False)
                        ins = nc.tensor.matmul(out, hh, w[0], start=False, stop=(k == KD - 1))
                ins.then_inc(tile_done, 1)
            pe.wait_ge(gate_split, 2)
            for t in range(NT):
                for k in range(KD):
                    hh, hl = [h[:, k, t * P:(t + 1) * P] for h in (h_hi, h_lo)]
                    gh, gw = [x[:, k * NDB:(k + 1) * NDB] for x in (gate_hi, gate_lo)]
                    out = ps[:, 5, t * NDB:(t + 1) * NDB]
                    nc.tensor.matmul(out, hl, gh, start=(k == 0), stop=False)
                    nc.tensor.matmul(out, hh, gw, start=False, stop=False)
                    ins = nc.tensor.matmul(out, hh, gh, start=False, stop=(k == KD - 1))
            ins.then_inc(gate_mm, 1)
            pe.wait_ge(sc_dve, 3)
            pe.wait_ge(pads_set, 4)
            for lhs, at, cols in ((const("tri_f"), 0, slice(0, 8)), (const("tri_b"), 40, slice(8, 16)),
                                  (ones_1[:], 80, slice(0, 16))):
                n = NT * (cols.stop - cols.start)
                ins = nc.tensor.matmul(ps[:, 6, at:at + n].rearrange("p (t n) -> p t n", t=NT), lhs, g_t[:, :, cols],
                                       start=True, stop=True)
            ins.then_inc(sc_pe, 1)
            pe.wait_ge(vb_ready, 1)
            for m in range(8):
                pe.wait_ge(l2_sq, m + 1)
                if m >= 2:
                    pe.wait_ge(l2_var, m - 1)
                for half in range(2):
                    ins = nc.tensor.matmul(ps[:, 2 * (m % 2) + half, 0:HT], const("headones"),
                                           square[m % 2][:, half * HT:half * HT + HT], start=True, stop=True)
                ins.then_inc(l2_mm, 1)
            for r in range(8):
                src = q_b[:, r % 4, TC:T] if r < 4 else k_b[:, r % 4, TC:T]
                if r >= 2:
                    pe.wait_ge(rot_done, r - 1)
                nc.tensor.matmul(ps[:, 4 + r % 2, :], const("perm"), src, start=True, stop=True).then_inc(rot_mm, 1)
            pe.wait_ge(sc_dve, 4)
            for src, bank in ((k_b, 6), (ck_tok, 7)):
                for hb in range(HB):
                    x = k_b[:, hb, 0:P] if bank == 6 else ck_tok[:, hb * P:(hb + 1) * P]
                    ins = nc.tensor.transpose(ps[:, bank, hb * P:(hb + 1) * P], x, ident[:])
                ins.then_inc(kt_turned, 1)

            def scores(v):
                hb, q0, nk = ATT_UNITS[v]
                if v >= 1:
                    pe.wait_ge(s_exp, 2 * v)
                for m in range(2):
                    rows = slice(m * DK, m * DK + DK)
                    q = q_b[rows, hb, q0:q0 + P]
                    if nk == P:
                        ins = nc.tensor.matmul(ps[:, 2 * m, 0:P], q, k_b[rows, hb, 0:P], start=True, stop=True)
                    else:
                        for half in range(2):
                            ins = nc.tensor.matmul(ps[:, 2 * m + half, 0:HT], q, k_all[rows, hb, half * HT:half * HT + HT],
                                                   start=True, stop=True)
                    ins.then_inc(s_mm, 1)

            pe.wait_ge(kt_copied, 2)
            pe.wait_ge(rot_done, 8)
            pe.wait_ge(l2_var, 8)
            scores(0)
            for v, (hb, q0, nk) in enumerate(ATT_UNITS):
                if v + 1 < NU:
                    scores(v + 1)
                pe.wait_ge(s_wts, v + 1)
                if v >= 1:
                    pe.wait_ge(s_turned, v)
                for kt in range(nk // P):
                    ins = nc.tensor.transpose(ps[:, 4 + kt // 4, (kt % 4) * P:(kt % 4 + 1) * P], att_w[:, kt * P:(kt + 1) * P],
                                              ident[:])
                ins.then_inc(s_turn, 1)
                pe.wait_ge(s_turned, v + 1)
                if v >= 1:
                    pe.wait_ge(s_out, v)
                for kt in range(nk // P):
                    vals = cv_tok[:, hb * P:(hb + 1) * P] if nk > P and kt == 0 else v_b[:, kt, hb * P:(hb + 1) * P]
                    ins = nc.tensor.matmul(ps[:, 6, 0:P], vals, att_wt[:, kt * P:(kt + 1) * P],
                                           start=(kt == 0), stop=(kt == nk // P - 1))
                ins.then_inc(s_pv, 1)
            for hb in range(HB):
                pe.wait_ge(an_sq, hb + 1)
                if hb >= 1:
                    pe.wait_ge(an_var, hb)
                for half in range(2):
                    ins = nc.tensor.matmul(ps[:, half, 0:HT], ones_d[:], square[0][:, half * HT:half * HT + HT],
                                           start=True, stop=True)
                ins.then_inc(an_mm, 1)

            pe.wait_ge(l2_done, 8)
            for i in range(2 * NT):
                if i >= 4:
                    pe.wait_ge(kv_copied, i - 3)
                for a in range(4):
                    ins = nc.tensor.transpose(ps[:, 4 + i % 4, a * P:(a + 1) * P],
                                              pre[:, 4 + 4 * (i % 2) + a, (i // 2) * P:(i // 2 + 1) * P], ident[:])
                ins.then_inc(kv_turned, 1)
            pe.wait_ge(an_done, 4)
            for s in range(NT):
                def qk(b, h, which):
                    g, t = b % 2, tile_of(s, b // 2)
                    rows = slice((h % 2) * DK, (h % 2) * DK + DK)
                    return pre[rows, which + 2 * g + h // 2, t * P:(t + 1) * P]

                for b in range(4):
                    d, g = b // 2, b % 2
                    if s >= 1:
                        pe.wait_ge(t_dve[b], s * DVE_T)
                    for h in range(4):
                        col = g_t[:, tile_of(s, d), 8 * d + 4 * g + h:8 * d + 4 * g + h + 1]
                        ins = nc.tensor.matmul(ps[:, b, h * P:(h + 1) * P], col.broadcast_to([P, P]),
                                               const(("tri_f", "tri_b")[d]), start=True, stop=True)
                    ins.then_inc(t_pe[b], 1)
                for i, which in ((1, 4), (2, 0)):
                    for e in range(2):
                        for b in range(4):
                            if e == 0:
                                pe.wait_ge(t_dve[b], s * DVE_T + i)
                            else:
                                pe.wait_ge(t_pe[b], s * PE_T + 2 * i)
                            for h in (e, e + 2):
                                ins = nc.tensor.matmul(ps[:, b, h * P:(h + 1) * P], qk(b, h, 4), qk(b, h, which),
                                                       start=True, stop=True)
                            ins.then_inc(t_pe[b], 1)
                for n in range(7):
                    if n >= 1:
                        for b in range(4):
                            pe.wait_ge(t_act[b], s * ACT_T + 1 + n)
                            for h in range(4):
                                ins = nc.tensor.matmul(ps[:, b, h * P:(h + 1) * P], m_t[b][:, h, :], t_n[b][:, h, :],
                                                       start=True, stop=True)
                            ins.then_inc(t_pe[b], 1)
                        for b in range(4):
                            pe.wait_ge(t_dve[b], s * DVE_T + 4 + 2 * (n - 1))
                            for h in range(4):
                                ins = nc.tensor.matmul(ps[:, b, h * P:(h + 1) * P], e_x[b][:, h, :], t_t[b][:, h, :],
                                                       start=True, stop=True)
                            ins.then_inc(t_pe[b], 1)
                    if n < 6:
                        for b in range(4):
                            if n == 0:
                                pe.wait_ge(t_pool[b], s * POOL_T + 1)
                                pe.wait_ge(t_dve[b], s * DVE_T + 3)
                            else:
                                pe.wait_ge(t_dve[b], s * DVE_T + 5 + 2 * (n - 1))
                            for h in range(4):
                                ins = nc.tensor.transpose(ps[:, b, h * P:(h + 1) * P], t_t[b][:, h, :], ident[:])
                            ins.then_inc(t_pe[b], 1)
                S = st[0 if s == 0 else 1]
                for b in range(4):
                    d, g = b // 2, b % 2
                    t = tile_of(s, d)
                    if s == 0:
                        pe.wait_ge(st_clear, 3)
                        pe.wait_ge(kv_copied, 2 * NT)
                    else:
                        pe.wait_ge(c_dve[b], s * DVE_C)
                    if s == 1:
                        pe.wait_ge(st_in, 64)
                    for which, at in ((4, 0), (0, 256)):
                        for cc in range(2):
                            ins = nc.tensor.matmul(ps[:, 4 + b, at + cc * P:at + cc * P + P],
                                                   pre[:, which + 2 * g + cc, t * P:(t + 1) * P], S[:, d, 2 * g + cc, :],
                                                   start=True, stop=True)
                    ins.then_inc(c_pe[b], 1)
                for b in range(4):
                    pe.wait_ge(c_dve[b], s * DVE_C + 2)
                    pe.wait_ge(t_dve[b], (s + 1) * DVE_T)
                    for h in range(4):
                        ins = nc.tensor.matmul(ps[:, 4 + b, h * DK:(h + 1) * DK], t_t[b][:, h, :], r_s[b][:, h * DK:(h + 1) * DK],
                                               start=True, stop=True)
                    ins.then_inc(c_pe[b], 1)
                for b in range(4):
                    pe.wait_ge(c_dve[b], s * DVE_C + 3)
                    pe.wait_ge(t_pool[b], (s + 1) * POOL_T)
                    for cc in range(2):
                        nc.tensor.matmul(ps[:, 4 + b, cc * P:(cc + 1) * P], kg[b][:, cc * P:(cc + 1) * P],
                                         u_s[b][:, cc * P:(cc + 1) * P], start=True, stop=True)
                    for h in range(4):
                        ins = nc.tensor.matmul(ps[:, 4 + b, 256 + h * DK:256 + (h + 1) * DK], p_t[b][:, h, :],
                                               u_s[b][:, h * DK:(h + 1) * DK], start=True, stop=True)
                    ins.then_inc(c_pe[b], 1)
            for t in range(NT):
                pe.wait_ge(o_dve, 4 * t + 2)
                for a in range(4):
                    ins = nc.tensor.transpose(ps[:, t % 4, a * P:(a + 1) * P], o_acc[:, t, a * P:(a + 1) * P], ident[:])
                ins.then_inc(o_pe, 1)
            pe.wait_ge(o_dve, 4 * NT)
            for m in range(2):
                pe.wait_ge(w_lo_ready, TILE_WOUT + m + 1)
                dense(m, 2 * m).then_inc(tile_done, 1)
            with pe.Fori(0, 3) as i:
                for k in range(2):
                    pe.wait_ge(w_lo_ready, i * 2 + (TILE_WOUT + 3 + k))
                    pe.wait_ge(x_updated, i * 2 + (8 + 1 + k))
                    dense(k, 2 * k).then_inc(tile_done, 1)
            mean(2)
            ffn(1)
            mean(3)
            for i in range(2 * NT):
                t, q = i // 2, i % 2
                if i == 0:
                    pe.wait_ge(var_ready, 4)
                    pe.wait_ge(y_scaled, KD)
                if i >= 4:
                    pe.wait_ge(y_copied, i - 3)
                for a in range(4):
                    ins = nc.tensor.transpose(ps[:, i % 4, a * P:(a + 1) * P], x_t[:, 4 * q + a, t * P:(t + 1) * P], ident[:])
                ins.then_inc(y_turned, 1)


_INS = ['x_prompt', 'x_sample', 'cache_diff_k', 'cache_diff_v', 'state_delta', 'c', 'c_ctx', 'w_ada', 'b_ada',
        'norm_ffn1', 'w_ffn1_in', 'w_ffn1_out', 'norm_mix', 'w_in', 'conv_w', 'a_log', 'dt_bias', 'delta_norm',
        'lambda_q1', 'lambda_k1', 'lambda_q2', 'lambda_k2', 'diff_norm', 'w_out', 'norm_ffn2', 'w_ffn2_in',
        'w_ffn2_out', 'norm_final']
_OUTS = [(1, TC, D), (1, TS, D), (TC, HB * P), (TC, HB * P), (2, HA, DK, DK)]


def kernel(**inputs):
    import concourse.bacc as bacc
    from concourse.bass_utils import run_bass_kernel_spmd

    nc = bacc.Bacc("TRN2", target_bir_lowering=False, num_devices=1, dynamic_dma_scratch_size=1024)
    arrays, args = {}, []
    tables = dict(zip(("consts", "rope"), shape_constants()))
    for name in _INS + ["consts", "rope"]:
        a = np.ascontiguousarray(tables[name] if name in tables else inputs[name])
        arrays[f"in_{name}"] = a
        args.append(nc.dram_tensor(f"in_{name}", a.shape, F32, kind="ExternalInput").ap())
    for i, shape in enumerate(_OUTS):
        args.append(nc.dram_tensor(f"out_{i}", shape, F32, kind="ExternalOutput").ap())
    hybrid_step(nc, *args)
    r = run_bass_kernel_spmd(nc, [arrays], core_ids=[0])
    y_p, y_s, nk, nv, ns = (r.results[0][f"out_{i}"] for i in range(len(_OUTS)))
    return (y_p, y_s, nk.reshape(1, 1, TC, HB, 2, DK), nv.reshape(1, 1, TC, HB, P),
            ns.reshape(1, 1, 2, HA, DK, DK))
```

```python
import math
from contextlib import ExitStack

import numpy as np
import concourse.bass as bass
from concourse import mybir

F32 = mybir.dt.float32
F32R = mybir.dt.float32r
ALU = mybir.AluOpType
ACT = mybir.ActivationFunctionType
AX = mybir.AxisListType

P = 128
D = 1024
KD = D // P
TC, TS = 128, 512
T = TC + TS
NT = T // P
HT = T // 2
DFF = 2816
NJ = DFF // P
HA, DK = 8, 64
HB = 4
NMOD = 9
CONV = 5
EPS = 1e-6
LAM_INIT = 0.8 - 0.6 * math.exp(-0.3 * 0)
LEVELS = [1, 2, 4, 8, 16, 32, 64]
COL_DEC = 2048
NDB = 4 * HA
COL_B = COL_DEC + NDB
SEGS = [(0, 0, 0, 0, TC), (1, 0, TC, TC, HT - TC), (1, 1, 0, HT, HT)]
ATT_UNITS = [(hb, 0, TC) for hb in range(HB)] + [(hb, q, P + TS) for hb in range(HB) for q in range(TC, T, P)]
NU = len(ATT_UNITS)
PE_T, DVE_T, ACT_T, POOL_T = 24, 23, 3, 10
MAKE_ORDER = [0, 1, 4, 2, 3]
MAKE_STAGES, MAKE_LAG = 26, 7
ROUNDS = [(2 * NT + 3 - c) // 4 for c in range(4)]
PE_C, DVE_C, POOL_C = 3, 6, 2
ADA_MARKS = 14


def tile_of(step, d):
    return step if d == 0 else (0 if step == 0 else NT - step)


def pick(x, j, *rest):
    if isinstance(j, int):
        return x[(slice(None), j) + rest]
    return x[(slice(None), bass.ds(j, 1)) + (rest or (slice(None),))].rearrange("p a b -> p (a b)")


def halves(x):
    return x.rearrange("p (a b) -> p a b", a=2)


def heads4(x, n):
    return x.rearrange("p (h n) -> p h n", n=n)


def spread(x, n):
    return x[:, :, None].broadcast_to([x.shape[0], x.shape[1], n])


N_IN, N_OUT = 2 * NJ, NJ
FFN_TILES = N_IN + N_OUT
TILE_FFN = [0, FFN_TILES + 28 + 8]
TILE_WIN = FFN_TILES
TILE_WBV = TILE_WIN + 24
TILE_WOUT = TILE_WIN + 28
PAIR = 2 * P
N_TILES = TILE_FFN[1] + FFN_TILES

CONST_NAMES = (["ident", "perm", "headones", "tri_f", "tri_b", "after", "before"] +
               [f"level{n}" for n in range(7)] + [f"sides{n}" for n in range(1, 7)])


def shape_constants():
    i = np.arange(P)
    ident = np.eye(P)
    perm = np.zeros((P, P))
    perm[i ^ 16, i] = 1.0
    headones = (i[:, None] // DK == i[None, :] // DK) * 1.0
    tri_f = (i[:, None] <= i[None, :]) * 1.0
    tri_b = (i[:, None] >= i[None, :]) * 1.0
    after, before = (i[:, None] < i[None, :]) * 1.0, (i[:, None] > i[None, :]) * 1.0
    level, sides = [], []
    for b in LEVELS:
        half = (i // b) % 2
        level.append(((i[:, None] // (2 * b) == i[None, :] // (2 * b)) & (half[:, None] != half[None, :])) * 1.0)
        sides.append(np.where(half[None, :] == 0, i[:, None] >= i[None, :], i[:, None] <= i[None, :]) * 1.0)
    n = np.arange(TS)
    d = i % DK
    pos = np.where((d // 32)[:, None] == 0, (n // 64)[None, :], (n % 64)[None, :]).astype(np.float32)
    inv = (np.float32(10000.0) ** (-(d % 16).astype(np.float32) / np.float32(16))).astype(np.float32)
    ang = (pos * inv[:, None]).astype(np.float32)
    sign = np.where(d % 32 < 16, -1.0, 1.0)[:, None]
    small = np.concatenate([ident, perm, headones, tri_f, tri_b, after, before] + level + sides[1:], 1).astype(np.float32)
    rope = np.concatenate([np.cos(ang), np.sin(ang) * sign], 1).astype(np.float32)
    return small, rope


N_SMALL = len(CONST_NAMES) * P


class Chain:

    def __init__(self, eng, sem):
        self.eng, self.sem, self.n, self.reg, self.m = eng, sem, 0, None, 0

    def link(self, ins):
        ins.then_inc(self.sem, 1)
        self.m += 1
        self.wait_back(0)

    def mark(self, ins):
        ins.then_inc(self.sem, 1)
        self.m += 1

    def wait_back(self, k):
        at = self.n + self.m - k
        self.eng.wait_ge(self.sem, at if self.reg is None else self.reg + at)

    def loop(self, i, per):
        self.n, self.m = self.n + self.m, 0
        self.reg, self.per = i * per, per

    def done(self, iters):
        assert self.m == self.per, (self.m, self.per)
        self.n, self.m, self.reg = self.n + iters * self.per, 0, None


def hybrid_step(nc, x_prompt, x_sample, cache_diff_k, cache_diff_v, state_delta, c, c_ctx, w_ada, b_ada,
                norm_ffn1, w_ffn1_in, w_ffn1_out, norm_mix, w_in, conv_w, a_log, dt_bias, delta_norm,
                lambda_q1, lambda_k1, lambda_q2, lambda_k2, diff_norm, w_out, norm_ffn2, w_ffn2_in,
                w_ffn2_out, norm_final, consts, rope, y_prompt, y_sample, new_k, new_v, new_state):
    ctx = ExitStack()
    with ctx:
        def sem(name):
            return ctx.enter_context(nc.semaphore(name))

        def holder(stack):
            return lambda name, shape, dt=F32: stack.enter_context(nc.sbuf_tensor(name, shape, dt))

        sb = holder(ctx)
        x_t = sb("x_t", [P, KD, T])
        w_raw = [sb(f"w_raw{i}", [P, D]) for i in range(2)]
        with ExitStack() as s:
            spare = [[holder(s)(f"spare{i}{c}", [P, 4, P]) for c in range(2)] for i in range(4)]
        w_hi = [sb(f"w_hi{i}", [P, D], F32R) for i in range(2)]
        w_lo = [sb(f"w_lo{i}", [P, D], F32R) for i in range(2)]
        with ExitStack() as s:
            h_hi, h_lo = [[holder(s)(f"h_{n}0", [P, 4, T], F32R)] for n in ("hi", "lo")]
        p_all = sb("p_all", [P, NT, 2, 4 * P])
        for h, n in ((h_hi, "hi"), (h_lo, "lo")):
            h.append(sb(f"h_{n}1", [P, 4, T], F32R))
        ones_col = sb("ones_col", [P, 1])
        cond = sb("cond", [P, KD, 2])
        ident = sb("ident", [P, P])
        ones_d = sb("ones_d", [P, P])
        cols_a = sb("cols_a", [P, 120])
        cols_b = sb("cols_b", [P, 62])
        mods = sb("mods", [P, NMOD * KD, 2])
        scales = sb("scales", [P, 3, KD, 2])
        root_dummy = sb("root_dummy", [P, 1])
        rstd = sb("rstd", [P, T])
        sumsq = sb("sumsq", [P, T])
        square = [sb(f"square{i}", [P, T]) for i in range(2)]
        scratch = [sb(f"scratch{i}", [P, T]) for i in range(2)]
        silu_g, act_f = square, scratch

        with ExitStack() as s:
            tb = holder(s)
            x_tok = tb("x_tok", [P, NT, D])
            ada_ring = [tb(f"ada_ring{i}", [P, D]) for i in range(8)]
            rows_a = tb("rows_a", [120, P])
            rows_b = tb("rows_b", [62, P])
        with ExitStack() as s:
            tb = holder(s)
            act_hi = tb("act_hi", [P, NJ, T], F32R)
            act_lo = tb("act_lo", [P, NJ, T], F32R)
            ada_ffn = [tb(f"ada_ffn{i}", [P, D]) for i in range(2)]
            ada_acc = tb("ada_acc", [P, 2 * PAIR])
            ada_accs = [ada_acc] + scratch
        with ExitStack() as s:
            y_tok = holder(s)("y_tok", [P, NT, D])
        mb = holder(ctx.enter_context(ExitStack()))
        cst = mb("cst", [P, N_SMALL])
        pre = mb("pre", [P, 12, T + 6])
        z_t = mb("z_t", [P, HB, T])
        vecs = mb("vecs", [P, 3, 16])
        g_t, beta, gc, egc, ekg, gl, sp_a, sp_b = [
            mb(n, [P, NT, 16]) for n in ("g_t", "beta", "gc", "egc", "ekg", "gl", "sp_a", "sp_b")]
        dn_col = mb("dn_col", [P, 1])
        with ExitStack() as s:
            tb = holder(s)
            rope_sb = tb("rope_sb", [P, 2 * TS])
            ones_1 = tb("ones_1", [P, P])
            exps = [tb(f"exps{i}", [P, T]) for i in range(2)]
            with ExitStack() as s2:
                gate_w = holder(s2)("gate_w", [P, KD * NDB])
                gate_hi = holder(s2)("gate_hi", [P, KD * NDB], F32R)
            nk_tok = tb("nk_tok", [P, HB * P])
            gate_lo = tb("gate_lo", [P, KD * NDB], F32R)
            conv_acc = [tb(f"conv_acc{i}", [P, T + 2]) for i in range(2)]
            q_b = tb("q_b", [P, HB, T])
            k_b = tb("k_b", [P, HB, T])
            k_all = tb("k_all", [P, HB, T])
            v_b = tb("v_b", [P, NT, HB * P])
            ck_tok = tb("ck_tok", [P, HB * P])
            cv_tok = tb("cv_tok", [P, HB * P])
            lam_in = tb("lam_in", [P, 4, DK])
            lam_t = tb("lam_t", [P, 8])
            att_s = tb("att_s", [P, 2, 8])
            att_v = tb("att_v", [P, T])
            att_wt = tb("att_wt", [P, T])
            att_p = [conv_acc, exps]
            rot_sin = [att_v, att_wt]
            att_w = sumsq
            att_q = q_b
        with ExitStack() as s:
            tb = holder(s)
            k_tok = tb("k_tok", [P, NT, HA * DK])
            v_tok = tb("v_tok", [P, NT, HA * DK])
            o_acc = pre[:, 8:12, :].rearrange("p a b -> p (a b)")[:, 0:NT * HA * DK].rearrange("p (t n) -> p t n", t=NT)
            st = [tb(f"st{i}", [P, 2, 4, P]) for i in range(2)]
            t_all = tb("t_all", [P, NT, 2, 4 * P])
            make = [[tb(f"{n}{c}", [P, 4, P]) for c in range(2)] for n in ("m_t", "x_w", "t_cols", "tt_cols")]
            t_one, p_one = make[0] + make[1], make[2] + make[3]
            for x, more in zip(make, spare):
                x += more
            m_t, x_w, t_cols, tt_cols = make
            r_s = [tb(f"r_s{i}", [P, 256]) for i in range(4)]
            u_s = r_s
            kg = [square[i // 2][:, (i % 2) * 256:(i % 2) * 256 + 256] for i in range(4)]
            oq = [x[:, i * 256:i * 256 + 256] for x in (rstd, sumsq) for i in range(2)]
            sq_o = [t_all[:, t, 0, :] for t in range(NT)]
            o_sum = tb("o_sum", [P, NT, HA])
        ps = ctx.enter_context(nc.psum_tensor("ps", [P, 8, 512], F32))

        def const(name):
            i = CONST_NAMES.index(name)
            return cst[:, i * P:(i + 1) * P]

        def over4(x):
            return x[:, None, :].broadcast_to([P, 4, P])

        def make_schedule():
            for at in range((2 * NT - 1) * MAKE_LAG + MAKE_STAGES):
                for u in range(2 * NT):
                    k = at - u * MAKE_LAG
                    if 0 <= k < MAKE_STAGES:
                        yield k, u % 4, u // 4, MAKE_ORDER[u // 2], u % 2

        w_landed = [sem(f"w_landed{i}") for i in range(2)]
        w_hi_ready, w_lo_ready, tile_done = sem("w_hi_ready"), sem("w_lo_ready"), sem("tile_done")
        small_in, x_in = sem("small_in"), sem("x_in")
        ada_landed = [sem(f"ada_landed{i}") for i in range(8)]
        ada_in = [sem(f"ada_in{i}") for i in range(2)]
        ada_read, ada_summed, mods_ready = sem("ada_read"), sem("ada_summed"), sem("mods_ready")
        ada_used, ones_set = sem("ada_used"), sem("ones_set")
        cols_turned, cols_ready, cond_ready = sem("cols_turned"), sem("cols_ready"), sem("cond_ready")
        x_turned, x_copied = sem("x_turned"), sem("x_copied")
        dve_own, act_own, pool_own = sem("dve_own"), sem("act_own"), sem("pool_own")
        sq_ready, sq_added, x_updated = sem("sq_ready"), sem("sq_added"), sem("x_updated")
        mean_mm, var_ready, sd_ready = sem("mean_mm"), sem("var_ready"), sem("sd_ready")
        scales_ready, rstd_ready, hn_ready, hf_ready, h_ready = sem("scales_ready"), sem("rstd_ready"), sem("hn_ready"), sem("hf_ready"), sem("h_ready")
        silu_ready, act_ready, acthi_ready, actlo_ready = (sem("silu_ready"), sem("act_ready"),
                                                           sem("acthi_ready"), sem("actlo_ready"))
        mix_in, proj_out, conv_ready, conv_silu = sem("mix_in"), sem("proj_out"), sem("conv_ready"), sem("conv_silu")
        pads_set, gate_split, gate_mm, vb_ready = sem("pads_set"), sem("gate_split"), sem("gate_mm"), sem("vb_ready")
        sc_pe, sc_act, sc_dve = sem("scalars_pe"), sem("scalars_act"), sem("scalars_dve")
        l2_sq, l2_mm, l2_var, l2_sd, l2_done = [sem("l2_" + n) for n in ("sq", "mm", "var", "sd", "done")]
        rot_mm, rot_cos, rot_done = sem("rot_mm"), sem("rot_cos"), sem("rot_done")
        kt_turned, kt_copied = sem("kt_turned"), sem("kt_copied")
        s_mm, s_max, s_exp, s_wts, s_turn, s_turned, s_pv, s_out = [
            sem("att_" + n) for n in ("scores", "max", "exp", "weights", "turn", "turned", "pv", "out")]
        an_sq, an_mm, an_var, an_sd, an_tmp, an_hi, an_done = [
            sem("att_norm_" + n) for n in ("sq", "mm", "var", "sd", "tmp", "hi", "done")]
        kv_out, st_out, st_in, st_clear, y_out = sem("kv_out"), sem("st_out"), sem("st_in"), sem("st_clear"), sem("y_out")
        kv_turned, kv_copied = sem("kv_turned"), sem("kv_copied")
        t_pe, t_dve, t_act, t_pool = [[sem(f"make_t_{n}{c}") for c in range(4)] for n in ("pe", "dve", "act", "pool")]
        c_pe, c_dve, c_pool = [[sem(f"scan_{n}{b}") for b in range(4)] for n in ("pe", "dve", "pool")]
        o_pe, o_dve, o_act = sem("delta_out_pe"), sem("delta_out_dve"), sem("delta_out_act")
        o_normed, o_scaled, o_hi, o_lo = [sem("delta_out_" + n) for n in ("normed", "scaled", "hi", "lo")]
        y_scaled, y_turned, y_copied = sem("y_scaled"), sem("y_turned"), sem("y_copied")

        block = ctx.enter_context(nc.Block())
        X_BASE = [0, 16]
        SEQ = [1, 3]
        ffn_w = [(w_ffn1_in, w_ffn1_out), (w_ffn2_in, w_ffn2_out)]
        win = w_in[0].rearrange("(k p) n -> p k n", p=P)

        @block.sync
        def _(sp):
            rows = [(0, b_ada[0].rearrange("(m p) -> m p", p=P)), (72, c.rearrange("a (m p) -> (a m) p", p=P)),
                    (80, c_ctx.rearrange("(m p) -> m p", p=P)), (88, norm_ffn1[0].rearrange("(m p) -> m p", p=P)),
                    (96, norm_mix[0].rearrange("(m p) -> m p", p=P)),
                    (104, norm_ffn2[0].rearrange("(m p) -> m p", p=P)),
                    (112, norm_final.rearrange("(m p) -> m p", p=P))]
            sp.dma_start(ident[:], consts[:, 0:P]).then_inc(small_in, 16)
            for at, src in rows:
                sp.dma_start(rows_a[at:at + src.shape[0], :], src).then_inc(small_in, 16)
            sp.dma_start(rows_b[0:60, :], conv_w[0].rearrange("t (m p) -> (t m) p", p=P)).then_inc(small_in, 16)
            for k in range(2):
                sp.dma_start(rows_b[60:61, k * DK:(k + 1) * DK], delta_norm).then_inc(small_in, 16)
            sp.dma_start(rows_b[61:62, :], diff_norm).then_inc(small_in, 16)
            sp.dma_start(x_tok[:, 0, :], x_prompt[0]).then_inc(x_in, 16)
            sp.dma_start(x_tok[:, 1:NT, :], x_sample[0].rearrange("(t p) d -> p t d", p=P)).then_inc(x_in, 16)
            ada_v = w_ada[0].rearrange("(k p) n -> p k n", p=P)

            for n in range(2 * KD):
                if n >= 8:
                    sp.wait_ge(ada_used, n - 7)
                sp.dma_start(ada_ring[n % 8][:].rearrange("p (k n) -> p k n", k=KD),
                             ada_v[:, :, n * P:(n + 1) * P]).then_inc(ada_landed[n % 8], 16)

            def ada_load(i, q, first=False):
                if not first:
                    sp.wait_ge(ada_read, i * 2 + (q - 1))
                col = i * PAIR + 2 * KD * P
                src = ada_v[:, 4 * q:4 * q + 4, col:col + PAIR] if isinstance(i, int) else \
                    ada_v[:, 4 * q:4 * q + 4, bass.ds(col, PAIR)]
                sp.dma_start(ada_ffn[q][:].rearrange("p (k n) -> p k n", k=4), src).then_inc(ada_in[q], 16)

            def w_load(n, s, src, first=False):
                if not first:
                    sp.wait_ge(w_lo_ready, n - 1)
                sp.dma_start(w_raw[s][:].rearrange("p (a b) -> p a b", a=src.shape[1]), src)\
                    .then_inc(w_landed[s], 16)

            def ffn_loads(f):
                base = TILE_FFN[f]
                wi = ffn_w[f][0][0].rearrange("(k p) n -> p k n", p=P)
                wo = ffn_w[f][1][0].rearrange("(j p) n -> p j n", p=P)
                for k in range(2):
                    w_load(base + k, k, wi[:, :, k * DFF:k * DFF + P], first=(f == 0))
                if f == 0:
                    sp.wait_ge(x_copied, 2 * NT)
                    sp.wait_ge(ada_used, 2 * KD)
                    for k in range(2):
                        ada_load(0, k, first=True)
                with sp.Fori(0, NJ - 1) as j:
                    for k in range(2):
                        w_load(j * 2 + (base + 2 + k), k, wi[:, :, bass.ds(j * P + (k * DFF + P), P)])
                    if f == 0:
                        for k in range(2):
                            ada_load(j + 1, k)
                for hf in range(2):
                    n = base + N_IN + 11 * hf
                    cols = slice(hf * 512, hf * 512 + 512)
                    w_load(n, n % 2, wo[:, 0:2, cols])
                    if f == 0:
                        for i in range(1, 11):
                            w_load(n + i, (n + i) % 2, wo[:, 2 * i:2 * i + 2, cols])
                            if i <= 6:
                                ada_load(NJ + 3 * hf + (i - 1) // 2, (i - 1) % 2)
                        continue
                    with sp.Fori(0, 5) as i:
                        for k in range(2):
                            w_load(i * 2 + (n + 1 + k), (n + 1 + k) % 2, wo[:, bass.ds(i * 4 + (2 + 2 * k), 2), cols])

            ffn_loads(0)
            sp.wait_ge(tile_done, FFN_TILES)
            sp.dma_start(cst[:], consts).then_inc(mix_in, 16)
            sp.dma_start(rope_sb[:], rope).then_inc(mix_in, 16)
            sp.dma_start(gate_w[:].rearrange("p (k n) -> p k n", k=KD), win[:, :, COL_DEC:COL_DEC + NDB]).then_inc(mix_in, 16)
            sp.dma_start(vecs[:, 0, :], a_log.rearrange("a d h -> a (d h)").broadcast_to([P, 16])).then_inc(mix_in, 16)
            sp.dma_start(vecs[:, 1, :], dt_bias.rearrange("a d h -> a (d h)").broadcast_to([P, 16])).then_inc(mix_in, 16)
            for i, v in enumerate((lambda_q1, lambda_k1, lambda_q2, lambda_k2)):
                sp.dma_start(lam_in[:, i, :], v.broadcast_to([P, DK])).then_inc(mix_in, 16)
            sp.dma_start(ck_tok[:], cache_diff_k[0, 0].rearrange("t h m d -> t (h m d)")).then_inc(mix_in, 16)
            sp.dma_start(cv_tok[:], cache_diff_v[0, 0].rearrange("t h e -> t (h e)")).then_inc(mix_in, 16)
            for i0, iters, col in ((0, 8, 0), (16, 4, COL_B)):
                with sp.Fori(0, iters) as i:
                    for k in range(2):
                        w_load(i * 2 + (TILE_WIN + i0 + k), k, win[:, :, bass.ds(i * (2 * P) + (col + k * P), P)])
            for q in range(4):
                w_load(TILE_WBV + q, q % 2, win[:, 2 * q:2 * q + 2, COL_B + 1024:COL_B + 1536])
            wo = w_out[0].rearrange("(k p) n -> p k n", p=P)
            for m in range(2):
                w_load(TILE_WOUT + m, m % 2, wo[:, :, m * P:(m + 1) * P])
            sp.wait_ge(vb_ready, 1)
            sp.dma_start(new_v, v_b[:, 0, :]).then_inc(kv_out, 16)
            sp.wait_ge(kt_copied, 1)
            sp.dma_start(new_k, nk_tok[:]).then_inc(kv_out, 16)
            sp.wait_ge(st_clear, 3)
            for d in range(2):
                for e in range(2):
                    sp.dma_start(st[1][e * DK:(e + 1) * DK, d, :, e * DK:(e + 1) * DK],
                                 state_delta[0, 0, d].rearrange("(c e) k v -> e k c v", e=2)[e]).then_inc(st_in, 16)
            for b in range(4):
                sp.wait_ge(c_dve[b], DVE_C)
            for d in range(2):
                for e in range(2):
                    sp.dma_start(new_state[d].rearrange("(c e) k v -> e k c v", e=2)[e],
                                 st[0][e * DK:(e + 1) * DK, d, :, e * DK:(e + 1) * DK]).then_inc(st_out, 16)
            with sp.Fori(0, 3) as i:
                for k in range(2):
                    w_load(i * 2 + (TILE_WOUT + 2 + k), k, wo[:, :, bass.ds(i * (2 * P) + (2 + k) * P, P)])
            ffn_loads(1)
            for t in range(NT):
                sp.wait_ge(y_copied, 2 * (t + 1))
                dst = y_prompt[0] if t == 0 else y_sample[0, (t - 1) * P:t * P, :]
                sp.dma_start(dst, y_tok[:, t, :]).then_inc(y_out, 16)
            sp.wait_ge(y_out, 16 * NT)
            sp.wait_ge(kv_out, 32)
            sp.wait_ge(st_out, 64)

        @block.scalar
        def _(act):
            own = Chain(act, act_own)

            def w_high(n, s, first=False):
                act.wait_ge(w_landed[s], n * 8 + (16 - 8 * s))
                if not first:
                    act.wait_ge(tile_done, n - 1)
                nc.scalar.copy(w_hi[s][:], w_raw[s][:]).then_inc(w_hi_ready, 1)

            def square_of(k, seq, after):
                if after is not None:
                    act.wait_ge(x_updated, after + k + 1)
                if seq * 8 + k >= 2:
                    act.wait_ge(sq_added, seq * 8 + k - 1)
                nc.scalar.activation(square[k % 2][:], x_t[:, k, :], ACT.Square).then_inc(sq_ready, 1)

            def norm(seq):
                nc.scalar.activation(root_dummy[:], ident[:, 0:1], ACT.Sqrt)
                act.wait_ge(var_ready, seq + 1)
                nc.scalar.activation(rstd[:], rstd[:], ACT.Sqrt).then_inc(sd_ready, 1)

            def modulate(nth):
                act.wait_ge(scales_ready, nth + 1)
                for k in range(KD):
                    act.wait_ge(hn_ready, nth * 8 + k + 1)
                    if k >= 2:
                        act.wait_ge(h_ready, nth * 8 + k - 1)
                    for grp, a, b in ((0, 0, TC), (1, TC, T)):
                        ins = nc.scalar.activation(square[k % 2][:, a:b], scratch[k % 2][:, a:b], ACT.Identity,
                                                   bias=mods[:, 24 * nth + k, grp:grp + 1],
                                                   scale=scales[:, nth, k, grp:grp + 1])
                    ins.then_inc(hf_ready, 1)

            def ffn(f):
                base, J = TILE_FFN[f], NJ * f

                def hidden(j, par, first):
                    w_high(j * 2 + (base + 1), 1, first=(f == 0 and first and par == 0))
                    act.wait_ge(tile_done, j * 2 + (base + 1))
                    if not first:
                        act.wait_ge(act_ready, j + (J - 1))
                    nc.scalar.activation(halves(silu_g[par][:]), ps[:, 4 * par:4 * par + 2, 0:HT],
                                         ACT.Silu).then_inc(silu_ready, 1)
                    w_high(j * 2 + (base + 2), 0)
                    act.wait_ge(act_ready, j + (J + 1))
                    nc.scalar.copy(pick(act_hi, j), act_f[par][:]).then_inc(acthi_ready, 1)

                hidden(0, 0, True)
                hidden(1, 1, True)
                with act.Fori(0, NJ // 2 - 1) as i:
                    for k in range(2):
                        hidden(i * 2 + (2 + k), k, False)
                for hf in range(2):
                    n = base + N_IN + 11 * hf
                    with act.Fori(0, 5) as i:
                        for k in range(2):
                            w_high(i * 2 + (n + 1 + k), (n + 1 + k) % 2)
                    if n + 11 < N_TILES:
                        w_high(n + 11, (n + 11) % 2)
                    for k in range(4 * hf, 4 * hf + 4):
                        square_of(k, SEQ[f], X_BASE[f])

            act.wait_ge(cols_turned, 2)
            nc.scalar.copy(cols_a[:], ps[:, 0, 0:120]).then_inc(cols_ready, 1)
            nc.scalar.copy(cols_b[:], ps[:, 1, 0:62]).then_inc(cols_ready, 1)
            act.wait_ge(cols_ready, 2)
            nc.scalar.activation(cond[:, :, 1], cols_a[:, 72:80], ACT.Silu).then_inc(cond_ready, 1)
            nc.scalar.activation(cond[:, :, 0], cols_a[:, 80:88], ACT.Silu).then_inc(cond_ready, 1)
            for i in range(2 * NT):
                t, q = i // 2, i % 2
                act.wait_ge(x_turned, i + 1)
                nc.scalar.copy(x_t[:, 4 * q:4 * q + 4, t * P:(t + 1) * P], heads4(ps[:, 2 + i % 4, :], P)).then_inc(x_copied, 1)
            act.wait_ge(x_copied, 2 * NT)
            for k in range(KD):
                square_of(k, 0, None)
            norm(0)
            w_high(0, 0, first=True)
            modulate(0)
            ffn(0)
            norm(1)
            modulate(1)

            def to_conv(m, k):
                w_high(m + (TILE_WIN + 1), 1 - k)
                act.wait_ge(tile_done, m + (TILE_WIN + 1))
                for grp, half, col, tok, ln in SEGS:
                    a = 2 + tok + 2 * grp
                    ins = nc.scalar.copy(pick(pre, m, slice(a, a + ln)), ps[:, 2 * k + half, col:col + ln])
                ins.then_inc(proj_out, 1)

            def from_conv(m, k):
                act.wait_ge(conv_ready, m + 1)
                nc.scalar.activation(pick(pre, m, slice(0, TC)), conv_acc[k][:, 0:TC], ACT.Silu)
                nc.scalar.activation(pick(pre, m, slice(TC, T)), conv_acc[k][:, TC + 2:T + 2], ACT.Silu)\
                    .then_inc(conv_silu, 1)

            act.wait_ge(pads_set, 3)
            to_conv(0, 0)
            to_conv(1, 1)
            from_conv(0, 0)
            with act.Fori(0, 5) as i:
                for k in range(2):
                    to_conv(i * 2 + (2 + k), k)
                    from_conv(i * 2 + (1 + k), 1 - k)
            act.wait_ge(mix_in, 16 * 11)
            for m in range(12, 28):
                if m < 27:
                    w_high(TILE_WIN + m + 1, (m + 1) % 2)
                if m == 12:
                    from_conv(11, 1)
                if m < 24:
                    act.wait_ge(tile_done, TILE_WIN + m + 1)
                    src = ps[:, 2 * (m % 2):2 * (m % 2) + 2, 0:HT]
                if m < 16:
                    nc.scalar.activation(halves(z_t[:, m - 12, :]), src, ACT.Silu).then_inc(proj_out, 1)
                elif m < 24:
                    dst = q_b[:, m - 16, :] if m < 20 else k_b[:, m - 20, :]
                    nc.scalar.copy(halves(dst), src).then_inc(proj_out, 1)
                if m == 12:
                    nc.scalar.copy(gate_hi[:], gate_w[:]).then_inc(gate_split, 1)
                if m == 14:
                    act.wait_ge(sc_dve, 1)
                    nc.scalar.activation(sp_a[:], sp_a[:], ACT.Exp, scale=-1.0).then_inc(sc_act, 1)
                    nc.scalar.activation(beta[:], beta[:], ACT.Exp, scale=-1.0).then_inc(sc_act, 1)
                    nc.scalar.activation(vecs[:, 2, :], vecs[:, 0, :], ACT.Exp).then_inc(sc_act, 1)
                    nc.scalar.activation(lam_t[:, 2:4], lam_t[:, 0:2], ACT.Exp).then_inc(sc_act, 1)
                if m == 15:
                    act.wait_ge(sc_dve, 2)
                    nc.scalar.activation(sp_a[:], sp_a[:], ACT.Ln).then_inc(sc_act, 1)
                if m == 17:
                    act.wait_ge(sc_dve, 4)
                    nc.scalar.activation(egc[:], gc[:], ACT.Exp).then_inc(sc_act, 1)
                    nc.scalar.activation(ekg[:], ekg[:], ACT.Exp).then_inc(sc_act, 1)
                    nc.scalar.activation(gl[:], gl[:], ACT.Exp).then_inc(sc_act, 1)
                if 14 <= m < 22:
                    i = m - 14
                    if i == 0:
                        act.wait_ge(conv_silu, 12)
                    if i >= 2:
                        act.wait_ge(l2_mm, i - 1)
                    nc.scalar.activation(square[i % 2][:], pre[:, i, 0:T], ACT.Square).then_inc(l2_sq, 1)
                if 16 <= m < 24:
                    i = m - 16
                    act.wait_ge(l2_var, i + 1)
                    nc.scalar.activation(scratch[i % 2][:], scratch[i % 2][:], ACT.Sqrt).then_inc(l2_sd, 1)
                if m == 25:
                    act.wait_ge(kt_turned, 1)
                    nc.scalar.copy(nk_tok[:], ps[:, 6, :]).then_inc(kt_copied, 1)
                if m == 27:
                    act.wait_ge(kt_turned, 2)
                    nc.scalar.copy(k_all[:, :, 0:P], heads4(ps[:, 6, :], P)).then_inc(kt_copied, 1)
            act.wait_ge(tile_done, TILE_WBV + 4)
            for t in range(NT):
                ins = nc.scalar.copy(v_b[:, t, :], ps[:, t, :])
            ins.then_inc(vb_ready, 1)

            def weights_out(v):
                nk = ATT_UNITS[v][2]
                act.wait_ge(s_turn, v + 1)
                if v >= 1:
                    act.wait_ge(s_pv, v)
                if nk == P:
                    nc.scalar.copy(att_wt[:, 0:P], ps[:, 4, 0:P]).then_inc(s_turned, 1)
                else:
                    nc.scalar.copy(att_wt[:, 0:512], ps[:, 4, :])
                    nc.scalar.copy(att_wt[:, 512:T], ps[:, 5, 0:P]).then_inc(s_turned, 1)

            act.wait_ge(rot_done, 8)
            for v, (hb, q0, nk) in enumerate(ATT_UNITS):
                for m in range(2):
                    act.wait_ge(s_max, 2 * v + m + 1)
                    if m == 0 and v >= 2:
                        act.wait_ge(s_wts, v - 1)
                    x = att_p[v % 2][m]
                    if nk == P:
                        src, dst = ps[:, 2 * m, 0:P], x[:, 0:P]
                    else:
                        src, dst = ps[:, 2 * m:2 * m + 2, 0:HT], halves(x[:, 0:T])
                    nc.scalar.activation(dst, src, ACT.Exp, bias=att_s[:, v % 2, m:m + 1], scale=DK ** -0.5,
                                         accum_out=att_s[:, v % 2, 2 + m:3 + m]).then_inc(s_exp, 1)
                if v >= 1:
                    weights_out(v - 1)
            weights_out(NU - 1)
            act.wait_ge(s_out, NU)
            for hb in range(HB):
                if hb >= 1:
                    act.wait_ge(an_mm, hb)
                nc.scalar.activation(square[0][:], att_q[:, hb, :], ACT.Square).then_inc(an_sq, 1)
                act.wait_ge(an_var, hb + 1)
                nc.scalar.activation(rstd[:], rstd[:], ACT.Sqrt).then_inc(an_sd, 1)
                act.wait_ge(an_tmp, hb + 1)
                nc.scalar.copy(h_hi[1][:, hb, :], scratch[0][:]).then_inc(an_hi, 1)

            act.wait_ge(an_done, 4)
            act.wait_ge(kv_out, 32)
            for i in range(2 * NT):
                act.wait_ge(kv_turned, i + 1)
                nc.scalar.copy((k_tok, v_tok)[i % 2][:, i // 2, :], ps[:, 4 + i % 4, :]).then_inc(kv_copied, 1)
            for k, c, r, t, g in make_schedule():
                if k == 0:
                    if r >= 1:
                        act.wait_ge(t_pe[c], r * PE_T)
                    for d, x, m in ((0, m_t[c], "after"), (1, tt_cols[c], "before")):
                        for h in range(4):
                            q = 8 * d + 4 * g + h
                            ins = nc.scalar.activation(x[:, h, :], const(m), ACT.Copy, scale=beta[:, t, q:q + 1])
                        ins.then_inc(t_act[c], 1)
                if k == 3:
                    act.wait_ge(t_dve[c], r * DVE_T + 3)
                    nc.scalar.activation(x_w[c][:], x_w[c][:], ACT.Exp).then_inc(t_act[c], 1)
            for c in range(4):
                act.wait_ge(t_pe[c], ROUNDS[c] * PE_T)
            w_high(TILE_WOUT, 0)
            for b in range(4):
                act.wait_ge(c_dve[b], NT * DVE_C)
            for t in range(NT):
                nc.scalar.activation(sq_o[t], o_acc[:, t, :], ACT.Square).then_inc(o_act, 1)
            act.wait_ge(o_dve, 1)
            nc.scalar.activation(o_sum[:], o_sum[:], ACT.Sqrt).then_inc(o_act, 1)
            for t in range(NT):
                act.wait_ge(o_scaled, t + 1)
                nc.scalar.copy(h_hi[0][:, :, t * P:(t + 1) * P], heads4(scratch[t % 2][:, 0:512], P)).then_inc(o_hi, 1)
            for m in range(8):
                w_high(TILE_WOUT + m + 1, (m + 1) % 2)
                square_of(m, 2, 8)
            norm(2)
            modulate(2)
            act.wait_ge(st_out, 64)
            ffn(1)
            norm(3)
            for i in range(2 * NT):
                act.wait_ge(y_turned, i + 1)
                nc.scalar.copy(y_tok[:, i // 2, (i % 2) * 512:(i % 2) * 512 + 512], ps[:, i % 4, :]).then_inc(y_copied, 1)

        @block.vector
        def _(dve):
            own = Chain(dve, dve_own)

            def w_low(n, s):
                dve.wait_ge(w_hi_ready, n + 1)
                nc.vector.tensor_tensor(w_lo[s][:], w_raw[s][:], w_hi[s][:].bitcast(F32), ALU.subtract)\
                    .then_inc(w_lo_ready, 1)

            def norm(seq):
                dve.wait_ge(mean_mm, seq + 1)
                nc.vector.tensor_scalar(halves(rstd[:]), ps[:, 0:2, 0:HT], EPS, None, ALU.add).then_inc(var_ready, 1)
                dve.wait_ge(sd_ready, seq + 1)
                nc.vector.reciprocal(rstd[:], rstd[:]).then_inc(rstd_ready, 1)

            def modulate(nth):
                if nth == 1:
                    dve.wait_ge(mods_ready, NJ + 2)
                nc.vector.scalar_tensor_tensor(scales[:, nth], mods[:, 24 * nth + 8:24 * nth + 16, :], 1.0,
                                               spread(cols_a[:, 88 + 8 * nth:96 + 8 * nth], 2),
                                               op0=ALU.add, op1=ALU.mult).then_inc(scales_ready, 1)
                for k in range(KD):
                    dve.wait_ge(hf_ready, nth * 8 + k + 1)
                    hi, lo = h_hi[k // 4][:, k % 4, :], h_lo[k // 4][:, k % 4, :]
                    own.link(nc.vector.tensor_copy(hi, square[k % 2][:]))
                    nc.vector.tensor_tensor(lo, square[k % 2][:], hi.bitcast(F32), ALU.subtract).then_inc(h_ready, 1)

            def update_x(m, banks, gate):
                for grp, half, col, tok, ln in SEGS:
                    ins = nc.vector.scalar_tensor_tensor(x_t[:, m, tok:tok + ln], ps[:, banks + half, col:col + ln],
                                                         mods[:, gate * KD + m, grp:grp + 1], x_t[:, m, tok:tok + ln],
                                                         op0=ALU.mult, op1=ALU.add)
                ins.then_inc(x_updated, 1)

            def ada_part(i, q, acc):
                dve.wait_ge(ada_in[q], i * 16 + 16)
                for k in range(4):
                    w = ada_ffn[q][:, k * PAIR:(k + 1) * PAIR]
                    for g in range(2):
                        a, col = acc[:, g * PAIR:(g + 1) * PAIR], cond[:, 4 * q + k, g:g + 1]
                        if q == 0 and k == 0:
                            ins = nc.vector.tensor_scalar(a, w, col, None, ALU.mult)
                        else:
                            own.wait_back(1)
                            ins = nc.vector.scalar_tensor_tensor(a, w, col, a, op0=ALU.mult, op1=ALU.add)
                        if k == 3 and g == 1:
                            ins.then_inc(ada_read, 1)
                            if q == 0:
                                dve.wait_ge(ada_read, i * 2 + 1)
                        else:
                            own.mark(ins)

            def mods_of(i, bank, n):
                m = i * 2 + 2 * KD
                at = slice(m, m + 2 * n) if isinstance(i, int) else bass.ds(m, 2 * n)
                nc.vector.tensor_tensor(mods[:, at, :], ps[:, bank, 400:400 + 4 * n].rearrange("p (m a) -> p m a", a=2),
                                        spread(cols_a[:, at], 2), ALU.add).then_inc(mods_ready, 1)

            def ffn(f):
                base, J = TILE_FFN[f], NJ * f

                def hidden(j, par, first=False):
                    w_low(j * 2 + (base + 1), 1)
                    w_low(j * 2 + (base + 2), 0)
                    if f == 0:
                        if not first:
                            dve.wait_ge(ada_summed, j)
                        for q in range(2):
                            ada_part(j, q, ada_acc)
                    dve.wait_ge(tile_done, j * 2 + (base + 2))
                    if f == 0 and not first:
                        mods_of(j - 1, 4 * par + 2, 1)
                    dve.wait_ge(silu_ready, j + (J + 1))
                    nc.vector.tensor_tensor(halves(act_f[par][:]), halves(silu_g[par][:]),
                                            ps[:, 4 * par + 2:4 * par + 4, 0:HT], ALU.mult).then_inc(act_ready, 1)
                    dve.wait_ge(acthi_ready, j + (J + 1))
                    nc.vector.tensor_tensor(pick(act_lo, j), act_f[par][:], pick(act_hi, j).bitcast(F32),
                                            ALU.subtract).then_inc(actlo_ready, 1)

                if f == 0:
                    hidden(0, 0, first=True)
                    hidden(1, 1)
                    with dve.Fori(0, NJ // 2 - 1) as i:
                        own.loop(i, 2 * ADA_MARKS)
                        for k in range(2):
                            hidden(i * 2 + (2 + k), k)
                        own.done(NJ // 2 - 1)
                else:
                    with dve.Fori(0, NJ // 2) as i:
                        for k in range(2):
                            hidden(i * 2 + k, k)
                gate = mods[:, (2 + 6 * f) * KD:(3 + 6 * f) * KD, :]
                if f == 0:
                    dve.wait_ge(mods_ready, NJ - 1)
                own.link(nc.vector.tensor_scalar(gate, gate, 0.5, None, ALU.mult))
                for hf in range(2):
                    n = base + N_IN + 11 * hf
                    if f == 0:
                        dve.wait_ge(ada_summed, NJ + 3 * hf)
                        for i in range(1, 11):
                            w_low(n + i, (n + i) % 2)
                            if i <= 6:
                                ada_part(NJ + 3 * hf + (i - 1) // 2, (i - 1) % 2, ada_accs[(i - 1) // 2])
                    else:
                        with dve.Fori(0, 5) as i:
                            for k in range(2):
                                w_low(i * 2 + (n + 1 + k), (n + 1 + k) % 2)
                    if n + 11 < N_TILES:
                        w_low(n + 11, (n + 11) % 2)
                    dve.wait_ge(tile_done, n + 11)
                    if f == 0:
                        mods_of((NJ - 1, NJ)[hf], 0, (1, 3)[hf])
                    for mm in range(4):
                        update_x(4 * hf + mm, 2 * mm, 2 + 6 * f)
                if f == 0:
                    dve.wait_ge(ada_summed, NJ + 6)
                    mods_of(NJ + 3, 7, 3)

            nc.vector.memset(ones_col[:], 1.0)
            nc.vector.memset(ones_d[:], 1.0 / D).then_inc(ones_set, 1)
            dve.wait_ge(x_copied, 2 * NT)
            norm(0)
            w_low(0, 0)
            dve.wait_ge(cols_ready, 2)
            dve.wait_ge(ada_used, 2 * KD)
            own.link(nc.vector.tensor_tensor(mods[:, 0:2 * KD, :], ps[:, 7, 0:4 * KD].rearrange("p (m a) -> p m a", a=2),
                                             spread(cols_a[:, 0:2 * KD], 2), ALU.add))
            modulate(0)
            ffn(0)
            norm(1)
            modulate(1)

            def conv(m, k):
                w_low(m + (TILE_WIN + 1), 1 - k)
                dve.wait_ge(proj_out, m + 1)
                if not isinstance(m, int) or m >= 2:
                    dve.wait_ge(conv_silu, m - 1)
                tap = lambda t: cols_b[:, bass.ds(m + 12 * t, 1)] if not isinstance(m, int) else cols_b[:, m + 12 * t:m + 12 * t + 1]
                own.link(nc.vector.tensor_scalar(conv_acc[k][:], pick(pre, m, slice(0, T + 2)), tap(0), None, ALU.mult))
                for t in range(1, CONV):
                    ins = nc.vector.scalar_tensor_tensor(conv_acc[k][:], pick(pre, m, slice(t, t + T + 2)), tap(t),
                                                         conv_acc[k][:], op0=ALU.mult, op1=ALU.add)
                    if t < CONV - 1:
                        own.link(ins)
                ins.then_inc(conv_ready, 1)

            conv(0, 0)
            conv(1, 1)
            with dve.Fori(0, 5) as i:
                own.loop(i, 2 * (CONV - 1))
                for k in range(2):
                    conv(i * 2 + (2 + k), k)
                own.done(5)
            def l2_mean(i):
                dve.wait_ge(l2_mm, i + 1)
                if i >= 2:
                    dve.wait_ge(l2_done, i - 1)
                nc.vector.tensor_scalar(halves(scratch[i % 2][:]), ps[:, 4:6, 0:HT], EPS, None, ALU.add).then_inc(l2_var, 1)

            def l2_scale(i):
                dve.wait_ge(l2_sd, i + 1)
                own.link(nc.vector.reciprocal(scratch[i % 2][:], scratch[i % 2][:]))
                nc.vector.scalar_tensor_tensor(pre[:, i, 0:T], pre[:, i, 0:T], DK ** -0.5 if i < 4 else 1.0,
                                               scratch[i % 2][:], op0=ALU.mult, op1=ALU.mult).then_inc(l2_done, 1)

            def rotate(r):
                dst = q_b[:, r % 4, TC:T] if r < 4 else k_all[:, r % 4, TC:T]
                dve.wait_ge(rot_mm, r + 1)
                own.link(nc.vector.tensor_tensor(rot_sin[r % 2][:, 0:TS], ps[:, 7, :], rope_sb[:, TS:2 * TS], ALU.mult))
                dve.wait_ge(rot_cos, r + 1)
                nc.vector.tensor_tensor(dst, rot_sin[r % 2][:, 0:TS], conv_acc[r % 2][:, 0:TS], ALU.add).then_inc(rot_done, 1)

            dve.wait_ge(mix_in, 16 * 11)
            for m in range(12, 28):
                if m < 27:
                    w_low(TILE_WIN + m + 1, (m + 1) % 2)
                if m == 12:
                    dve.wait_ge(gate_split, 1)
                    nc.vector.tensor_tensor(gate_lo[:], gate_w[:], gate_hi[:].bitcast(F32), ALU.subtract).then_inc(gate_split, 1)
                if m == 13:
                    dve.wait_ge(gate_mm, 1)
                    raw = ps[:, 6, 0:NT * NDB].rearrange("p (t n) -> p t n", t=NT)
                    own.link(nc.vector.tensor_tensor(sp_b[:], raw[:, :, 0:16], vecs[:, 1:2, :].broadcast_to([P, NT, 16]), ALU.add))
                    own.link(nc.vector.scalar_tensor_tensor(sp_a[:], sp_b[:], -1.0, sp_b[:], op0=ALU.mult, op1=ALU.max))
                    own.link(nc.vector.tensor_copy(beta[:], raw[:, :, 16:32]))
                    own.link(nc.vector.tensor_tensor(lam_in[:, 0:2, :], lam_in[:, 0:4:2, :], lam_in[:, 1:4:2, :], ALU.mult))
                    nc.vector.tensor_reduce(lam_t[:, 0:2], lam_in[:, 0:2, :], AX.X, ALU.add).then_inc(sc_dve, 1)
                if m == 14:
                    dve.wait_ge(sc_act, 4)
                    nc.vector.tensor_scalar(sp_a[:], sp_a[:], 1.0, None, ALU.add).then_inc(sc_dve, 1)
                    own.link(nc.vector.tensor_scalar(beta[:], beta[:], 1.0, None, ALU.add))
                    own.link(nc.vector.reciprocal(beta[:], beta[:]))
                    own.link(nc.vector.tensor_tensor(lam_t[:, 4:5], lam_t[:, 2:3], lam_t[:, 3:4], ALU.subtract))
                    own.link(nc.vector.tensor_scalar(lam_t[:, 4:5], lam_t[:, 4:5], LAM_INIT, None, ALU.add))
                    nc.vector.tensor_scalar(dn_col[:], cols_b[:, 61:62], 1.0 - LAM_INIT, None, ALU.mult)
                if m == 15:
                    dve.wait_ge(sc_act, 5)
                    own.link(nc.vector.scalar_tensor_tensor(sp_a[:], sp_b[:], 0.0, sp_a[:], op0=ALU.max, op1=ALU.add))
                    nc.vector.scalar_tensor_tensor(g_t[:], sp_a[:], -1.0, vecs[:, 2:3, :].broadcast_to([P, NT, 16]),
                                                   op0=ALU.mult, op1=ALU.mult).then_inc(sc_dve, 1)
                if m == 16:
                    dve.wait_ge(sc_pe, 1)
                    sums = ps[:, 6, 0:240]
                    for d in range(2):
                        own.link(nc.vector.tensor_copy(gc[:, :, 8 * d:8 * d + 8],
                                                       sums[:, 40 * d:40 * d + 40].rearrange("p (t n) -> p t n", t=NT)))
                    total = sums[:, 80:160].rearrange("p (t n) -> p t n", t=NT)
                    own.link(nc.vector.tensor_copy(gl[:], total))
                    nc.vector.tensor_tensor(ekg[:], total, gc[:], ALU.subtract).then_inc(sc_dve, 1)
                if 15 <= m < 23:
                    l2_mean(m - 15)
                if 16 <= m < 24:
                    l2_scale(m - 16)
                if m >= 20:
                    rotate(m - 20)

            def att_max(v, m):
                nk = ATT_UNITS[v][2]
                dve.wait_ge(s_mm, 2 * v + m + 1)
                src = ps[:, 2 * m, 0:P] if nk == P else ps[:, 2 * m:2 * m + 2, 0:HT]
                own.link(nc.vector.tensor_reduce(att_s[:, v % 2, 6 + m:7 + m], src, AX.X if nk == P else AX.XY, ALU.max))
                nc.vector.tensor_scalar(att_s[:, v % 2, m:m + 1], att_s[:, v % 2, 6 + m:7 + m], -DK ** -0.5, None,
                                        ALU.mult).then_inc(s_max, 1)

            def att_weights(v):
                nk, a = ATT_UNITS[v][2], att_s[:, v % 2, :]
                dve.wait_ge(s_exp, 2 * v + 2)
                own.link(nc.vector.reciprocal(a[:, 4:6], a[:, 2:4]))
                own.link(nc.vector.tensor_tensor(a[:, 5:6], a[:, 5:6], lam_t[:, 4:5], ALU.mult))
                own.link(nc.vector.tensor_scalar(att_v[:, 0:nk], att_p[v % 2][1][:, 0:nk], a[:, 5:6], None, ALU.mult))
                if v >= 1:
                    dve.wait_ge(s_turn, v)
                nc.vector.scalar_tensor_tensor(att_w[:, 0:nk], att_p[v % 2][0][:, 0:nk], a[:, 4:5], att_v[:, 0:nk],
                                               op0=ALU.mult, op1=ALU.subtract).then_inc(s_wts, 1)

            def att_out(v):
                hb, q0, nk = ATT_UNITS[v]
                dve.wait_ge(s_pv, v + 1)
                nc.vector.tensor_copy(att_q[:, hb, q0:q0 + P], ps[:, 6, 0:P]).then_inc(s_out, 1)

            att_max(0, 0)
            att_max(0, 1)
            for v in range(NU):
                if v + 1 < NU:
                    att_max(v + 1, 0)
                att_weights(v)
                if v + 1 < NU:
                    att_max(v + 1, 1)
                if v >= 1:
                    att_out(v - 1)
            att_out(NU - 1)
            for hb in range(HB):
                dve.wait_ge(an_mm, hb + 1)
                nc.vector.tensor_scalar(halves(rstd[:]), ps[:, 0:2, 0:HT], D / P, EPS, ALU.mult, ALU.add).then_inc(an_var, 1)
                dve.wait_ge(an_sd, hb + 1)
                own.link(nc.vector.reciprocal(rstd[:], rstd[:]))
                nc.vector.scalar_tensor_tensor(scratch[0][:], att_q[:, hb, :], dn_col[:], rstd[:],
                                               op0=ALU.mult, op1=ALU.mult).then_inc(an_tmp, 1)
                dve.wait_ge(an_hi, hb + 1)
                nc.vector.tensor_tensor(h_lo[1][:, hb, :], scratch[0][:], h_hi[1][:, hb, :].bitcast(F32),
                                        ALU.subtract).then_inc(an_done, 1)

            dve.wait_ge(sc_act, 8)
            dve.wait_ge(st_clear, 3)
            def where(s, b):
                d, g = b // 2, b % 2
                return d, g, tile_of(s, d), 8 * d + 4 * g

            for k, c, r, t, g in make_schedule():
                pe0, bank = r * PE_T, 2 * c
                if k == 1:
                    for d, x, m in ((0, x_w[c], "after"), (1, t_cols[c], "before")):
                        q = 8 * d + 4 * g
                        dve.wait_ge(t_pe[c], pe0 + 1 + d)
                        for h in range(4):
                            ins = nc.vector.scalar_tensor_tensor(x[:, h, :], ps[:, bank + d, h * P:(h + 1) * P],
                                                                 gc[:, t, q + h:q + h + 1], const(m),
                                                                 op0=ALU.subtract, op1=ALU.mult)
                        ins.then_inc(t_dve[c], 1)
                if k == 2:
                    dve.wait_ge(t_dve[c], r * DVE_T + 2)
                    nc.vector.tensor_tensor(x_w[c][:], x_w[c][:], t_cols[c][:], ALU.add).then_inc(t_dve[c], 1)
                if k == 5:
                    dve.wait_ge(t_pe[c], pe0 + 4)
                    dve.wait_ge(t_pool[c], r * POOL_T + 2)
                    nc.vector.tensor_tensor(m_t[c][:], heads4(ps[:, bank, :], P), tt_cols[c][:], ALU.mult).then_inc(t_dve[c], 1)
                    dve.wait_ge(t_pe[c], pe0 + 6)
                    nc.vector.tensor_tensor(heads4(p_all[:, t, g, :], P), heads4(ps[:, bank + 1, :], P), x_w[c][:],
                                            ALU.mult).then_inc(t_dve[c], 1)
                n, part = divmod(k - 6, 3)
                if n >= 1 and part == 0:
                    dve.wait_ge(t_pe[c], pe0 + 8 + 3 * (n - 1))
                    nc.vector.tensor_tensor(x_w[c][:], heads4(ps[:, bank, :], P), over4(const(f"level{n}")),
                                            ALU.mult).then_inc(t_dve[c], 1)
                if n >= 1 and part == 1:
                    dve.wait_ge(t_pe[c], pe0 + 9 + 3 * (n - 1))
                    dve.wait_ge(t_pool[c], r * POOL_T + 4 + n)
                    nc.vector.tensor_tensor(t_all[:, t, g, :], t_all[:, t, g, :], ps[:, bank, :],
                                            ALU.subtract).then_inc(t_dve[c], 1)
                if n >= 0 and part == 2 and n < 6:
                    dve.wait_ge(t_pe[c], pe0 + 7 + 3 * n)
                    nc.vector.tensor_tensor(t_cols[c][:], heads4(ps[:, bank, :], P), over4(const(f"sides{n + 1}")),
                                            ALU.mult).then_inc(t_dve[c], 1)

            def scan_a(s, b):
                d, g, t, q = where(s, b)
                dve.wait_ge(c_pe[b], s * PE_C + 1)
                own.link(nc.vector.tensor_tensor(heads4(r_s[b][:], DK), heads4(ps[:, 4 + b, 0:256], DK),
                                                 spread(egc[:, t, q:q + 4], DK), ALU.mult))
                nc.vector.tensor_tensor(r_s[b][:], v_tok[:, t, g * 256:g * 256 + 256], r_s[b][:],
                                        ALU.subtract).then_inc(c_dve[b], 1)
                nc.vector.tensor_tensor(heads4(oq[b], DK), heads4(ps[:, 4 + b, 256:512], DK),
                                        spread(egc[:, t, q:q + 4], DK), ALU.mult).then_inc(c_dve[b], 1)
                if s == 0:
                    for c in range(2):
                        dve.wait_ge(t_pe[c], ROUNDS[c] * PE_T)
                nc.vector.tensor_tensor(p_one[b][:], heads4(p_all[:, t, g, :], P), over4(const(("tri_f", "tri_b")[d])),
                                        ALU.mult).then_inc(c_dve[b], 1)

            def scan_b(s, b):
                d, g, t, q = where(s, b)
                dve.wait_ge(c_pe[b], s * PE_C + 2)
                nc.vector.tensor_tensor(heads4(u_s[b][:], DK), heads4(ps[:, 4 + b, 0:256], DK),
                                        spread(beta[:, t, q:q + 4], DK), ALU.mult).then_inc(c_dve[b], 1)

            def scan_c(s, b):
                d, g, t, q = where(s, b)
                S = st[0 if s == 0 else 1]
                if s == 1:
                    dve.wait_ge(st_in, 64)
                dve.wait_ge(c_pe[b], s * PE_C + 3)
                for h in range(4):
                    cc, e = h // 2, h % 2
                    rows, cols = slice(e * DK, e * DK + DK), slice(e * DK, e * DK + DK)
                    ins = nc.vector.scalar_tensor_tensor(
                        S[rows, d, 2 * g + cc, cols], S[rows, d, 2 * g + cc, cols], gl[rows, t, q + h:q + h + 1],
                        ps[rows, 4 + b, cc * P + e * DK:cc * P + e * DK + DK], op0=ALU.mult, op1=ALU.add)
                ins.then_inc(c_dve[b], 1)
                own.link(nc.vector.tensor_tensor(oq[b], oq[b], ps[:, 4 + b, 256:512], ALU.add))
                nc.vector.tensor_tensor(o_acc[:, t, g * 256:g * 256 + 256], o_acc[:, t, g * 256:g * 256 + 256],
                                        oq[b], ALU.add).then_inc(c_dve[b], 1)

            for s in range(NT):
                for stage in (scan_a, scan_b, scan_c):
                    for b in range(4):
                        stage(s, b)
            w_low(TILE_WOUT, 0)
            for t in range(NT):
                dve.wait_ge(o_act, t + 1)
                own.link(nc.vector.tensor_reduce(o_sum[:, t, :], heads4(sq_o[t], DK), AX.X, ALU.add))
            nc.vector.tensor_scalar(o_sum[:], o_sum[:], 1.0 / DK, EPS, ALU.mult, ALU.add).then_inc(o_dve, 1)
            dve.wait_ge(o_act, NT + 1)
            own.link(nc.vector.reciprocal(o_sum[:], o_sum[:]))
            for t in range(NT):
                nc.vector.tensor_tensor(heads4(o_acc[:, t, :], DK), heads4(o_acc[:, t, :], DK),
                                        spread(o_sum[:, t, :], DK), ALU.mult).then_inc(o_normed, 1)

            def o_gate(t):
                dve.wait_ge(o_pe, t + 1)
                if t >= 2:
                    dve.wait_ge(o_lo, t - 1)
                nc.vector.scalar_tensor_tensor(heads4(scratch[t % 2][:, 0:512], P), heads4(ps[:, t % 4, :], P),
                                               cols_b[:, 60:61], z_t[:, :, t * P:(t + 1) * P],
                                               op0=ALU.mult, op1=ALU.mult).then_inc(o_scaled, 1)

            o_gate(0)
            for t in range(NT):
                if t + 1 < NT:
                    o_gate(t + 1)
                dve.wait_ge(o_hi, t + 1)
                nc.vector.tensor_tensor(h_lo[0][:, :, t * P:(t + 1) * P], heads4(scratch[t % 2][:, 0:512], P),
                                        h_hi[0][:, :, t * P:(t + 1) * P].bitcast(F32), ALU.subtract).then_inc(o_lo, 1)
            for m in range(8):
                w_low(TILE_WOUT + m + 1, (m + 1) % 2)
                dve.wait_ge(tile_done, TILE_WOUT + m + 1)
                update_x(m, 2 * (m % 2), 5)
            norm(2)
            modulate(2)
            ffn(1)
            norm(3)
            dve.wait_ge(rstd_ready, 4)
            for k in range(KD):
                nc.vector.scalar_tensor_tensor(x_t[:, k, :], x_t[:, k, :], cols_a[:, 112 + k:113 + k], rstd[:],
                                               op0=ALU.mult, op1=ALU.mult).then_inc(y_scaled, 1)

        @block.gpsimd
        def _(pool):
            own = Chain(pool, pool_own)

            def add_squares(seq):
                for k in range(KD):
                    pool.wait_ge(sq_ready, seq * 8 + k + 1)
                    if k == 0:
                        if seq >= 1:
                            pool.wait_ge(mean_mm, seq)
                        nc.gpsimd.tensor_copy(sumsq[:], square[0][:]).then_inc(sq_added, 1)
                    else:
                        pool.wait_ge(sq_added, seq * 8 + k)
                        nc.gpsimd.tensor_tensor(sumsq[:], sumsq[:], square[k % 2][:], ALU.add).then_inc(sq_added, 1)

            def scale_x(nth, seq):
                pool.wait_ge(rstd_ready, seq + 1)
                for k in range(KD):
                    if k >= 2:
                        pool.wait_ge(hf_ready, nth * 8 + k - 1)
                    nc.gpsimd.tensor_tensor(scratch[k % 2][:], x_t[:, k, :], rstd[:], ALU.mult).then_inc(hn_ready, 1)

            add_squares(0)
            scale_x(0, 0)
            add_squares(1)
            scale_x(1, 1)
            pool.wait_ge(tile_done, FFN_TILES)
            for a in (0, TC + 2, T + 4):
                nc.gpsimd.memset(pre[:, :, a:a + 2], 0.0).then_inc(pads_set, 1)
            nc.gpsimd.memset(ones_1[:], 1.0).then_inc(pads_set, 1)
            pool.wait_ge(mix_in, 16 * 11)
            pool.wait_ge(conv_silu, 12)
            for r in range(8):
                pool.wait_ge(proj_out, 17 + r)
                src = q_b[:, r % 4, TC:T] if r < 4 else k_b[:, r % 4, TC:T]
                if r >= 2:
                    pool.wait_ge(rot_done, r - 1)
                nc.gpsimd.tensor_tensor(conv_acc[r % 2][:, 0:TS], src, rope_sb[:, 0:TS], ALU.mult).then_inc(rot_cos, 1)
            pool.wait_ge(an_done, 4)
            pool.wait_ge(kv_out, 32)
            nc.gpsimd.memset(st[0][:], 0.0).then_inc(st_clear, 1)
            nc.gpsimd.memset(st[1][:], 0.0).then_inc(st_clear, 1)
            pool.wait_ge(kv_copied, 2 * NT)
            nc.gpsimd.memset(o_acc, 0.0).then_inc(st_clear, 1)
            for k, c, r, t, g in make_schedule():
                tt, dve0, pool0 = heads4(t_all[:, t, g, :], P), r * DVE_T, r * POOL_T
                if k == 2:
                    pool.wait_ge(t_act[c], r * ACT_T + 2)
                    nc.gpsimd.tensor_tensor(tt_cols[c][:], tt_cols[c][:], m_t[c][:], ALU.add).then_inc(t_pool[c], 1)
                if k == 4:
                    pool.wait_ge(t_act[c], r * ACT_T + 3)
                    pool.wait_ge(t_pool[c], pool0 + 1)
                    nc.gpsimd.tensor_tensor(tt_cols[c][:], tt_cols[c][:], x_w[c][:], ALU.mult).then_inc(t_pool[c], 1)
                if k == 6:
                    pool.wait_ge(t_dve[c], dve0 + 4)
                    nc.gpsimd.tensor_tensor(tt, m_t[c][:], over4(const("level0")), ALU.mult).then_inc(t_pool[c], 1)
                if k == 7:
                    pool.wait_ge(t_pool[c], pool0 + 3)
                    nc.gpsimd.tensor_tensor(tt, over4(const("ident")), tt, ALU.subtract).then_inc(t_pool[c], 1)
                if k >= 8 and k % 3 == 2 and k < 24:
                    n = (k - 5) // 3
                    if n == 1:
                        pool.wait_ge(t_pool[c], pool0 + 4)
                    else:
                        pool.wait_ge(t_dve[c], dve0 + 8 + 3 * (n - 2))
                    nc.gpsimd.tensor_tensor(tt_cols[c][:], tt, over4(const(f"sides{n}")), ALU.mult).then_inc(t_pool[c], 1)
            for c in range(4):
                pool.wait_ge(t_dve[c], ROUNDS[c] * DVE_T)
            for s in range(NT):
                for b in range(4):
                    d, g = b // 2, b % 2
                    t, tri = tile_of(s, d), over4(const(("tri_f", "tri_b")[d]))
                    if s >= 1:
                        pool.wait_ge(c_pe[b], s * PE_C)
                    nc.gpsimd.tensor_tensor(t_one[b][:], heads4(t_all[:, t, g, :], P), tri, ALU.mult).then_inc(c_pool[b], 1)
                    nc.gpsimd.tensor_tensor(heads4(kg[b], DK), heads4(k_tok[:, t, g * 256:g * 256 + 256], DK),
                                            spread(ekg[:, t, 8 * d + 4 * g:8 * d + 4 * g + 4], DK), ALU.mult)\
                        .then_inc(c_pool[b], 1)
            add_squares(2)
            scale_x(2, 2)
            add_squares(3)

        @block.tensor
        def _(pe):
            def product(out, k0, weights, x_parts, start, stop):
                hi, lo = weights
                xh, xl = x_parts
                nc.tensor.matmul(out, lo, xh, start=start, stop=False)
                nc.tensor.matmul(out, hi, xl, start=False, stop=False)
                return nc.tensor.matmul(out, hi, xh, start=False, stop=stop)

            def dense(s, banks, per_k=None):
                for k in range(KD):
                    if per_k is not None:
                        pe.wait_ge(h_ready, per_k + k + 1)
                    w = (w_hi[s][:, k * P:(k + 1) * P], w_lo[s][:, k * P:(k + 1) * P])
                    for half in range(2):
                        x = [h[k // 4][:, k % 4, half * HT:half * HT + HT] for h in (h_hi, h_lo)]
                        ins = product(ps[:, banks + half, 0:HT], k, w, x, k == 0, k == KD - 1)
                return ins

            def mean(seq):
                pe.wait_ge(sq_added, 8 * (seq + 1))
                for half in range(2):
                    ins = nc.tensor.matmul(ps[:, half, 0:HT], ones_d[:], sumsq[:, half * HT:half * HT + HT],
                                           start=True, stop=True)
                ins.then_inc(mean_mm, 1)

            def ada(tile, out):
                for a in range(KD):
                    ins = nc.tensor.matmul(out, tile[:, a * P:(a + 1) * P], cond[:, a, :], start=(a == 0), stop=(a == KD - 1))
                ins.then_inc(ada_used, 1)

            def ada_sum(i, bank, at, acc):
                pe.wait_ge(ada_read, i * 2 + 2)
                for u in range(2):
                    for g in range(2):
                        c = 400 + 4 * at + 2 * u + g
                        ins = nc.tensor.matmul(ps[:, bank, c:c + 1], acc[:, g * PAIR + u * P:g * PAIR + (u + 1) * P],
                                               ones_col[:], start=True, stop=True)
                ins.then_inc(ada_summed, 1)

            def ffn(f):
                base, J = TILE_FFN[f], NJ * f

                def hidden(j, par, first):
                    pe.wait_ge(w_lo_ready, j * 2 + (base + 1))
                    if not first:
                        pe.wait_ge(silu_ready, j + (J - 1))
                    dense(0, 4 * par, 16 * f if first and par == 0 else None).then_inc(tile_done, 1)
                    pe.wait_ge(w_lo_ready, j * 2 + (base + 2))
                    if not first:
                        pe.wait_ge(act_ready, j + (J - 1))
                    if f == 0 and (par == 1 or not first):
                        ada_sum(j - 1, 4 * par + 2, 0, ada_acc)
                    dense(1, 4 * par + 2).then_inc(tile_done, 1)

                def down(n, s, j, mm_wait, start, stop):
                    pe.wait_ge(w_lo_ready, n + 1)
                    for jj in range(2):
                        for mm in range(4):
                            if mm_wait is not None and jj == 0:
                                pe.wait_ge(x_updated, mm_wait + mm + 1)
                            at = jj * 512 + mm * P
                            w = (w_hi[s][:, at:at + P], w_lo[s][:, at:at + P])
                            for half in range(2):
                                x = [pick(a, j + jj, slice(half * HT, half * HT + HT)) for a in (act_hi, act_lo)]
                                ins = product(ps[:, 2 * mm + half, 0:HT], None, w, x, start and jj == 0, stop and jj == 1)
                    ins.then_inc(tile_done, 1)

                hidden(0, 0, True)
                hidden(1, 1, True)
                with pe.Fori(0, NJ // 2 - 1) as i:
                    for k in range(2):
                        hidden(i * 2 + (2 + k), k, False)
                pe.wait_ge(actlo_ready, NJ * (f + 1))
                for hf in range(2):
                    n = base + N_IN + 11 * hf
                    if f == 0 and hf == 0:
                        ada_sum(NJ - 1, 0, 0, ada_acc)
                    elif f == 0:
                        pe.wait_ge(x_updated, X_BASE[f] + 1)
                        for i in range(3):
                            ada_sum(NJ + i, 0, i, ada_accs[i])
                    down(n, n % 2, 0, X_BASE[f] if hf else None, True, False)
                    with pe.Fori(0, 4) as i:
                        for k in range(2):
                            down(i * 2 + (n + 1 + k), (n + 1 + k) % 2, i * 4 + (2 + 2 * k), None, False, False)
                    down(n + 9, (n + 9) % 2, 18, None, False, False)
                    down(n + 10, (n + 10) % 2, 20, None, False, True)
                if f == 0:
                    pe.wait_ge(x_updated, X_BASE[f] + 8)
                    for i in range(3):
                        ada_sum(NJ + 3 + i, 7, i, ada_accs[i])

            pe.wait_ge(small_in, 16 * 12)
            nc.tensor.transpose(ps[:, 0, 0:120], rows_a[:], ident[0:120, 0:120]).then_inc(cols_turned, 1)
            nc.tensor.transpose(ps[:, 1, 0:62], rows_b[:], ident[0:62, 0:62]).then_inc(cols_turned, 1)
            pe.wait_ge(x_in, 32)
            for i in range(2 * NT):
                t, q = i // 2, i % 2
                if i >= 4:
                    pe.wait_ge(x_copied, i - 3)
                for a in range(4):
                    ins = nc.tensor.transpose(ps[:, 2 + i % 4, a * P:(a + 1) * P], x_tok[:, t, (4 * q + a) * P:(4 * q + a + 1) * P],
                                              ident[:])
                ins.then_inc(x_turned, 1)
            pe.wait_ge(cond_ready, 2)
            pe.wait_ge(ones_set, 1)
            mean(0)
            for n in range(2 * KD):
                pe.wait_ge(ada_landed[n % 8], 16 * (n // 8 + 1))
                ada(ada_ring[n % 8], ps[:, 7, 2 * n:2 * n + 2])
            ffn(0)
            mean(1)
            pe.wait_ge(w_lo_ready, TILE_WIN + 1)
            dense(0, 0, 8).then_inc(tile_done, 1)
            pe.wait_ge(w_lo_ready, TILE_WIN + 2)
            dense(1, 2).then_inc(tile_done, 1)
            with pe.Fori(0, 5) as i:
                for k in range(2):
                    pe.wait_ge(w_lo_ready, i * 2 + (TILE_WIN + 3 + k))
                    pe.wait_ge(proj_out, i * 2 + (1 + k))
                    dense(k, 2 * k).then_inc(tile_done, 1)

            def values(q):
                s = q % 2
                for kk in range(2):
                    k = 2 * q + kk
                    w = [x[s][:, kk * 512:kk * 512 + 512] for x in (w_hi, w_lo)]
                    for t in range(NT):
                        hh, hl = [h[k // 4][:, k % 4, t * P:(t + 1) * P] for h in (h_hi, h_lo)]
                        out = ps[:, t, :]
                        nc.tensor.matmul(out, hl, w[0], start=(k == 0), stop=False)
                        nc.tensor.matmul(out, hh, w[1], start=False, stop=False)
                        ins = nc.tensor.matmul(out, hh, w[0], start=False, stop=(k == KD - 1))
                ins.then_inc(tile_done, 1)

            def gates():
                pe.wait_ge(gate_split, 2)
                for t in range(NT):
                    for k in range(KD):
                        hh, hl = [h[k // 4][:, k % 4, t * P:(t + 1) * P] for h in (h_hi, h_lo)]
                        gh, gw = [x[:, k * NDB:(k + 1) * NDB] for x in (gate_hi, gate_lo)]
                        out = ps[:, 6, t * NDB:(t + 1) * NDB]
                        nc.tensor.matmul(out, hl, gh, start=(k == 0), stop=False)
                        nc.tensor.matmul(out, hh, gw, start=False, stop=False)
                        ins = nc.tensor.matmul(out, hh, gh, start=False, stop=(k == KD - 1))
                ins.then_inc(gate_mm, 1)

            def decays():
                pe.wait_ge(sc_dve, 3)
                pe.wait_ge(pads_set, 4)
                for lhs, at, cols in ((const("tri_f"), 0, slice(0, 8)), (const("tri_b"), 40, slice(8, 16)),
                                      (ones_1[:], 80, slice(0, 16))):
                    n = NT * (cols.stop - cols.start)
                    ins = nc.tensor.matmul(ps[:, 6, at:at + n].rearrange("p (t n) -> p t n", t=NT), lhs, g_t[:, :, cols],
                                           start=True, stop=True)
                ins.then_inc(sc_pe, 1)

            for m in range(12, 28):
                pe.wait_ge(w_lo_ready, TILE_WIN + m + 1)
                if m < 24:
                    pe.wait_ge(proj_out, m - 1)
                    dense(m % 2, 2 * (m % 2)).then_inc(tile_done, 1)
                else:
                    if m == 24:
                        pe.wait_ge(proj_out, 24)
                        pe.wait_ge(l2_var, 8)
                    values(m - 24)
                if m == 13:
                    pe.wait_ge(mix_in, 16 * 11)
                    gates()
                if m == 16:
                    decays()
                if 15 <= m < 23:
                    i = m - 15
                    pe.wait_ge(l2_sq, i + 1)
                    if i >= 1:
                        pe.wait_ge(l2_var, i)
                    for half in range(2):
                        ins = nc.tensor.matmul(ps[:, 4 + half, 0:HT], const("headones"),
                                               square[i % 2][:, half * HT:half * HT + HT], start=True, stop=True)
                    ins.then_inc(l2_mm, 1)
                if m >= 20:
                    r = m - 20
                    src = q_b[:, r % 4, TC:T] if r < 4 else k_b[:, r % 4, TC:T]
                    pe.wait_ge(proj_out, 17 + r)
                    if r >= 1:
                        pe.wait_ge(rot_done, r)
                    nc.tensor.matmul(ps[:, 7, :], const("perm"), src, start=True, stop=True).then_inc(rot_mm, 1)
                if m in (24, 26):
                    pe.wait_ge(sc_dve, 4)
                    if m == 26:
                        pe.wait_ge(kt_copied, 1)
                    for hb in range(HB):
                        x = k_b[:, hb, 0:P] if m == 24 else ck_tok[:, hb * P:(hb + 1) * P]
                        ins = nc.tensor.transpose(ps[:, 6, hb * P:(hb + 1) * P], x, ident[:])
                    ins.then_inc(kt_turned, 1)

            def scores(v):
                hb, q0, nk = ATT_UNITS[v]
                for m in range(2):
                    if v >= 1:
                        pe.wait_ge(s_exp, 2 * v - 1 + m)
                    rows = slice(m * DK, m * DK + DK)
                    q = q_b[rows, hb, q0:q0 + P]
                    if nk == P:
                        ins = nc.tensor.matmul(ps[:, 2 * m, 0:P], q, k_b[rows, hb, 0:P], start=True, stop=True)
                    else:
                        for half in range(2):
                            ins = nc.tensor.matmul(ps[:, 2 * m + half, 0:HT], q, k_all[rows, hb, half * HT:half * HT + HT],
                                                   start=True, stop=True)
                    ins.then_inc(s_mm, 1)

            def turn(v):
                nk = ATT_UNITS[v][2]
                pe.wait_ge(s_wts, v + 1)
                if v >= 1:
                    pe.wait_ge(s_turned, v)
                for kt in range(nk // P):
                    ins = nc.tensor.transpose(ps[:, 4 + kt // 4, (kt % 4) * P:(kt % 4 + 1) * P], att_w[:, kt * P:(kt + 1) * P],
                                              ident[:])
                ins.then_inc(s_turn, 1)

            def weigh(v):
                hb, q0, nk = ATT_UNITS[v]
                pe.wait_ge(s_turned, v + 1)
                if v >= 1:
                    pe.wait_ge(s_out, v)
                for kt in range(nk // P):
                    vals = cv_tok[:, hb * P:(hb + 1) * P] if nk > P and kt == 0 else v_b[:, kt, hb * P:(hb + 1) * P]
                    ins = nc.tensor.matmul(ps[:, 6, 0:P], vals, att_wt[:, kt * P:(kt + 1) * P],
                                           start=(kt == 0), stop=(kt == nk // P - 1))
                ins.then_inc(s_pv, 1)

            pe.wait_ge(kt_copied, 2)
            pe.wait_ge(rot_done, 8)
            pe.wait_ge(vb_ready, 1)
            scores(0)
            for v in range(NU):
                if v + 1 < NU:
                    scores(v + 1)
                turn(v)
                if v >= 1:
                    weigh(v - 1)
            weigh(NU - 1)
            for hb in range(HB):
                pe.wait_ge(an_sq, hb + 1)
                if hb >= 1:
                    pe.wait_ge(an_var, hb)
                for half in range(2):
                    ins = nc.tensor.matmul(ps[:, half, 0:HT], ones_d[:], square[0][:, half * HT:half * HT + HT],
                                           start=True, stop=True)
                ins.then_inc(an_mm, 1)

            pe.wait_ge(l2_done, 8)
            for i in range(2 * NT):
                if i >= 4:
                    pe.wait_ge(kv_copied, i - 3)
                for a in range(4):
                    ins = nc.tensor.transpose(ps[:, 4 + i % 4, a * P:(a + 1) * P],
                                              pre[:, 4 + 4 * (i % 2) + a, (i // 2) * P:(i // 2 + 1) * P], ident[:])
                ins.then_inc(kv_turned, 1)
            pe.wait_ge(an_done, 4)

            def qk(t, g, h, which):
                rows = slice((h % 2) * DK, (h % 2) * DK + DK)
                return pre[rows, which + 2 * g + h // 2, t * P:(t + 1) * P]

            def products(t, g, c, bank, which, e):
                for h in (e, e + 2):
                    ins = nc.tensor.matmul(ps[:, bank, h * P:(h + 1) * P], qk(t, g, h, 4), qk(t, g, h, which),
                                           start=True, stop=True)
                ins.then_inc(t_pe[c], 1)

            def four(c, op):
                for h in range(4):
                    ins = op(ps[:, 2 * c, h * P:(h + 1) * P], h)
                ins.then_inc(t_pe[c], 1)

            for k, c, r, t, g in make_schedule():
                dve0, pool0, bank = r * DVE_T, r * POOL_T, 2 * c
                if k == 0:
                    if r >= 1:
                        pe.wait_ge(t_dve[c], dve0)
                    elif c >= 2:
                        pe.wait_ge(kv_copied, 2 * NT)
                    for d in range(2):
                        for h in range(4):
                            col = g_t[:, t, 8 * d + 4 * g + h:8 * d + 4 * g + h + 1]
                            ins = nc.tensor.matmul(ps[:, bank + d, h * P:(h + 1) * P], col.broadcast_to([P, P]),
                                                   const(("tri_f", "tri_b")[d]), start=True, stop=True)
                        ins.then_inc(t_pe[c], 1)
                if k == 2:
                    pe.wait_ge(t_dve[c], dve0 + 1)
                    products(t, g, c, bank, 4, 0)
                if k == 3:
                    pe.wait_ge(t_pe[c], r * PE_T + 3)
                    products(t, g, c, bank, 4, 1)
                    pe.wait_ge(t_dve[c], dve0 + 2)
                    products(t, g, c, bank + 1, 0, 0)
                if k == 4:
                    pe.wait_ge(t_pe[c], r * PE_T + 5)
                    products(t, g, c, bank + 1, 0, 1)
                if k == 8:
                    pe.wait_ge(t_pool[c], pool0 + 4)
                    four(c, lambda out, h: nc.tensor.transpose(out, t_all[:, t, g, h * P:(h + 1) * P], ident[:]))
                n, part = divmod(k - 6, 3)
                if n >= 1 and part == 0:
                    pe.wait_ge(t_dve[c], dve0 + 6 + 3 * (n - 1))
                    four(c, lambda out, h: nc.tensor.matmul(out, m_t[c][:, h, :], t_cols[c][:, h, :], start=True, stop=True))
                if n >= 1 and part == 1:
                    pe.wait_ge(t_dve[c], dve0 + 7 + 3 * (n - 1))
                    pe.wait_ge(t_pool[c], pool0 + 4 + n)
                    four(c, lambda out, h: nc.tensor.matmul(out, x_w[c][:, h, :], tt_cols[c][:, h, :], start=True, stop=True))
                if n >= 1 and part == 2:
                    pe.wait_ge(t_dve[c], dve0 + 8 + 3 * (n - 1))
                    four(c, lambda out, h: nc.tensor.transpose(out, t_all[:, t, g, h * P:(h + 1) * P], ident[:]))

            def scan_a(s, b):
                d, g = b // 2, b % 2
                t, S = tile_of(s, d), st[0 if s == 0 else 1]
                if s == 0:
                    pe.wait_ge(st_clear, 3)
                    for c in (2, 3):
                        pe.wait_ge(t_dve[c], ROUNDS[c] * DVE_T)
                else:
                    pe.wait_ge(c_dve[b], s * DVE_C)
                if s == 1:
                    pe.wait_ge(st_in, 64)
                for which, at in ((4, 0), (0, 256)):
                    for cc in range(2):
                        ins = nc.tensor.matmul(ps[:, 4 + b, at + cc * P:at + cc * P + P],
                                               pre[:, which + 2 * g + cc, t * P:(t + 1) * P], S[:, d, 2 * g + cc, :],
                                               start=True, stop=True)
                ins.then_inc(c_pe[b], 1)

            def scan_b(s, b):
                pe.wait_ge(c_dve[b], s * DVE_C + 2)
                pe.wait_ge(c_pool[b], s * POOL_C + 1)
                for h in range(4):
                    ins = nc.tensor.matmul(ps[:, 4 + b, h * DK:(h + 1) * DK], t_one[b][:, h, :],
                                           r_s[b][:, h * DK:(h + 1) * DK], start=True, stop=True)
                ins.then_inc(c_pe[b], 1)

            def scan_c(s, b):
                pe.wait_ge(c_dve[b], s * DVE_C + 4)
                pe.wait_ge(c_pool[b], s * POOL_C + 2)
                for cc in range(2):
                    nc.tensor.matmul(ps[:, 4 + b, cc * P:(cc + 1) * P], kg[b][:, cc * P:(cc + 1) * P],
                                     u_s[b][:, cc * P:(cc + 1) * P], start=True, stop=True)
                for h in range(4):
                    ins = nc.tensor.matmul(ps[:, 4 + b, 256 + h * DK:256 + (h + 1) * DK], p_one[b][:, h, :],
                                           u_s[b][:, h * DK:(h + 1) * DK], start=True, stop=True)
                ins.then_inc(c_pe[b], 1)

            for s in range(NT):
                for stage in (scan_a, scan_b, scan_c):
                    for b in range(4):
                        stage(s, b)
            for t in range(NT):
                pe.wait_ge(o_normed, t + 1)
                if t >= 4:
                    pe.wait_ge(o_scaled, t - 3)
                for a in range(4):
                    ins = nc.tensor.transpose(ps[:, t % 4, a * P:(a + 1) * P], o_acc[:, t, a * P:(a + 1) * P], ident[:])
                ins.then_inc(o_pe, 1)
            pe.wait_ge(o_lo, NT)
            for m in range(2):
                pe.wait_ge(w_lo_ready, TILE_WOUT + m + 1)
                dense(m, 2 * m).then_inc(tile_done, 1)
            with pe.Fori(0, 3) as i:
                for k in range(2):
                    pe.wait_ge(w_lo_ready, i * 2 + (TILE_WOUT + 3 + k))
                    pe.wait_ge(x_updated, i * 2 + (8 + 1 + k))
                    dense(k, 2 * k).then_inc(tile_done, 1)
            mean(2)
            ffn(1)
            mean(3)
            for i in range(2 * NT):
                t, q = i // 2, i % 2
                if i == 0:
                    pe.wait_ge(var_ready, 4)
                    pe.wait_ge(y_scaled, KD)
                if i >= 4:
                    pe.wait_ge(y_copied, i - 3)
                for a in range(4):
                    ins = nc.tensor.transpose(ps[:, i % 4, a * P:(a + 1) * P], x_t[:, 4 * q + a, t * P:(t + 1) * P], ident[:])
                ins.then_inc(y_turned, 1)


_INS = ['x_prompt', 'x_sample', 'cache_diff_k', 'cache_diff_v', 'state_delta', 'c', 'c_ctx', 'w_ada', 'b_ada',
        'norm_ffn1', 'w_ffn1_in', 'w_ffn1_out', 'norm_mix', 'w_in', 'conv_w', 'a_log', 'dt_bias', 'delta_norm',
        'lambda_q1', 'lambda_k1', 'lambda_q2', 'lambda_k2', 'diff_norm', 'w_out', 'norm_ffn2', 'w_ffn2_in',
        'w_ffn2_out', 'norm_final']
_OUTS = [(1, TC, D), (1, TS, D), (TC, HB * P), (TC, HB * P), (2, HA, DK, DK)]


def kernel(**inputs):
    import concourse.bacc as bacc
    from concourse.bass_utils import run_bass_kernel_spmd

    nc = bacc.Bacc("TRN2", target_bir_lowering=False, num_devices=1, dynamic_dma_scratch_size=1024)
    arrays, args = {}, []
    tables = dict(zip(("consts", "rope"), shape_constants()))
    for name in _INS + ["consts", "rope"]:
        a = np.ascontiguousarray(tables[name] if name in tables else inputs[name])
        arrays[f"in_{name}"] = a
        args.append(nc.dram_tensor(f"in_{name}", a.shape, F32, kind="ExternalInput").ap())
    for i, shape in enumerate(_OUTS):
        args.append(nc.dram_tensor(f"out_{i}", shape, F32, kind="ExternalOutput").ap())
    hybrid_step(nc, *args)
    r = run_bass_kernel_spmd(nc, [arrays], core_ids=[0])
    y_p, y_s, nk, nv, ns = (r.results[0][f"out_{i}"] for i in range(len(_OUTS)))
    return (y_p, y_s, nk.reshape(1, 1, TC, HB, 2, DK), nv.reshape(1, 1, TC, HB, P),
            ns.reshape(1, 1, 2, HA, DK, DK))
```

```python
import math
from contextlib import ExitStack

import numpy as np
import concourse.bass as bass
from concourse import mybir

F32 = mybir.dt.float32
F32R = mybir.dt.float32r
ALU = mybir.AluOpType
ACT = mybir.ActivationFunctionType
AX = mybir.AxisListType

P = 128
D = 1024
KD = D // P
TC, TS = 128, 512
T = TC + TS
NT = T // P
HT = T // 2
DFF = 2816
NJ = DFF // P
HA, DK = 8, 64
HB = 4
NMOD = 9
CONV = 5
EPS = 1e-6
LAM_INIT = 0.8 - 0.6 * math.exp(-0.3 * 0)
LEVELS = [1, 2, 4, 8, 16, 32, 64]
COL_DEC = 2048
NDB = 4 * HA
COL_B = COL_DEC + NDB
SEGS = [(0, 0, 0, 0, TC), (1, 0, TC, TC, HT - TC), (1, 1, 0, HT, HT)]
ATT_UNITS = [(hb, 0, TC) for hb in range(HB)] + [(hb, q, P + TS) for hb in range(HB) for q in range(TC, T, P)]
NU = len(ATT_UNITS)
NORM_END = NU + 6
PE_T, DVE_T, ACT_T, POOL_T = 24, 23, 3, 10
MAKE_ORDER = [0, 1, 4, 2, 3]
OUT_ORDER = [0, 2, 3, 1, 4]
OUT_EARLY = 3
MAKE_STAGES, MAKE_LAG = 26, 7
ROUNDS = [(2 * NT + 3 - c) // 4 for c in range(4)]
PE_C, DVE_C, POOL_C = 3, [6, 6, 5, 5], [2, 2, 3, 3]
ADA_PE, ADA_DVE = 10, 3
ADA_MARKS = 14


def tile_of(step, d):
    return step if d == 0 else (0 if step == 0 else NT - step)


def norm_at(v):
    return divmod(v - 6, 4) if v >= 6 else (None, None)


def heads4_of(x, j):
    return x[:, :, 0:TC] if j == 0 else heads4(x[:, j - 1, TC:T], P)


def pick(x, j, *rest):
    if isinstance(j, int):
        return x[(slice(None), j) + rest]
    return x[(slice(None), bass.ds(j, 1)) + (rest or (slice(None),))].rearrange("p a b -> p (a b)")


def halves(x):
    return x.rearrange("p (a b) -> p a b", a=2)


def heads4(x, n):
    return x.rearrange("p (h n) -> p h n", n=n)


def spread(x, n):
    return x[:, :, None].broadcast_to([x.shape[0], x.shape[1], n])


N_IN, N_OUT = 2 * NJ, NJ
FFN_TILES = N_IN + N_OUT
TILE_FFN = [0, FFN_TILES + 28 + 8]
TILE_WIN = FFN_TILES
TILE_WBV = TILE_WIN + 24
TILE_WOUT = TILE_WIN + 28
PAIR = 2 * P
N_TILES = TILE_FFN[1] + FFN_TILES

CONST_NAMES = (["ident", "perm", "headones", "tri_f", "tri_b", "after", "before"] +
               [f"level{n}" for n in range(7)] + [f"sides{n}" for n in range(1, 7)])


def shape_constants():
    i = np.arange(P)
    ident = np.eye(P)
    perm = np.zeros((P, P))
    perm[i ^ 16, i] = 1.0
    headones = (i[:, None] // DK == i[None, :] // DK) * 1.0
    tri_f = (i[:, None] <= i[None, :]) * 1.0
    tri_b = (i[:, None] >= i[None, :]) * 1.0
    after, before = (i[:, None] < i[None, :]) * 1.0, (i[:, None] > i[None, :]) * 1.0
    level, sides = [], []
    for b in LEVELS:
        half = (i // b) % 2
        level.append(((i[:, None] // (2 * b) == i[None, :] // (2 * b)) & (half[:, None] != half[None, :])) * 1.0)
        sides.append(np.where(half[None, :] == 0, i[:, None] >= i[None, :], i[:, None] <= i[None, :]) * 1.0)
    n = np.arange(TS)
    d = i % DK
    pos = np.where((d // 32)[:, None] == 0, (n // 64)[None, :], (n % 64)[None, :]).astype(np.float32)
    inv = (np.float32(10000.0) ** (-(d % 16).astype(np.float32) / np.float32(16))).astype(np.float32)
    ang = (pos * inv[:, None]).astype(np.float32)
    sign = np.where(d % 32 < 16, -1.0, 1.0)[:, None]
    small = np.concatenate([ident, perm, headones, tri_f, tri_b, after, before] + level + sides[1:], 1).astype(np.float32)
    rope = np.concatenate([np.cos(ang), np.sin(ang) * sign], 1).astype(np.float32)
    return small, rope


N_SMALL = len(CONST_NAMES) * P


class Chain:

    def __init__(self, eng, sem):
        self.eng, self.sem, self.n, self.reg, self.m = eng, sem, 0, None, 0

    def link(self, ins):
        ins.then_inc(self.sem, 1)
        self.m += 1
        self.wait_back(0)

    def mark(self, ins):
        ins.then_inc(self.sem, 1)
        self.m += 1

    def wait_back(self, k):
        at = self.n + self.m - k
        self.eng.wait_ge(self.sem, at if self.reg is None else self.reg + at)

    def loop(self, i, per):
        self.n, self.m = self.n + self.m, 0
        self.reg, self.per = i * per, per

    def done(self, iters):
        assert self.m == self.per, (self.m, self.per)
        self.n, self.m, self.reg = self.n + iters * self.per, 0, None


def hybrid_step(nc, x_prompt, x_sample, cache_diff_k, cache_diff_v, state_delta, c, c_ctx, w_ada, b_ada,
                norm_ffn1, w_ffn1_in, w_ffn1_out, norm_mix, w_in, conv_w, a_log, dt_bias, delta_norm,
                lambda_q1, lambda_k1, lambda_q2, lambda_k2, diff_norm, w_out, norm_ffn2, w_ffn2_in,
                w_ffn2_out, norm_final, consts, rope, y_prompt, y_sample, new_k, new_v, new_state):
    ctx = ExitStack()
    with ctx:
        def sem(name):
            return ctx.enter_context(nc.semaphore(name))

        def holder(stack):
            return lambda name, shape, dt=F32: stack.enter_context(nc.sbuf_tensor(name, shape, dt))

        sb = holder(ctx)
        x_t = sb("x_t", [P, KD, T])
        w_raw = [sb(f"w_raw{i}", [P, D]) for i in range(2)]
        with ExitStack() as s:
            spare = [[holder(s)(f"spare{i}{c}", [P, 4, P]) for c in range(2)] for i in range(4)]
        w_hi = [sb(f"w_hi{i}", [P, D], F32R) for i in range(2)]
        w_lo = [sb(f"w_lo{i}", [P, D], F32R) for i in range(2)]
        with ExitStack() as s:
            h_hi, h_lo = [[holder(s)(f"h_{n}0", [P, 4, T], F32R)] for n in ("hi", "lo")]
        p_all = sb("p_all", [P, NT, 2, 4 * P])
        for h, n in ((h_hi, "hi"), (h_lo, "lo")):
            h.append(sb(f"h_{n}1", [P, 4, T], F32R))
        ones_col = sb("ones_col", [P, 1])
        cond = sb("cond", [P, KD, 2])
        ident = sb("ident", [P, P])
        ones_d = sb("ones_d", [P, P])
        cols_a = sb("cols_a", [P, 120])
        cols_b = sb("cols_b", [P, 62])
        mods = sb("mods", [P, NMOD * KD, 2])
        scales = sb("scales", [P, 3, KD, 2])
        root_dummy = sb("root_dummy", [P, 1])
        tok_rs = sb("tok_rs", [P, 8])
        rstd = sb("rstd", [P, T])
        sumsq = sb("sumsq", [P, T])
        square = [sb(f"square{i}", [P, T]) for i in range(2)]
        scratch = [sb(f"scratch{i}", [P, T]) for i in range(2)]
        silu_g, act_f = square, scratch

        with ExitStack() as s:
            tb = holder(s)
            x_tok = tb("x_tok", [P, NT, D])
            ada_tiles = [tb(f"ada_tile{i}", [P, D]) for i in range(ADA_PE)]
            ada_row = tb("ada_row", [2, ADA_PE * P])
            ada_wide = [tb(f"ada_wide{i}", [P, 2 * D]) for i in range(ADA_DVE)]
            ada_wide_acc = [tb(f"ada_wide_acc{i}", [P, 2 * PAIR]) for i in range(ADA_DVE)]
            rows_a = tb("rows_a", [120, P])
            rows_b = tb("rows_b", [62, P])
        with ExitStack() as s:
            tb = holder(s)
            act_hi = tb("act_hi", [P, NJ, T], F32R)
            act_lo = tb("act_lo", [P, NJ, T], F32R)
            ada_ffn = [tb(f"ada_ffn{i}", [P, D]) for i in range(2)]
            ada_acc = tb("ada_acc", [P, 2 * PAIR])
            ada_accs = [ada_acc] + scratch
        with ExitStack() as s:
            y_tok = holder(s)("y_tok", [P, NT, D])
        mb = holder(ctx.enter_context(ExitStack()))
        cst = mb("cst", [P, N_SMALL])
        pre = mb("pre", [P, 12, T + 6])
        z_t = mb("z_t", [P, HB, T])
        vecs = mb("vecs", [P, 3, 16])
        g_t, beta, gc, egc, ekg, gl, sp_a, sp_b = [
            mb(n, [P, NT, 16]) for n in ("g_t", "beta", "gc", "egc", "ekg", "gl", "sp_a", "sp_b")]
        dn_col = mb("dn_col", [P, 1])
        with ExitStack() as s:
            tb = holder(s)
            rope_sb = tb("rope_sb", [P, 2 * TS])
            ones_1 = tb("ones_1", [P, P])
            exps = [tb(f"exps{i}", [P, T]) for i in range(2)]
            with ExitStack() as s2:
                gate_w = holder(s2)("gate_w", [P, KD * NDB])
                gate_hi = holder(s2)("gate_hi", [P, KD * NDB], F32R)
            nk_tok = tb("nk_tok", [P, HB * P])
            gate_lo = tb("gate_lo", [P, KD * NDB], F32R)
            conv_acc = [tb(f"conv_acc{i}", [P, T + 2]) for i in range(2)]
            q_b = tb("q_b", [P, HB, T])
            k_b = tb("k_b", [P, HB, T])
            k_all = tb("k_all", [P, HB, T])
            v_b = tb("v_b", [P, NT, HB * P])
            ck_tok = tb("ck_tok", [P, HB * P])
            cv_tok = tb("cv_tok", [P, HB * P])
            lam_in = tb("lam_in", [P, 4, DK])
            lam_t = tb("lam_t", [P, 8])
            att_s = tb("att_s", [P, 2, 8])
            att_v = tb("att_v", [P, T])
            att_wt = tb("att_wt", [P, T])
            att_p = [conv_acc, exps]
            rot_sin = [att_v, att_wt]
            gate_fm = att_v[0:NDB, :]
            att_w = [sumsq, scratch[1]]
            att_q = q_b
        with ExitStack() as s:
            tb = holder(s)
            k_tok = tb("k_tok", [P, NT, HA * DK])
            v_tok = tb("v_tok", [P, NT, HA * DK])
            o_acc = pre[:, 8:12, :].rearrange("p a b -> p (a b)")[:, 0:NT * HA * DK].rearrange("p (t n) -> p t n", t=NT)
            st = [tb(f"st{i}", [P, 2, 4, P]) for i in range(2)]
            t_all = tb("t_all", [P, NT, 2, 4 * P])
            make = [[tb(f"{n}{c}", [P, 4, P]) for c in range(2)] for n in ("m_t", "x_w", "t_cols", "tt_cols")]
            t_one, p_one = make[0] + make[1], make[2] + make[3]
            for x, more in zip(make, spare):
                x += more
            m_t, x_w, t_cols, tt_cols = make
            r_s = [tb(f"r_s{i}", [P, 256]) for i in range(4)]
            u_s = r_s
            kg = [square[i // 2][:, (i % 2) * 256:(i % 2) * 256 + 256] for i in range(4)]
            oq = [x[:, i * 256:i * 256 + 256] for x in (rstd, sumsq) for i in range(2)]
            sq_o = [t_all[:, t, 0, :] for t in range(NT)]
            o_sum = tb("o_sum", [P, NT, HA])
        ps = ctx.enter_context(nc.psum_tensor("ps", [P, 8, 512], F32))

        def const(name):
            i = CONST_NAMES.index(name)
            return cst[:, i * P:(i + 1) * P]

        def over4(x):
            return x[:, None, :].broadcast_to([P, 4, P])

        def make_schedule():
            for at in range((2 * NT - 1) * MAKE_LAG + MAKE_STAGES):
                for u in range(2 * NT):
                    k = at - u * MAKE_LAG
                    if 0 <= k < MAKE_STAGES:
                        yield k, u % 4, u // 4, MAKE_ORDER[u // 2], u % 2

        w_landed = [sem(f"w_landed{i}") for i in range(2)]
        w_hi_ready, w_lo_ready, tile_done = sem("w_hi_ready"), sem("w_lo_ready"), sem("tile_done")
        small_in, x_in = sem("small_in"), sem("x_in")
        ada_landed = [sem(f"ada_landed{i}") for i in range(ADA_PE)]
        ada_wide_in = [sem(f"ada_wide_in{i}") for i in range(ADA_DVE)]
        ada_wide_read, ada_rows, ada_turned = sem("ada_wide_read"), sem("ada_rows"), sem("ada_turned")
        ada_in = [sem(f"ada_in{i}") for i in range(2)]
        ada_read, ada_summed, mods_ready = sem("ada_read"), sem("ada_summed"), sem("mods_ready")
        ada_used, ones_set = sem("ada_used"), sem("ones_set")
        cols_turned, cols_ready, cond_ready = sem("cols_turned"), sem("cols_ready"), sem("cond_ready")
        x_turned, x_copied = sem("x_turned"), sem("x_copied")
        dve_own, act_own, pool_own = sem("dve_own"), sem("act_own"), sem("pool_own")
        sq_ready, sq_added, x_updated = sem("sq_ready"), sem("sq_added"), sem("x_updated")
        down_done = sem("down_done")
        mean_mm, var_ready, sd_ready = sem("mean_mm"), sem("var_ready"), sem("sd_ready")
        tokrs_ready, spread_mm = sem("tokrs_ready"), sem("spread_mm")
        scales_ready, rstd_ready, hn_ready, hf_ready, h_ready = sem("scales_ready"), sem("rstd_ready"), sem("hn_ready"), sem("hf_ready"), sem("h_ready")
        silu_ready, act_ready, acthi_ready, actlo_ready = (sem("silu_ready"), sem("act_ready"),
                                                           sem("acthi_ready"), sem("actlo_ready"))
        mix_in, proj_out, conv_ready, conv_silu = sem("mix_in"), sem("proj_out"), sem("conv_ready"), sem("conv_silu")
        pads_set, gate_split, gate_mm, vb_ready = sem("pads_set"), sem("gate_split"), sem("gate_mm"), sem("vb_ready")
        sc_pe, sc_act, sc_dve = sem("scalars_pe"), sem("scalars_act"), sem("scalars_dve")
        l2_sq, l2_mm, l2_var, l2_sd, l2_done = [sem("l2_" + n) for n in ("sq", "mm", "var", "sd", "done")]
        rot_mm, rot_cos, rot_done = sem("rot_mm"), sem("rot_cos"), sem("rot_done")
        gate_copied = sem("gate_copied")
        kt_turned, kt_copied = sem("kt_turned"), sem("kt_copied")
        s_mm, s_max, s_exp, s_wts, s_turn, s_turned, s_pv, s_out = [
            sem("att_" + n) for n in ("scores", "max", "exp", "weights", "turn", "turned", "pv", "out")]
        an_sq, an_mm, an_var, an_sd, an_rs, an_spread, an_tmp, an_hi, an_done = [
            sem("att_norm_" + n) for n in ("sq", "mm", "var", "sd", "rs", "spread", "tmp", "hi", "done")]
        kv_out, st_out, st_in, st_clear, y_out = sem("kv_out"), sem("st_out"), sem("st_in"), sem("st_clear"), sem("y_out")
        kv_turned, kv_copied = sem("kv_turned"), sem("kv_copied")
        t_pe, t_dve, t_act, t_pool = [[sem(f"make_t_{n}{c}") for c in range(4)] for n in ("pe", "dve", "act", "pool")]
        c_pe, c_dve, c_pool, c_act, o_added = [[sem(f"scan_{n}{b}") for b in range(4)]
                                               for n in ("pe", "dve", "pool", "act", "out")]
        o_pe, o_dve, o_act = sem("delta_out_pe"), sem("delta_out_dve"), sem("delta_out_act")
        o_sd = sem("delta_out_sd")
        o_normed, o_scaled, o_hi, o_lo = [sem("delta_out_" + n) for n in ("normed", "scaled", "hi", "lo")]
        y_scaled, y_turned = sem("y_scaled"), sem("y_turned")
        y_copied = [sem("y_copied_act"), sem("y_copied_dve")]

        block = ctx.enter_context(nc.Block())
        X_BASE = [0, 16]
        SEQ = [1, 3]
        ffn_w = [(w_ffn1_in, w_ffn1_out), (w_ffn2_in, w_ffn2_out)]
        win = w_in[0].rearrange("(k p) n -> p k n", p=P)

        def ada_load(eng, i, q, first=False):
            if not first:
                eng.wait_ge(ada_read, i * 2 + (q - 1))
            cols = slice(i * PAIR + 2 * KD * P, (i + 1) * PAIR + 2 * KD * P) if isinstance(i, int) else \
                bass.ds(i * PAIR + 2 * KD * P, PAIR)
            src = w_ada[0].rearrange("(k p) n -> p k n", p=P)[:, 4 * q:4 * q + 4, cols]
            eng.dma_start(ada_ffn[q][:].rearrange("p (k n) -> p k n", k=4), src).then_inc(ada_in[q], 16)

        @block.sync
        def _(sp):
            rows = [(0, b_ada[0].rearrange("(m p) -> m p", p=P)), (72, c.rearrange("a (m p) -> (a m) p", p=P)),
                    (80, c_ctx.rearrange("(m p) -> m p", p=P)), (88, norm_ffn1[0].rearrange("(m p) -> m p", p=P)),
                    (96, norm_mix[0].rearrange("(m p) -> m p", p=P)),
                    (104, norm_ffn2[0].rearrange("(m p) -> m p", p=P)),
                    (112, norm_final.rearrange("(m p) -> m p", p=P))]
            sp.dma_start(ident[:], consts[:, 0:P]).then_inc(small_in, 16)
            for at, src in rows:
                sp.dma_start(rows_a[at:at + src.shape[0], :], src).then_inc(small_in, 16)
            sp.dma_start(rows_b[0:60, :], conv_w[0].rearrange("t (m p) -> (t m) p", p=P)).then_inc(small_in, 16)
            for k in range(2):
                sp.dma_start(rows_b[60:61, k * DK:(k + 1) * DK], delta_norm).then_inc(small_in, 16)
            sp.dma_start(rows_b[61:62, :], diff_norm).then_inc(small_in, 16)
            sp.dma_start(x_tok[:, 0, :], x_prompt[0]).then_inc(x_in, 16)
            sp.dma_start(x_tok[:, 1:NT, :], x_sample[0].rearrange("(t p) d -> p t d", p=P)).then_inc(x_in, 16)
            ada_v = w_ada[0].rearrange("(k p) n -> p k n", p=P)

            for n in range(ADA_PE):
                if n % 3 == 0 and n // 3 < ADA_DVE:
                    col = ADA_PE * P + n // 3 * PAIR
                    sp.dma_start(ada_wide[n // 3][:].rearrange("p (k n) -> p k n", k=KD),
                                 ada_v[:, :, col:col + PAIR]).then_inc(ada_wide_in[n // 3], 16)
                sp.dma_start(ada_tiles[n][:].rearrange("p (k n) -> p k n", k=KD),
                             ada_v[:, :, n * P:(n + 1) * P]).then_inc(ada_landed[n], 16)

            def w_load(n, s, src, first=False):
                if not first:
                    sp.wait_ge(w_lo_ready, n - 1)
                sp.dma_start(w_raw[s][:].rearrange("p (a b) -> p a b", a=src.shape[1]), src)\
                    .then_inc(w_landed[s], 16)

            def ffn_loads(f):
                base = TILE_FFN[f]
                wi = ffn_w[f][0][0].rearrange("(k p) n -> p k n", p=P)
                wo = ffn_w[f][1][0].rearrange("(j p) n -> p j n", p=P)
                for k in range(2):
                    w_load(base + k, k, wi[:, :, k * DFF:k * DFF + P], first=(f == 0))
                if f == 0:
                    sp.wait_ge(x_copied, 2 * NT)
                    sp.wait_ge(ada_turned, 1)
                    sp.wait_ge(ada_summed, ADA_DVE)
                    for k in range(2):
                        ada_load(sp, 0, k, first=True)
                with sp.Fori(0, NJ - 1) as j:
                    for k in range(2):
                        w_load(j * 2 + (base + 2 + k), k, wi[:, :, bass.ds(j * P + (k * DFF + P), P)])
                for hf in range(2):
                    n = base + N_IN + 11 * hf
                    cols = slice(hf * 512, hf * 512 + 512)
                    w_load(n, n % 2, wo[:, 0:2, cols])
                    if f == 0:
                        for i in range(1, 11):
                            w_load(n + i, (n + i) % 2, wo[:, 2 * i:2 * i + 2, cols])
                            if i <= 6 and (hf, i) != (0, 1):
                                ada_load(sp, NJ + 3 * hf + (i - 1) // 2, (i - 1) % 2)
                        continue
                    with sp.Fori(0, 5) as i:
                        for k in range(2):
                            w_load(i * 2 + (n + 1 + k), (n + 1 + k) % 2, wo[:, bass.ds(i * 4 + (2 + 2 * k), 2), cols])

            ffn_loads(0)
            for k in range(2):
                w_load(TILE_WIN + k, k, win[:, :, k * P:(k + 1) * P])
            sp.wait_ge(tile_done, FFN_TILES)
            sp.dma_start(cst[:], consts).then_inc(mix_in, 16)
            sp.dma_start(rope_sb[:], rope).then_inc(mix_in, 16)
            sp.dma_start(gate_w[:].rearrange("p (k n) -> p k n", k=KD), win[:, :, COL_DEC:COL_DEC + NDB]).then_inc(mix_in, 16)
            sp.dma_start(vecs[:, 0, :], a_log.rearrange("a d h -> a (d h)").broadcast_to([P, 16])).then_inc(mix_in, 16)
            sp.dma_start(vecs[:, 1, :], dt_bias.rearrange("a d h -> a (d h)").broadcast_to([P, 16])).then_inc(mix_in, 16)
            for i, v in enumerate((lambda_q1, lambda_k1, lambda_q2, lambda_k2)):
                sp.dma_start(lam_in[:, i, :], v.broadcast_to([P, DK])).then_inc(mix_in, 16)
            sp.dma_start(ck_tok[:], cache_diff_k[0, 0].rearrange("t h m d -> t (h m d)")).then_inc(mix_in, 16)
            sp.dma_start(cv_tok[:], cache_diff_v[0, 0].rearrange("t h e -> t (h e)")).then_inc(mix_in, 16)
            for i0, iters, col in ((2, 7, 2 * P), (16, 4, COL_B)):
                with sp.Fori(0, iters) as i:
                    for k in range(2):
                        w_load(i * 2 + (TILE_WIN + i0 + k), k, win[:, :, bass.ds(i * (2 * P) + (col + k * P), P)])
            for q in range(4):
                w_load(TILE_WBV + q, q % 2, win[:, 2 * q:2 * q + 2, COL_B + 1024:COL_B + 1536])
            wo = w_out[0].rearrange("(k p) n -> p k n", p=P)
            for m in range(2):
                w_load(TILE_WOUT + m, m % 2, wo[:, :, m * P:(m + 1) * P])
            sp.wait_ge(vb_ready, 1)
            sp.dma_start(new_v, v_b[:, 0, :]).then_inc(kv_out, 16)
            sp.wait_ge(kt_copied, 1)
            sp.dma_start(new_k, nk_tok[:]).then_inc(kv_out, 16)
            sp.wait_ge(st_clear, 3)
            for d in range(2):
                for e in range(2):
                    sp.dma_start(st[1][e * DK:(e + 1) * DK, d, :, e * DK:(e + 1) * DK],
                                 state_delta[0, 0, d].rearrange("(c e) k v -> e k c v", e=2)[e]).then_inc(st_in, 16)
            for b in range(4):
                sp.wait_ge(c_dve[b], DVE_C[b])
            for d in range(2):
                for e in range(2):
                    sp.dma_start(new_state[d].rearrange("(c e) k v -> e k c v", e=2)[e],
                                 st[0][e * DK:(e + 1) * DK, d, :, e * DK:(e + 1) * DK]).then_inc(st_out, 16)
            with sp.Fori(0, 3) as i:
                for k in range(2):
                    w_load(i * 2 + (TILE_WOUT + 2 + k), k, wo[:, :, bass.ds(i * (2 * P) + (2 + k) * P, P)])
            ffn_loads(1)
            for t in range(NT):
                for i in (t, t + NT):
                    sp.wait_ge(y_copied[i % 2], i // 2 + 1)
                dst = y_prompt[0] if t == 0 else y_sample[0, (t - 1) * P:t * P, :]
                sp.dma_start(dst, y_tok[:, t, :]).then_inc(y_out, 16)
            sp.wait_ge(y_out, 16 * NT)
            sp.wait_ge(kv_out, 32)
            sp.wait_ge(st_out, 64)

        @block.scalar
        def _(act):
            own = Chain(act, act_own)

            def w_high(n, s, first=False):
                act.wait_ge(w_landed[s], n * 8 + (16 - 8 * s))
                if not first:
                    act.wait_ge(tile_done, n - 1)
                nc.scalar.copy(w_hi[s][:], w_raw[s][:]).then_inc(w_hi_ready, 1)

            def square_of(k, seq, after):
                if after is not None:
                    act.wait_ge(x_updated, after + k + 1)
                if seq * 8 + k >= 2:
                    act.wait_ge(sq_added, seq * 8 + k - 1)
                nc.scalar.activation(square[k % 2][:], x_t[:, k, :], ACT.Square).then_inc(sq_ready, 1)

            def norm(seq, spread=True):
                act.wait_ge(var_ready, seq + 1)
                nc.scalar.activation(tok_rs[:, 0:NT], tok_rs[:, 0:NT], ACT.Sqrt).then_inc(sd_ready, 1)
                if spread:
                    act.wait_ge(spread_mm, seq + 1)
                    nc.scalar.copy(halves(rstd[:]), ps[:, 2:4, 0:HT]).then_inc(rstd_ready, 1)

            def load_root_table():
                nc.scalar.activation(root_dummy[:], ident[:, 0:1], ACT.Sqrt)

            def modulate(nth):
                act.wait_ge(scales_ready, nth + 1)
                for k in range(KD):
                    act.wait_ge(hn_ready, nth * 8 + k + 1)
                    if k >= 2:
                        act.wait_ge(h_ready, nth * 8 + k - 1)
                    for grp, a, b in ((0, 0, TC), (1, TC, T)):
                        ins = nc.scalar.activation(square[k % 2][:, a:b], scratch[k % 2][:, a:b], ACT.Identity,
                                                   bias=mods[:, 24 * nth + k, grp:grp + 1],
                                                   scale=scales[:, nth, k, grp:grp + 1])
                    ins.then_inc(hf_ready, 1)

            def ffn(f):
                base, J = TILE_FFN[f], NJ * f

                def hidden(j, par, first):
                    w_high(j * 2 + (base + 1), 1, first=(f == 0 and first and par == 0))
                    if f == 0 and (par == 1 or not first):
                        ada_load(act, j, 1)
                    act.wait_ge(tile_done, j * 2 + (base + 1))
                    if not first:
                        act.wait_ge(act_ready, j + (J - 1))
                    nc.scalar.activation(halves(silu_g[par][:]), ps[:, 4 * par:4 * par + 2, 0:HT],
                                         ACT.Silu).then_inc(silu_ready, 1)
                    w_high(j * 2 + (base + 2), 0)
                    act.wait_ge(act_ready, j + (J + 1))
                    nc.scalar.copy(pick(act_hi, j), act_f[par][:]).then_inc(acthi_ready, 1)
                    if f == 0:
                        ada_load(act, j + 1, 0)

                hidden(0, 0, True)
                hidden(1, 1, True)
                with act.Fori(0, NJ // 2 - 1) as i:
                    for k in range(2):
                        hidden(i * 2 + (2 + k), k, False)
                for hf in range(2):
                    n = base + N_IN + 11 * hf
                    with act.Fori(0, 5) as i:
                        for k in range(2):
                            w_high(i * 2 + (n + 1 + k), (n + 1 + k) % 2)
                    if n + 11 < N_TILES:
                        w_high(n + 11, (n + 11) % 2)
                    if hf == 1:
                        load_root_table()
                    for k in range(4 * hf, 4 * hf + 4):
                        square_of(k, SEQ[f], X_BASE[f])

            act.wait_ge(cols_turned, 2)
            nc.scalar.copy(cols_a[:], ps[:, 0, 0:120]).then_inc(cols_ready, 1)
            nc.scalar.copy(cols_b[:], ps[:, 1, 0:62]).then_inc(cols_ready, 1)
            act.wait_ge(cols_ready, 2)
            nc.scalar.activation(cond[:, :, 1], cols_a[:, 72:80], ACT.Silu).then_inc(cond_ready, 1)
            nc.scalar.activation(cond[:, :, 0], cols_a[:, 80:88], ACT.Silu).then_inc(cond_ready, 1)
            for i in range(2 * NT):
                t, q = i // 2, i % 2
                act.wait_ge(x_turned, i + 1)
                nc.scalar.copy(x_t[:, 4 * q:4 * q + 4, t * P:(t + 1) * P], heads4(ps[:, 2 + i % 4, :], P)).then_inc(x_copied, 1)
            act.wait_ge(x_copied, 2 * NT)
            load_root_table()
            for k in range(KD):
                square_of(k, 0, None)
            norm(0)
            w_high(0, 0, first=True)
            act.wait_ge(ada_used, ADA_PE)
            for n in range(0, ADA_PE, 4):
                end = min(n + 4, ADA_PE)
                ins = nc.scalar.copy(ada_row[:, n * P:end * P], ps[0:2, 4 + n // 4, 0:(end - n) * P])
            ins.then_inc(ada_rows, 1)
            modulate(0)
            ffn(0)
            norm(1)
            modulate(1)

            def to_conv(m, k):
                w_high(m + (TILE_WIN + 1), 1 - k)
                act.wait_ge(tile_done, m + (TILE_WIN + 1))
                for grp, half, col, tok, ln in SEGS:
                    a = 2 + tok + 2 * grp
                    ins = nc.scalar.copy(pick(pre, m, slice(a, a + ln)), ps[:, 2 * k + half, col:col + ln])
                ins.then_inc(proj_out, 1)

            def from_conv(m, k):
                act.wait_ge(conv_ready, m + 1)
                nc.scalar.activation(pick(pre, m, slice(0, TC)), conv_acc[k][:, 0:TC], ACT.Silu)
                nc.scalar.activation(pick(pre, m, slice(TC, T)), conv_acc[k][:, TC + 2:T + 2], ACT.Silu)\
                    .then_inc(conv_silu, 1)

            act.wait_ge(pads_set, 3)
            to_conv(0, 0)
            to_conv(1, 1)
            from_conv(0, 0)
            with act.Fori(0, 5) as i:
                for k in range(2):
                    to_conv(i * 2 + (2 + k), k)
                    from_conv(i * 2 + (1 + k), 1 - k)
            act.wait_ge(mix_in, 16 * 11)
            for m in range(12, 28):
                if m < 27:
                    w_high(TILE_WIN + m + 1, (m + 1) % 2)
                if m == 12:
                    from_conv(11, 1)
                if m < 24:
                    act.wait_ge(tile_done, TILE_WIN + m + 1)
                    src = ps[:, 2 * (m % 2):2 * (m % 2) + 2, 0:HT]
                if m < 16:
                    nc.scalar.activation(halves(z_t[:, m - 12, :]), src, ACT.Silu).then_inc(proj_out, 1)
                elif m < 24:
                    dst = q_b[:, m - 16, :] if m < 20 else k_b[:, m - 20, :]
                    nc.scalar.copy(halves(dst), src).then_inc(proj_out, 1)
                if m == 12:
                    nc.scalar.copy(gate_hi[:], gate_w[:]).then_inc(gate_split, 1)
                if m == 13:
                    act.wait_ge(gate_mm, 1)
                    nc.scalar.copy(halves(gate_fm), ps[0:NDB, 4:6, 0:HT]).then_inc(gate_copied, 1)
                if m == 15:
                    act.wait_ge(sc_dve, 1)
                    nc.scalar.activation(sp_a[:], sp_a[:], ACT.Exp, scale=-1.0).then_inc(sc_act, 1)
                    nc.scalar.activation(beta[:], beta[:], ACT.Exp, scale=-1.0).then_inc(sc_act, 1)
                    nc.scalar.activation(vecs[:, 2, :], vecs[:, 0, :], ACT.Exp).then_inc(sc_act, 1)
                    nc.scalar.activation(lam_t[:, 2:4], lam_t[:, 0:2], ACT.Exp).then_inc(sc_act, 1)
                if m == 16:
                    act.wait_ge(sc_dve, 2)
                    nc.scalar.activation(sp_a[:], sp_a[:], ACT.Ln).then_inc(sc_act, 1)
                if m == 18:
                    act.wait_ge(sc_dve, 4)
                    nc.scalar.activation(egc[:], gc[:], ACT.Exp).then_inc(sc_act, 1)
                    nc.scalar.activation(ekg[:], ekg[:], ACT.Exp).then_inc(sc_act, 1)
                    nc.scalar.activation(gl[:], gl[:], ACT.Exp).then_inc(sc_act, 1)
                if 14 <= m < 22:
                    i = m - 14
                    if i == 0:
                        act.wait_ge(conv_silu, 12)
                    if i >= 2:
                        act.wait_ge(l2_mm, i - 1)
                    nc.scalar.activation(square[i % 2][:], pre[:, i, 0:T], ACT.Square).then_inc(l2_sq, 1)
                if 16 <= m < 24:
                    i = m - 16
                    act.wait_ge(l2_var, i + 1)
                    nc.scalar.activation(scratch[i % 2][:], scratch[i % 2][:], ACT.Sqrt).then_inc(l2_sd, 1)
                if m == 25:
                    act.wait_ge(kt_turned, 1)
                    nc.scalar.copy(nk_tok[:], ps[:, 6, :]).then_inc(kt_copied, 1)
                if m == 27:
                    act.wait_ge(kt_turned, 2)
                    nc.scalar.copy(k_all[:, :, 0:P], heads4(ps[:, 6, :], P)).then_inc(kt_copied, 1)
            act.wait_ge(tile_done, TILE_WBV + 4)
            for t in range(NT):
                ins = nc.scalar.copy(v_b[:, t, :], ps[:, t, :])
            ins.then_inc(vb_ready, 1)

            def weights_out(v):
                nk = ATT_UNITS[v][2]
                act.wait_ge(s_turn, v + 1)
                if v >= 1:
                    act.wait_ge(s_pv, v)
                if nk == P:
                    nc.scalar.copy(att_wt[:, 0:P], ps[:, 4, 0:P]).then_inc(s_turned, 1)
                else:
                    nc.scalar.copy(att_wt[:, 0:512], ps[:, 4, :])
                    nc.scalar.copy(att_wt[:, 512:T], ps[:, 5, 0:P]).then_inc(s_turned, 1)

            act.wait_ge(rot_done, 8)
            def exponentials(v):
                nk = ATT_UNITS[v][2]
                for m in range(2):
                    act.wait_ge(s_max, 2 * v + m + 1)
                    if m == 0 and v >= 2:
                        act.wait_ge(s_wts, v - 1)
                    x = att_p[v % 2][m]
                    if nk == P:
                        src, dst = ps[:, 2 * m, 0:P], x[:, 0:P]
                    else:
                        src, dst = ps[:, 2 * m:2 * m + 2, 0:HT], halves(x[:, 0:T])
                    nc.scalar.activation(dst, src, ACT.Exp, bias=att_s[:, v % 2, m:m + 1], scale=DK ** -0.5,
                                         accum_out=att_s[:, v % 2, 2 + m:3 + m]).then_inc(s_exp, 1)

            for v in range(NORM_END):
                if v < NU:
                    exponentials(v)
                if 2 <= v <= NU + 1:
                    weights_out(v - 2)
                j, k = norm_at(v)
                if k == 0:
                    act.wait_ge(s_out, 4 * j + 4)
                    nc.scalar.activation(heads4(square[0][:, 0:512], P), heads4_of(att_q, j), ACT.Square).then_inc(an_sq, 1)
                if k == 1:
                    act.wait_ge(an_var, j + 1)
                    nc.scalar.activation(tok_rs[:, 0:4], tok_rs[:, 0:4], ACT.Sqrt).then_inc(an_sd, 1)
                if k == 3:
                    act.wait_ge(an_tmp, j + 1)
                    nc.scalar.copy(heads4_of(h_hi[1], j), heads4(scratch[0][:, 0:512], P)).then_inc(an_hi, 1)

            act.wait_ge(an_done, 5)
            act.wait_ge(kv_out, 32)
            for i in range(2 * NT):
                act.wait_ge(kv_turned, i + 1)
                nc.scalar.copy((k_tok, v_tok)[i % 2][:, i // 2, :], ps[:, 4 + i % 4, :]).then_inc(kv_copied, 1)
            for k, c, r, t, g in make_schedule():
                if k == 0:
                    if r >= 1:
                        act.wait_ge(t_pe[c], r * PE_T)
                    for d, x, m in ((0, m_t[c], "after"), (1, tt_cols[c], "before")):
                        for h in range(4):
                            q = 8 * d + 4 * g + h
                            ins = nc.scalar.activation(x[:, h, :], const(m), ACT.Copy, scale=beta[:, t, q:q + 1])
                        ins.then_inc(t_act[c], 1)
                if k == 3:
                    act.wait_ge(t_dve[c], r * DVE_T + 3)
                    nc.scalar.activation(x_w[c][:], x_w[c][:], ACT.Exp).then_inc(t_act[c], 1)
            for c in range(4):
                act.wait_ge(t_pe[c], ROUNDS[c] * PE_T)
            for m in range(2):
                w_high(TILE_WOUT + m, m)
            for s in range(NT):
                for b in range(4):
                    act.wait_ge(c_dve[b], s * DVE_C[b] + 1)
                    if s >= 1:
                        act.wait_ge(o_added[b], s)
                    for h in range(4):
                        q = 8 * (b // 2) + 4 * (b % 2) + h
                        ins = nc.scalar.activation(oq[b][:, h * DK:(h + 1) * DK], ps[:, 4 + b, 256 + h * DK:256 + (h + 1) * DK],
                                                   ACT.Copy, scale=egc[:, tile_of(s, b // 2), q:q + 1])
                    ins.then_inc(c_act[b], 1)
            load_root_table()
            for p, t in enumerate(OUT_ORDER):
                if p in (0, OUT_EARLY):
                    for b in range(4):
                        act.wait_ge(o_added[b], NT - 1 if p == 0 else NT)
                nc.scalar.activation(sq_o[t], o_acc[:, t, :], ACT.Square).then_inc(o_act, 1)
                if p in (OUT_EARLY - 1, NT - 1):
                    for i in range(0 if p < OUT_EARLY else OUT_EARLY, p + 1):
                        act.wait_ge(o_dve, i + 1)
                        x = o_sum[:, OUT_ORDER[i], :]
                        nc.scalar.activation(x, x, ACT.Sqrt).then_inc(o_sd, 1)
            for p, t in enumerate(OUT_ORDER):
                act.wait_ge(o_scaled, p + 1)
                nc.scalar.copy(h_hi[0][:, :, t * P:(t + 1) * P], heads4(scratch[p % 2][:, 0:512], P)).then_inc(o_hi, 1)
            load_root_table()
            for m in range(8):
                if m >= 1:
                    w_high(TILE_WOUT + m + 1, (m + 1) % 2)
                square_of(m, 2, 8)
            norm(2)
            modulate(2)
            act.wait_ge(st_out, 64)
            ffn(1)
            norm(3, spread=False)
            act.wait_ge(tokrs_ready, 4)
            for i in range(0, 2 * NT, 2):
                t, q = i % NT, i // NT
                act.wait_ge(y_turned, i + 1)
                nc.scalar.activation(y_tok[:, t, q * 512:q * 512 + 512], ps[:, 1 + i % 7, :], ACT.Copy,
                                     scale=tok_rs[:, t:t + 1]).then_inc(y_copied[0], 1)

        @block.vector
        def _(dve):
            own = Chain(dve, dve_own)

            def w_low(n, s):
                dve.wait_ge(w_hi_ready, n + 1)
                nc.vector.tensor_tensor(w_lo[s][:], w_raw[s][:], w_hi[s][:].bitcast(F32), ALU.subtract)\
                    .then_inc(w_lo_ready, 1)

            def add_square(k, seq):
                dve.wait_ge(sq_ready, seq * 8 + k + 1)
                if k == 0:
                    if seq >= 1:
                        dve.wait_ge(mean_mm, seq)
                    nc.vector.tensor_copy(sumsq[:], square[0][:]).then_inc(sq_added, 1)
                else:
                    dve.wait_ge(sq_added, seq * 8 + k)
                    nc.vector.tensor_tensor(sumsq[:], sumsq[:], square[k % 2][:], ALU.add).then_inc(sq_added, 1)

            def norm(seq):
                dve.wait_ge(mean_mm, seq + 1)
                nc.vector.tensor_scalar(tok_rs[:, 0:NT], ps[:, 0, 0:NT], EPS, None, ALU.add).then_inc(var_ready, 1)
                dve.wait_ge(sd_ready, seq + 1)
                nc.vector.reciprocal(tok_rs[:, 0:NT], tok_rs[:, 0:NT]).then_inc(tokrs_ready, 1)

            def modulate(nth):
                if nth >= 1:
                    dve.wait_ge(mods_ready, NJ + nth)
                nc.vector.scalar_tensor_tensor(scales[:, nth], mods[:, 24 * nth + 8:24 * nth + 16, :], 1.0,
                                               spread(cols_a[:, 88 + 8 * nth:96 + 8 * nth], 2),
                                               op0=ALU.add, op1=ALU.mult).then_inc(scales_ready, 1)
                for k in range(KD):
                    dve.wait_ge(hf_ready, nth * 8 + k + 1)
                    hi, lo = h_hi[k // 4][:, k % 4, :], h_lo[k // 4][:, k % 4, :]
                    own.link(nc.vector.tensor_copy(hi, square[k % 2][:]))
                    nc.vector.tensor_tensor(lo, square[k % 2][:], hi.bitcast(F32), ALU.subtract).then_inc(h_ready, 1)

            def update_x(m, banks, gate):
                for grp, half, col, tok, ln in SEGS:
                    ins = nc.vector.scalar_tensor_tensor(x_t[:, m, tok:tok + ln], ps[:, banks + half, col:col + ln],
                                                         mods[:, gate * KD + m, grp:grp + 1], x_t[:, m, tok:tok + ln],
                                                         op0=ALU.mult, op1=ALU.add)
                ins.then_inc(x_updated, 1)

            def ada_terms(acc, tile, ks, k0, last):
                for k in ks:
                    for g in range(2):
                        at = (k - k0) * PAIR
                        w, a, col = tile[:, at:at + PAIR], acc[:, g * PAIR:(g + 1) * PAIR], cond[:, k, g:g + 1]
                        if k == 0:
                            ins = nc.vector.tensor_scalar(a, w, col, None, ALU.mult)
                        else:
                            if k > k0:
                                own.wait_back(1)
                            ins = nc.vector.scalar_tensor_tensor(a, w, col, a, op0=ALU.mult, op1=ALU.add)
                        if (k, g) == (last, 1):
                            return ins
                        own.mark(ins)

            def ada_part(i, q, acc, ks=None):
                ks = ks or range(4 * q, 4 * q + 4)
                dve.wait_ge(ada_in[q], i * 16 + 16)
                if ks[0] == 4:
                    dve.wait_ge(ada_read, i * 2 + 1)
                ins = ada_terms(acc, ada_ffn[q], ks, 4 * q, 4 * q + 3)
                if ins is not None:
                    ins.then_inc(ada_read, 1)

            def mods_of(i, bank, n):
                m = i * 2 + 2 * KD
                at = slice(m, m + 2 * n) if isinstance(i, int) else bass.ds(m, 2 * n)
                nc.vector.tensor_tensor(mods[:, at, :], ps[:, bank, 400:400 + 4 * n].rearrange("p (m a) -> p m a", a=2),
                                        spread(cols_a[:, at], 2), ALU.add).then_inc(mods_ready, 1)

            def ffn(f):
                base, J = TILE_FFN[f], NJ * f

                def hidden(j, par, first=False):
                    w_low(j * 2 + (base + 1), 1)
                    w_low(j * 2 + (base + 2), 0)
                    if f == 0:
                        if not first:
                            dve.wait_ge(ada_summed, j + ADA_DVE)
                        ada_part(j, 0, ada_acc)
                        ada_part(j, 1, ada_acc, range(4, 6))
                    dve.wait_ge(tile_done, j * 2 + (base + 2))
                    if f == 0 and not first:
                        mods_of(j - 1, 4 * par + 2, 1)
                    dve.wait_ge(silu_ready, j + (J + 1))
                    nc.vector.tensor_tensor(halves(act_f[par][:]), halves(silu_g[par][:]),
                                            ps[:, 4 * par + 2:4 * par + 4, 0:HT], ALU.mult).then_inc(act_ready, 1)
                    if f == 0:
                        ada_part(j, 1, ada_acc, range(6, 8))
                    dve.wait_ge(acthi_ready, j + (J + 1))
                    nc.vector.tensor_tensor(pick(act_lo, j), act_f[par][:], pick(act_hi, j).bitcast(F32),
                                            ALU.subtract).then_inc(actlo_ready, 1)

                if f == 0:
                    hidden(0, 0, first=True)
                    hidden(1, 1)
                    with dve.Fori(0, NJ // 2 - 1) as i:
                        own.loop(i, 2 * ADA_MARKS)
                        for k in range(2):
                            hidden(i * 2 + (2 + k), k)
                        own.done(NJ // 2 - 1)
                else:
                    with dve.Fori(0, NJ // 2) as i:
                        for k in range(2):
                            hidden(i * 2 + k, k)
                gate = mods[:, (2 + 6 * f) * KD:(3 + 6 * f) * KD, :]
                if f == 0:
                    dve.wait_ge(mods_ready, NJ - 1)
                own.link(nc.vector.tensor_scalar(gate, gate, 0.5, None, ALU.mult))
                for hf in range(2):
                    n = base + N_IN + 11 * hf
                    if f == 0:
                        dve.wait_ge(ada_summed, ADA_DVE + NJ + 3 * hf)
                        for i in range(1, 11):
                            w_low(n + i, (n + i) % 2)
                            if i <= 6:
                                ada_part(NJ + 3 * hf + (i - 1) // 2, (i - 1) % 2, ada_accs[(i - 1) // 2])
                    else:
                        with dve.Fori(0, 5) as i:
                            for k in range(2):
                                w_low(i * 2 + (n + 1 + k), (n + 1 + k) % 2)
                    if n + 11 < N_TILES:
                        w_low(n + 11, (n + 11) % 2)
                    for mm in range(4):
                        if mm == 3:
                            dve.wait_ge(tile_done, n + 11)
                        elif f == 0 and mm == 0:
                            dve.wait_ge(ada_summed, ADA_DVE + NJ + 3 * (hf + 1))
                            mods_of(NJ + 3 * hf, 0, 3)
                        else:
                            dve.wait_ge(down_done, mm + 2 * hf if f == 0 else 4 + mm + 1 + 3 * hf)
                        if f == 0 and mm == 3 and hf == 0:
                            mods_of(NJ - 1, 6, 1)
                        update_x(4 * hf + mm, 2 * mm, 2 + 6 * f)
                        if mm >= 1:
                            add_square(4 * hf + mm - 1, SEQ[f])
                    add_square(4 * hf + 3, SEQ[f])
                    if f == 1:
                        for k in range(4 * hf, 4 * hf + 4):
                            nc.vector.tensor_scalar(x_t[:, k, :], x_t[:, k, :], cols_a[:, 112 + k:113 + k], None,
                                                    ALU.mult).then_inc(y_scaled, 1)

            nc.vector.memset(ones_col[:], 1.0)
            nc.vector.memset(ones_d[:], 1.0 / D).then_inc(ones_set, 1)
            def ada_setup(i):
                dve.wait_ge(ada_wide_in[i], 16)
                ada_terms(ada_wide_acc[i], ada_wide[i], range(KD), 0, KD - 1).then_inc(ada_wide_read, 1)

            dve.wait_ge(cond_ready, 2)
            ada_setup(0)
            for k in range(KD):
                add_square(k, 0)
            ada_setup(1)
            norm(0)
            ada_setup(2)
            w_low(0, 0)
            dve.wait_ge(cols_ready, 2)
            dve.wait_ge(ada_turned, 1)
            dve.wait_ge(ada_summed, ADA_DVE)
            own.link(nc.vector.tensor_tensor(mods[:, 0:2 * KD, :], ps[:, 7, 0:4 * KD].rearrange("p (m a) -> p m a", a=2),
                                             spread(cols_a[:, 0:2 * KD], 2), ALU.add))
            modulate(0)
            ffn(0)
            norm(1)
            modulate(1)

            def conv(m, k):
                w_low(m + (TILE_WIN + 1), 1 - k)
                dve.wait_ge(proj_out, m + 1)
                if not isinstance(m, int) or m >= 2:
                    dve.wait_ge(conv_silu, m - 1)
                tap = lambda t: cols_b[:, bass.ds(m + 12 * t, 1)] if not isinstance(m, int) else cols_b[:, m + 12 * t:m + 12 * t + 1]
                own.link(nc.vector.tensor_scalar(conv_acc[k][:], pick(pre, m, slice(0, T + 2)), tap(0), None, ALU.mult))
                for t in range(1, CONV):
                    ins = nc.vector.scalar_tensor_tensor(conv_acc[k][:], pick(pre, m, slice(t, t + T + 2)), tap(t),
                                                         conv_acc[k][:], op0=ALU.mult, op1=ALU.add)
                    if t < CONV - 1:
                        own.link(ins)
                ins.then_inc(conv_ready, 1)

            conv(0, 0)
            conv(1, 1)
            with dve.Fori(0, 5) as i:
                own.loop(i, 2 * (CONV - 1))
                for k in range(2):
                    conv(i * 2 + (2 + k), k)
                own.done(5)
            def l2_mean(i):
                dve.wait_ge(l2_mm, i + 1)
                if i >= 2:
                    dve.wait_ge(l2_done, i - 1)
                nc.vector.tensor_scalar(halves(scratch[i % 2][:]), ps[:, 4:6, 0:HT], EPS, None, ALU.add).then_inc(l2_var, 1)

            def l2_scale(i):
                dve.wait_ge(l2_sd, i + 1)
                own.link(nc.vector.reciprocal(scratch[i % 2][:], scratch[i % 2][:]))
                nc.vector.scalar_tensor_tensor(pre[:, i, 0:T], pre[:, i, 0:T], DK ** -0.5 if i < 4 else 1.0,
                                               scratch[i % 2][:], op0=ALU.mult, op1=ALU.mult).then_inc(l2_done, 1)

            def rotate(r):
                dst = q_b[:, r % 4, TC:T] if r < 4 else k_all[:, r % 4, TC:T]
                dve.wait_ge(rot_mm, r + 1)
                own.link(nc.vector.tensor_tensor(rot_sin[r % 2][:, 0:TS], ps[:, 7, :], rope_sb[:, TS:2 * TS], ALU.mult))
                dve.wait_ge(rot_cos, r + 1)
                nc.vector.tensor_tensor(dst, rot_sin[r % 2][:, 0:TS], conv_acc[r % 2][:, 0:TS], ALU.add).then_inc(rot_done, 1)

            dve.wait_ge(mix_in, 16 * 11)
            for m in range(12, 28):
                if m < 27:
                    w_low(TILE_WIN + m + 1, (m + 1) % 2)
                if m == 12:
                    dve.wait_ge(gate_split, 1)
                    nc.vector.tensor_tensor(gate_lo[:], gate_w[:], gate_hi[:].bitcast(F32), ALU.subtract).then_inc(gate_split, 1)
                if m == 14:
                    dve.wait_ge(gate_mm, 2)
                    raw = ps[:, 6, 0:NT * NDB].rearrange("p (t n) -> p t n", t=NT)
                    own.link(nc.vector.tensor_tensor(sp_b[:], raw[:, :, 0:16], vecs[:, 1:2, :].broadcast_to([P, NT, 16]), ALU.add))
                    own.link(nc.vector.scalar_tensor_tensor(sp_a[:], sp_b[:], -1.0, sp_b[:], op0=ALU.mult, op1=ALU.max))
                    own.link(nc.vector.tensor_copy(beta[:], raw[:, :, 16:32]))
                    own.link(nc.vector.tensor_tensor(lam_in[:, 0:2, :], lam_in[:, 0:4:2, :], lam_in[:, 1:4:2, :], ALU.mult))
                    nc.vector.tensor_reduce(lam_t[:, 0:2], lam_in[:, 0:2, :], AX.X, ALU.add).then_inc(sc_dve, 1)
                if m == 15:
                    dve.wait_ge(sc_act, 4)
                    nc.vector.tensor_scalar(sp_a[:], sp_a[:], 1.0, None, ALU.add).then_inc(sc_dve, 1)
                    own.link(nc.vector.tensor_scalar(beta[:], beta[:], 1.0, None, ALU.add))
                    own.link(nc.vector.reciprocal(beta[:], beta[:]))
                    own.link(nc.vector.tensor_tensor(lam_t[:, 4:5], lam_t[:, 2:3], lam_t[:, 3:4], ALU.subtract))
                    own.link(nc.vector.tensor_scalar(lam_t[:, 4:5], lam_t[:, 4:5], LAM_INIT, None, ALU.add))
                    nc.vector.tensor_scalar(dn_col[:], cols_b[:, 61:62], 1.0 - LAM_INIT, None, ALU.mult)
                if m == 16:
                    dve.wait_ge(sc_act, 5)
                    own.link(nc.vector.scalar_tensor_tensor(sp_a[:], sp_b[:], 0.0, sp_a[:], op0=ALU.max, op1=ALU.add))
                    nc.vector.scalar_tensor_tensor(g_t[:], sp_a[:], -1.0, vecs[:, 2:3, :].broadcast_to([P, NT, 16]),
                                                   op0=ALU.mult, op1=ALU.mult).then_inc(sc_dve, 1)
                if m == 17:
                    dve.wait_ge(sc_pe, 1)
                    sums = ps[:, 6, 0:240]
                    for d in range(2):
                        own.link(nc.vector.tensor_copy(gc[:, :, 8 * d:8 * d + 8],
                                                       sums[:, 40 * d:40 * d + 40].rearrange("p (t n) -> p t n", t=NT)))
                    total = sums[:, 80:160].rearrange("p (t n) -> p t n", t=NT)
                    own.link(nc.vector.tensor_copy(gl[:], total))
                    nc.vector.tensor_tensor(ekg[:], total, gc[:], ALU.subtract).then_inc(sc_dve, 1)
                if 15 <= m < 23:
                    l2_mean(m - 15)
                if 16 <= m < 24:
                    l2_scale(m - 16)
                if m >= 20:
                    rotate(m - 20)

            def att_max(v, m):
                nk = ATT_UNITS[v][2]
                dve.wait_ge(s_mm, 2 * v + m + 1)
                src = ps[:, 2 * m, 0:P] if nk == P else ps[:, 2 * m:2 * m + 2, 0:HT]
                own.link(nc.vector.tensor_reduce(att_s[:, v % 2, 6 + m:7 + m], src, AX.X if nk == P else AX.XY, ALU.max))
                nc.vector.tensor_scalar(att_s[:, v % 2, m:m + 1], att_s[:, v % 2, 6 + m:7 + m], -DK ** -0.5, None,
                                        ALU.mult).then_inc(s_max, 1)

            def att_weights(v):
                nk, a = ATT_UNITS[v][2], att_s[:, v % 2, :]
                dve.wait_ge(s_exp, 2 * v + 2)
                own.link(nc.vector.reciprocal(a[:, 4:6], a[:, 2:4]))
                own.link(nc.vector.tensor_tensor(a[:, 5:6], a[:, 5:6], lam_t[:, 4:5], ALU.mult))
                own.link(nc.vector.tensor_scalar(att_v[:, 0:nk], att_p[v % 2][1][:, 0:nk], a[:, 5:6], None, ALU.mult))
                if v >= 2:
                    dve.wait_ge(s_turn, v - 1)
                nc.vector.scalar_tensor_tensor(att_w[v % 2][:, 0:nk], att_p[v % 2][0][:, 0:nk], a[:, 4:5], att_v[:, 0:nk],
                                               op0=ALU.mult, op1=ALU.subtract).then_inc(s_wts, 1)

            def att_out(v):
                hb, q0, nk = ATT_UNITS[v]
                dve.wait_ge(s_pv, v + 1)
                nc.vector.tensor_copy(att_q[:, hb, q0:q0 + P], ps[:, 6, 0:P]).then_inc(s_out, 1)

            att_max(0, 0)
            att_max(0, 1)
            for v in range(NORM_END):
                j, k = norm_at(v)
                if k == 2:
                    dve.wait_ge(an_sd, j + 1)
                    nc.vector.reciprocal(tok_rs[:, 0:4], tok_rs[:, 0:4]).then_inc(an_rs, 1)
                if v + 1 < NU:
                    att_max(v + 1, 0)
                if v < NU:
                    att_weights(v)
                if v + 1 < NU:
                    att_max(v + 1, 1)
                if 2 <= v <= NU + 1:
                    att_out(v - 2)
                if k == 1:
                    dve.wait_ge(an_mm, j + 1)
                    nc.vector.tensor_scalar(tok_rs[:, 0:4], ps[:, 7, 0:4], D / P, EPS, ALU.mult, ALU.add).then_inc(an_var, 1)
                if k == 2:
                    dve.wait_ge(an_spread, j + 1)
                    nc.vector.scalar_tensor_tensor(heads4(scratch[0][:, 0:512], P), heads4_of(att_q, j), dn_col[:],
                                                   heads4(ps[:, 7, :], P), op0=ALU.mult, op1=ALU.mult).then_inc(an_tmp, 1)
                if k == 3:
                    dve.wait_ge(an_hi, j + 1)
                    nc.vector.tensor_tensor(heads4_of(h_lo[1], j), heads4(scratch[0][:, 0:512], P),
                                            heads4_of(h_hi[1], j).bitcast(F32), ALU.subtract).then_inc(an_done, 1)

            dve.wait_ge(sc_act, 8)
            dve.wait_ge(st_clear, 3)
            def where(s, b):
                d, g = b // 2, b % 2
                return d, g, tile_of(s, d), 8 * d + 4 * g

            for k, c, r, t, g in make_schedule():
                pe0, bank = r * PE_T, 2 * c
                if k == 1:
                    for d, x, m in ((0, x_w[c], "after"), (1, t_cols[c], "before")):
                        q = 8 * d + 4 * g
                        dve.wait_ge(t_pe[c], pe0 + 1 + d)
                        for h in range(4):
                            ins = nc.vector.scalar_tensor_tensor(x[:, h, :], ps[:, bank + d, h * P:(h + 1) * P],
                                                                 gc[:, t, q + h:q + h + 1], const(m),
                                                                 op0=ALU.subtract, op1=ALU.mult)
                        ins.then_inc(t_dve[c], 1)
                if k == 2:
                    dve.wait_ge(t_dve[c], r * DVE_T + 2)
                    nc.vector.tensor_tensor(x_w[c][:], x_w[c][:], t_cols[c][:], ALU.add).then_inc(t_dve[c], 1)
                if k == 5:
                    dve.wait_ge(t_pe[c], pe0 + 4)
                    dve.wait_ge(t_pool[c], r * POOL_T + 2)
                    nc.vector.tensor_tensor(m_t[c][:], heads4(ps[:, bank, :], P), tt_cols[c][:], ALU.mult).then_inc(t_dve[c], 1)
                    dve.wait_ge(t_pe[c], pe0 + 6)
                    nc.vector.tensor_tensor(heads4(p_all[:, t, g, :], P), heads4(ps[:, bank + 1, :], P), x_w[c][:],
                                            ALU.mult).then_inc(t_dve[c], 1)
                n, part = divmod(k - 6, 3)
                if n >= 1 and part == 0:
                    dve.wait_ge(t_pe[c], pe0 + 8 + 3 * (n - 1))
                    nc.vector.tensor_tensor(x_w[c][:], heads4(ps[:, bank, :], P), over4(const(f"level{n}")),
                                            ALU.mult).then_inc(t_dve[c], 1)
                if n >= 1 and part == 1:
                    dve.wait_ge(t_pe[c], pe0 + 9 + 3 * (n - 1))
                    dve.wait_ge(t_pool[c], r * POOL_T + 4 + n)
                    nc.vector.tensor_tensor(t_all[:, t, g, :], t_all[:, t, g, :], ps[:, bank, :],
                                            ALU.subtract).then_inc(t_dve[c], 1)
                if n >= 0 and part == 2 and n < 6:
                    dve.wait_ge(t_pe[c], pe0 + 7 + 3 * n)
                    nc.vector.tensor_tensor(t_cols[c][:], heads4(ps[:, bank, :], P), over4(const(f"sides{n + 1}")),
                                            ALU.mult).then_inc(t_dve[c], 1)

            def scan_a(s, b):
                d, g, t, q = where(s, b)
                dve.wait_ge(c_pe[b], s * PE_C + 1)
                nc.vector.tensor_tensor(heads4(r_s[b][:], DK), heads4(ps[:, 4 + b, 0:256], DK),
                                        spread(egc[:, t, q:q + 4], DK), ALU.mult).then_inc(c_dve[b], 1)
                dve.wait_ge(c_dve[b], s * DVE_C[b] + 1)
                nc.vector.tensor_tensor(r_s[b][:], v_tok[:, t, g * 256:g * 256 + 256], r_s[b][:],
                                        ALU.subtract).then_inc(c_dve[b], 1)

            def one_p(s, b):
                d, g, t, q = where(s, b)
                if s == 0:
                    for c in range(2):
                        dve.wait_ge(t_pe[c], ROUNDS[c] * PE_T)
                nc.vector.tensor_tensor(p_one[b][:], heads4(p_all[:, t, g, :], P), over4(const(("tri_f", "tri_b")[d])),
                                        ALU.mult).then_inc(c_dve[b], 1)

            def scan_b(s, b):
                d, g, t, q = where(s, b)
                dve.wait_ge(c_pe[b], s * PE_C + 2)
                nc.vector.tensor_tensor(heads4(u_s[b][:], DK), heads4(ps[:, 4 + b, 0:256], DK),
                                        spread(beta[:, t, q:q + 4], DK), ALU.mult).then_inc(c_dve[b], 1)

            def scan_c(s, b):
                d, g, t, q = where(s, b)
                S = st[0 if s == 0 else 1]
                if s == 1:
                    dve.wait_ge(st_in, 64)
                dve.wait_ge(c_pe[b], s * PE_C + 3)
                for h in range(4):
                    cc, e = h // 2, h % 2
                    rows, cols = slice(e * DK, e * DK + DK), slice(e * DK, e * DK + DK)
                    ins = nc.vector.scalar_tensor_tensor(
                        S[rows, d, 2 * g + cc, cols], S[rows, d, 2 * g + cc, cols], gl[rows, t, q + h:q + h + 1],
                        ps[rows, 4 + b, cc * P + e * DK:cc * P + e * DK + DK], op0=ALU.mult, op1=ALU.add)
                ins.then_inc(c_dve[b], 1)
                nc.vector.tensor_tensor(oq[b], oq[b], ps[:, 4 + b, 256:512], ALU.add).then_inc(c_dve[b], 1)

            def o_mean(p):
                x = o_sum[:, OUT_ORDER[p], :]
                dve.wait_ge(o_act, p + 1)
                own.link(nc.vector.tensor_reduce(x, heads4(sq_o[OUT_ORDER[p]], DK), AX.X, ALU.add))
                nc.vector.tensor_scalar(x, x, 1.0 / DK, EPS, ALU.mult, ALU.add).then_inc(o_dve, 1)

            def o_norm(p):
                t = OUT_ORDER[p]
                x = o_sum[:, t, :]
                dve.wait_ge(o_sd, p + 1)
                own.link(nc.vector.reciprocal(x, x))
                nc.vector.tensor_tensor(heads4(o_acc[:, t, :], DK), heads4(o_acc[:, t, :], DK), spread(x, DK),
                                        ALU.mult).then_inc(o_normed, 1)

            def o_gate(p):
                t = OUT_ORDER[p]
                dve.wait_ge(o_pe, p + 1)
                if p >= 2:
                    dve.wait_ge(o_lo, p - 1)
                nc.vector.scalar_tensor_tensor(heads4(scratch[p % 2][:, 0:512], P), heads4(ps[:, 4 + p % 4, :], P),
                                               cols_b[:, 60:61], z_t[:, :, t * P:(t + 1) * P],
                                               op0=ALU.mult, op1=ALU.mult).then_inc(o_scaled, 1)

            def o_low(p):
                t = OUT_ORDER[p]
                dve.wait_ge(o_hi, p + 1)
                nc.vector.tensor_tensor(h_lo[0][:, :, t * P:(t + 1) * P], heads4(scratch[p % 2][:, 0:512], P),
                                        h_hi[0][:, :, t * P:(t + 1) * P].bitcast(F32), ALU.subtract).then_inc(o_lo, 1)

            for s in range(NT):
                if s == 1:
                    for m in range(2):
                        w_low(TILE_WOUT + m, m)
                for stage, slots in ((scan_a, 4), (one_p, 2), (scan_b, 4), (scan_c, 4)):
                    if s == NT - 1 and stage is scan_c:
                        for p in range(OUT_EARLY):
                            o_mean(p)
                    for b in range(slots):
                        stage(s, b)
            for p in range(OUT_EARLY):
                o_norm(p)
            for p in range(OUT_EARLY, NT):
                o_mean(p)
            o_gate(0)
            o_gate(1)
            for p in range(OUT_EARLY, NT):
                o_norm(p)
            for p in range(NT):
                o_low(p)
                if p + 2 < NT:
                    o_gate(p + 2)
            for m in range(8):
                if m >= 1:
                    w_low(TILE_WOUT + m + 1, (m + 1) % 2)
                dve.wait_ge(tile_done, TILE_WOUT + m + 1)
                update_x(m, 2 * (m % 2), 5)
                add_square(m, 2)
            norm(2)
            modulate(2)
            ffn(1)
            norm(3)
            dve.wait_ge(tokrs_ready, 4)
            for i in range(1, 2 * NT, 2):
                t, q = i % NT, i // NT
                dve.wait_ge(y_turned, i + 1)
                nc.vector.tensor_scalar(y_tok[:, t, q * 512:q * 512 + 512], ps[:, 1 + i % 7, :], tok_rs[:, t:t + 1], None,
                                        ALU.mult).then_inc(y_copied[1], 1)

        @block.gpsimd
        def _(pool):
            own = Chain(pool, pool_own)

            def scale_x(nth, seq):
                pool.wait_ge(rstd_ready, seq + 1)
                for k in range(KD):
                    if k >= 2:
                        pool.wait_ge(hf_ready, nth * 8 + k - 1)
                    nc.gpsimd.tensor_tensor(scratch[k % 2][:], x_t[:, k, :], rstd[:], ALU.mult).then_inc(hn_ready, 1)

            scale_x(0, 0)
            scale_x(1, 1)
            pool.wait_ge(tile_done, FFN_TILES)
            for a in (0, TC + 2, T + 4):
                nc.gpsimd.memset(pre[:, :, a:a + 2], 0.0).then_inc(pads_set, 1)
            nc.gpsimd.memset(ones_1[:], 1.0).then_inc(pads_set, 1)
            pool.wait_ge(mix_in, 16 * 11)
            pool.wait_ge(conv_silu, 12)
            for r in range(8):
                pool.wait_ge(proj_out, 17 + r)
                src = q_b[:, r % 4, TC:T] if r < 4 else k_b[:, r % 4, TC:T]
                if r >= 2:
                    pool.wait_ge(rot_done, r - 1)
                nc.gpsimd.tensor_tensor(conv_acc[r % 2][:, 0:TS], src, rope_sb[:, 0:TS], ALU.mult).then_inc(rot_cos, 1)
            pool.wait_ge(an_done, 5)
            pool.wait_ge(kv_out, 32)
            nc.gpsimd.memset(st[0][:], 0.0).then_inc(st_clear, 1)
            nc.gpsimd.memset(st[1][:], 0.0).then_inc(st_clear, 1)
            pool.wait_ge(kv_copied, 2 * NT)
            nc.gpsimd.memset(o_acc, 0.0).then_inc(st_clear, 1)
            for k, c, r, t, g in make_schedule():
                tt, dve0, pool0 = heads4(t_all[:, t, g, :], P), r * DVE_T, r * POOL_T
                if k == 2:
                    pool.wait_ge(t_act[c], r * ACT_T + 2)
                    nc.gpsimd.tensor_tensor(tt_cols[c][:], tt_cols[c][:], m_t[c][:], ALU.add).then_inc(t_pool[c], 1)
                if k == 4:
                    pool.wait_ge(t_act[c], r * ACT_T + 3)
                    pool.wait_ge(t_pool[c], pool0 + 1)
                    nc.gpsimd.tensor_tensor(tt_cols[c][:], tt_cols[c][:], x_w[c][:], ALU.mult).then_inc(t_pool[c], 1)
                if k == 6:
                    pool.wait_ge(t_dve[c], dve0 + 4)
                    nc.gpsimd.tensor_tensor(tt, m_t[c][:], over4(const("level0")), ALU.mult).then_inc(t_pool[c], 1)
                if k == 7:
                    pool.wait_ge(t_pool[c], pool0 + 3)
                    nc.gpsimd.tensor_tensor(tt, over4(const("ident")), tt, ALU.subtract).then_inc(t_pool[c], 1)
                if k >= 8 and k % 3 == 2 and k < 24:
                    n = (k - 5) // 3
                    if n == 1:
                        pool.wait_ge(t_pool[c], pool0 + 4)
                    else:
                        pool.wait_ge(t_dve[c], dve0 + 8 + 3 * (n - 2))
                    nc.gpsimd.tensor_tensor(tt_cols[c][:], tt, over4(const(f"sides{n}")), ALU.mult).then_inc(t_pool[c], 1)
            for c in range(4):
                pool.wait_ge(t_dve[c], ROUNDS[c] * DVE_T)
            def add_out(s, b):
                t, g = tile_of(s, b // 2), b % 2
                pool.wait_ge(c_dve[b], (s + 1) * DVE_C[b])
                out = o_acc[:, t, g * 256:g * 256 + 256]
                if b >= 2 and s == 0:
                    pool.wait_ge(o_added[b - 2], 1)
                elif s > NT - s:
                    pool.wait_ge(o_added[(b + 2) % 4], NT - s + 1)
                nc.gpsimd.tensor_tensor(out, out, oq[b], ALU.add).then_inc(o_added[b], 1)

            pool.wait_ge(st_clear, 3)
            for s in range(NT):
                for b in range(4):
                    t, g = tile_of(s, b // 2), b % 2
                    if s >= 1:
                        pool.wait_ge(c_pe[b], (s - 1) * PE_C + 2)
                    nc.gpsimd.tensor_tensor(t_one[b][:], heads4(t_all[:, t, g, :], P), over4(const(("tri_f", "tri_b")[b // 2])),
                                            ALU.mult).then_inc(c_pool[b], 1)
                for b in range(4):
                    if s >= 1:
                        add_out(s - 1, b)
                    d, t, g = b // 2, tile_of(s, b // 2), b % 2
                    if s >= 1:
                        pool.wait_ge(c_pe[b], s * PE_C)
                    nc.gpsimd.tensor_tensor(heads4(kg[b], DK), heads4(k_tok[:, t, g * 256:g * 256 + 256], DK),
                                            spread(ekg[:, t, 8 * d + 4 * g:8 * d + 4 * g + 4], DK), ALU.mult)\
                        .then_inc(c_pool[b], 1)
                    if b >= 2:
                        nc.gpsimd.tensor_tensor(p_one[b][:], heads4(p_all[:, t, g, :], P),
                                                over4(const(("tri_f", "tri_b")[d])), ALU.mult).then_inc(c_pool[b], 1)
            for b in range(4):
                add_out(NT - 1, b)
            scale_x(2, 2)

        @block.tensor
        def _(pe):
            def product(out, k0, weights, x_parts, start, stop):
                hi, lo = weights
                xh, xl = x_parts
                nc.tensor.matmul(out, lo, xh, start=start, stop=False)
                nc.tensor.matmul(out, hi, xl, start=False, stop=False)
                return nc.tensor.matmul(out, hi, xh, start=False, stop=stop)

            def dense(s, banks, per_k=None, ks=range(KD), first=0, last=KD - 1):
                for k in ks:
                    if per_k is not None:
                        pe.wait_ge(h_ready, per_k + k + 1)
                    w = (w_hi[s][:, k * P:(k + 1) * P], w_lo[s][:, k * P:(k + 1) * P])
                    for half in range(2):
                        x = [h[k // 4][:, k % 4, half * HT:half * HT + HT] for h in (h_hi, h_lo)]
                        ins = product(ps[:, banks + half, 0:HT], k, w, x, k == first, k == last)
                return ins

            def mean(seq):
                pe.wait_ge(sq_added, 8 * (seq + 1))
                for t in range(NT):
                    ins = nc.tensor.matmul(ps[:, 0, t:t + 1], sumsq[:, t * P:(t + 1) * P], ones_d[:, 0:1], start=True, stop=True)
                ins.then_inc(mean_mm, 1)

            def spread_rs(seq):
                pe.wait_ge(tokrs_ready, seq + 1)
                for t in range(NT):
                    for a, b in ((t * P, min(t * P + P, HT)), (max(t * P, HT), t * P + P)):
                        if a < b:
                            bank, at = 2 + a // HT, a % HT
                            ins = nc.tensor.matmul(ps[:, bank, at:at + b - a], tok_rs[:, t:t + 1].broadcast_to([P, P]),
                                                   ident[:, a - t * P:b - t * P], start=True, stop=True)
                ins.then_inc(spread_mm, 1)

            def ada(n):
                pe.wait_ge(ada_landed[n], 16)
                for a in range(KD):
                    ins = nc.tensor.matmul(ps[0:2, 4 + n // 4, (n % 4) * P:(n % 4 + 1) * P], cond[:, a, :],
                                           ada_tiles[n][:, a * P:(a + 1) * P], start=(a == 0), stop=(a == KD - 1))
                ins.then_inc(ada_used, 1)

            def ada_sum(bank, at, acc):
                for u in range(2):
                    for g in range(2):
                        c = at + 2 * u + g
                        ins = nc.tensor.matmul(ps[:, bank, c:c + 1], acc[:, g * PAIR + u * P:g * PAIR + (u + 1) * P],
                                               ones_col[:], start=True, stop=True)
                ins.then_inc(ada_summed, 1)

            def ffn(f):
                base, J = TILE_FFN[f], NJ * f

                def hidden(j, par, first):
                    pe.wait_ge(w_lo_ready, j * 2 + (base + 1))
                    if not first:
                        pe.wait_ge(silu_ready, j + (J - 1))
                    dense(0, 4 * par, 16 * f if first and par == 0 else None).then_inc(tile_done, 1)
                    pe.wait_ge(w_lo_ready, j * 2 + (base + 2))
                    if not first:
                        pe.wait_ge(act_ready, j + (J - 1))
                    if f == 0 and (par == 1 or not first):
                        pe.wait_ge(ada_read, j * 2)
                        ada_sum(4 * par + 2, 400, ada_acc)
                    dense(1, 4 * par + 2).then_inc(tile_done, 1)

                def down(n, s, j, mm_wait, start, stop, hf, before_last=None):
                    pe.wait_ge(w_lo_ready, n + 1)
                    order = [(jj, mm) for jj in range(2) for mm in range(4)]
                    if stop:
                        order.sort(key=lambda x: x[1])
                    for jj, mm in order:
                        if start and hf == 0 and jj == 0 and mm == 2:
                            pe.wait_ge(silu_ready, NJ * (f + 1))
                        if start and hf == 0 and jj == 0 and mm == 3:
                            pe.wait_ge(act_ready, NJ * (f + 1))
                        if before_last is not None and jj == 0 and mm == 3:
                            before_last()
                        if mm_wait is not None and jj == 0:
                            pe.wait_ge(x_updated, mm_wait + mm + 1)
                        at = jj * 512 + mm * P
                        w = (w_hi[s][:, at:at + P], w_lo[s][:, at:at + P])
                        for half in range(2):
                            x = [pick(a, j + jj, slice(half * HT, half * HT + HT)) for a in (act_hi, act_lo)]
                            ins = product(ps[:, 2 * mm + half, 0:HT], None, w, x, start and jj == 0, stop and jj == 1)
                        if stop and jj == 1:
                            if mm == 0 and f == 0:
                                pe.wait_ge(ada_read, 2 * (NJ + 3 + 3 * hf))
                                for i in range(3):
                                    ada_sum(0, 400 + 4 * i, ada_accs[i])
                            if mm == 3:
                                ins.then_inc(tile_done, 1)
                            elif mm > 0 or f == 1:
                                ins.then_inc(down_done, 1)
                    if not stop:
                        ins.then_inc(tile_done, 1)

                hidden(0, 0, True)
                hidden(1, 1, True)
                with pe.Fori(0, NJ // 2 - 1) as i:
                    for k in range(2):
                        hidden(i * 2 + (2 + k), k, False)
                pe.wait_ge(actlo_ready, NJ * (f + 1) - 1)
                for hf in range(2):
                    n = base + N_IN + 11 * hf
                    def last_pair():
                        pe.wait_ge(ada_read, 2 * NJ)
                        ada_sum(6, 400, ada_acc)

                    down(n, n % 2, 0, X_BASE[f] if hf else None, True, False, hf, last_pair if f == 0 and hf == 0 else None)
                    with pe.Fori(0, 4) as i:
                        for k in range(2):
                            down(i * 2 + (n + 1 + k), (n + 1 + k) % 2, i * 4 + (2 + 2 * k), None, False, False, hf)
                    down(n + 9, (n + 9) % 2, 18, None, False, False, hf)
                    pe.wait_ge(actlo_ready, NJ * (f + 1))
                    down(n + 10, (n + 10) % 2, 20, None, False, True, hf)

            pe.wait_ge(small_in, 16 * 12)
            nc.tensor.transpose(ps[:, 0, 0:120], rows_a[:], ident[0:120, 0:120]).then_inc(cols_turned, 1)
            nc.tensor.transpose(ps[:, 1, 0:62], rows_b[:], ident[0:62, 0:62]).then_inc(cols_turned, 1)
            pe.wait_ge(x_in, 32)
            for i in range(2 * NT):
                t, q = i // 2, i % 2
                if i >= 4:
                    pe.wait_ge(x_copied, i - 3)
                for a in range(4):
                    ins = nc.tensor.transpose(ps[:, 2 + i % 4, a * P:(a + 1) * P], x_tok[:, t, (4 * q + a) * P:(4 * q + a + 1) * P],
                                              ident[:])
                ins.then_inc(x_turned, 1)
            pe.wait_ge(cond_ready, 2)
            pe.wait_ge(ones_set, 1)
            pe.wait_ge(x_copied, 2 * NT)
            for n in range(ADA_PE):
                if n == 5:
                    mean(0)
                if n == 7:
                    spread_rs(0)
                ada(n)
            for i in range(ADA_DVE):
                pe.wait_ge(ada_wide_read, i + 1)
                ada_sum(7, 2 * ADA_PE + 4 * i, ada_wide_acc[i])
            pe.wait_ge(ada_rows, 1)
            for n in range(ADA_PE):
                ins = nc.tensor.transpose(ps[:, 7, 2 * n:2 * n + 2], ada_row[:, n * P:(n + 1) * P], ident[0:2, 0:2])
            ins.then_inc(ada_turned, 1)
            ffn(0)
            mean(1)
            spread_rs(1)
            pe.wait_ge(w_lo_ready, TILE_WIN + 1)
            dense(0, 0, 8).then_inc(tile_done, 1)
            pe.wait_ge(w_lo_ready, TILE_WIN + 2)
            dense(1, 2).then_inc(tile_done, 1)
            with pe.Fori(0, 5) as i:
                for k in range(2):
                    pe.wait_ge(w_lo_ready, i * 2 + (TILE_WIN + 3 + k))
                    pe.wait_ge(proj_out, i * 2 + (1 + k))
                    dense(k, 2 * k).then_inc(tile_done, 1)

            def values(q):
                s = q % 2
                for kk in range(2):
                    k = 2 * q + kk
                    w = [x[s][:, kk * 512:kk * 512 + 512] for x in (w_hi, w_lo)]
                    for t in range(NT):
                        hh, hl = [h[k // 4][:, k % 4, t * P:(t + 1) * P] for h in (h_hi, h_lo)]
                        out = ps[:, t, :]
                        nc.tensor.matmul(out, hl, w[0], start=(k == 0), stop=False)
                        nc.tensor.matmul(out, hh, w[1], start=False, stop=False)
                        ins = nc.tensor.matmul(out, hh, w[0], start=False, stop=(k == KD - 1))
                ins.then_inc(tile_done, 1)

            def gates():
                pe.wait_ge(gate_split, 2)
                for half in range(2):
                    for k in range(KD):
                        x = [h[k // 4][:, k % 4, half * HT:half * HT + HT] for h in (h_hi, h_lo)]
                        w = [g[:, k * NDB:(k + 1) * NDB] for g in (gate_hi, gate_lo)]
                        ins = product(ps[0:NDB, 4 + half, 0:HT], k, w, x, k == 0, k == KD - 1)
                ins.then_inc(gate_mm, 1)

            def gates_turn():
                pe.wait_ge(gate_copied, 1)
                for t in range(NT):
                    ins = nc.tensor.transpose(ps[:, 6, t * NDB:(t + 1) * NDB], gate_fm[:, t * P:(t + 1) * P],
                                              ident[0:NDB, 0:NDB])
                ins.then_inc(gate_mm, 1)

            def decays():
                pe.wait_ge(sc_dve, 3)
                pe.wait_ge(pads_set, 4)
                for lhs, at, cols in ((const("tri_f"), 0, slice(0, 8)), (const("tri_b"), 40, slice(8, 16)),
                                      (ones_1[:], 80, slice(0, 16))):
                    n = NT * (cols.stop - cols.start)
                    ins = nc.tensor.matmul(ps[:, 6, at:at + n].rearrange("p (t n) -> p t n", t=NT), lhs, g_t[:, :, cols],
                                           start=True, stop=True)
                ins.then_inc(sc_pe, 1)

            for m in range(12, 28):
                pe.wait_ge(w_lo_ready, TILE_WIN + m + 1)
                if m < 24:
                    pe.wait_ge(proj_out, m - 1)
                    dense(m % 2, 2 * (m % 2)).then_inc(tile_done, 1)
                else:
                    if m == 24:
                        pe.wait_ge(proj_out, 24)
                        pe.wait_ge(l2_var, 8)
                    values(m - 24)
                if m == 13:
                    pe.wait_ge(mix_in, 16 * 11)
                    gates()
                if m == 14:
                    gates_turn()
                if m == 17:
                    decays()
                if 15 <= m < 23:
                    i = m - 15
                    pe.wait_ge(l2_sq, i + 1)
                    if i >= 1:
                        pe.wait_ge(l2_var, i)
                    for half in range(2):
                        ins = nc.tensor.matmul(ps[:, 4 + half, 0:HT], const("headones"),
                                               square[i % 2][:, half * HT:half * HT + HT], start=True, stop=True)
                    ins.then_inc(l2_mm, 1)
                if m >= 20:
                    r = m - 20
                    src = q_b[:, r % 4, TC:T] if r < 4 else k_b[:, r % 4, TC:T]
                    pe.wait_ge(proj_out, 17 + r)
                    if r >= 1:
                        pe.wait_ge(rot_done, r)
                    nc.tensor.matmul(ps[:, 7, :], const("perm"), src, start=True, stop=True).then_inc(rot_mm, 1)
                if m in (24, 26):
                    pe.wait_ge(sc_dve, 4)
                    if m == 26:
                        pe.wait_ge(kt_copied, 1)
                    for hb in range(HB):
                        x = k_b[:, hb, 0:P] if m == 24 else ck_tok[:, hb * P:(hb + 1) * P]
                        ins = nc.tensor.transpose(ps[:, 6, hb * P:(hb + 1) * P], x, ident[:])
                    ins.then_inc(kt_turned, 1)

            def scores(v):
                hb, q0, nk = ATT_UNITS[v]
                for m in range(2):
                    if v >= 1:
                        pe.wait_ge(s_exp, 2 * v - 1 + m)
                    rows = slice(m * DK, m * DK + DK)
                    q = q_b[rows, hb, q0:q0 + P]
                    if nk == P:
                        ins = nc.tensor.matmul(ps[:, 2 * m, 0:P], q, k_b[rows, hb, 0:P], start=True, stop=True)
                    else:
                        for half in range(2):
                            ins = nc.tensor.matmul(ps[:, 2 * m + half, 0:HT], q, k_all[rows, hb, half * HT:half * HT + HT],
                                                   start=True, stop=True)
                    ins.then_inc(s_mm, 1)

            def turn(v):
                nk = ATT_UNITS[v][2]
                pe.wait_ge(s_wts, v + 1)
                if v >= 1:
                    pe.wait_ge(s_turned, v)
                for kt in range(nk // P):
                    ins = nc.tensor.transpose(ps[:, 4 + kt // 4, (kt % 4) * P:(kt % 4 + 1) * P], att_w[v % 2][:, kt * P:(kt + 1) * P],
                                              ident[:])
                ins.then_inc(s_turn, 1)

            def weigh(v):
                hb, q0, nk = ATT_UNITS[v]
                pe.wait_ge(s_turned, v + 1)
                if v >= 1:
                    pe.wait_ge(s_out, v)
                for kt in range(nk // P):
                    vals = cv_tok[:, hb * P:(hb + 1) * P] if nk > P and kt == 0 else v_b[:, kt, hb * P:(hb + 1) * P]
                    ins = nc.tensor.matmul(ps[:, 6, 0:P], vals, att_wt[:, kt * P:(kt + 1) * P],
                                           start=(kt == 0), stop=(kt == nk // P - 1))
                ins.then_inc(s_pv, 1)

            pe.wait_ge(kt_copied, 2)
            pe.wait_ge(rot_done, 8)
            pe.wait_ge(vb_ready, 1)
            scores(0)
            for v in range(NORM_END):
                j, k = norm_at(v)
                if k == 2:
                    pe.wait_ge(an_rs, j + 1)
                    for i in range(4):
                        ins = nc.tensor.matmul(ps[:, 7, i * P:(i + 1) * P], tok_rs[:, i:i + 1].broadcast_to([P, P]), ident[:],
                                               start=True, stop=True)
                    ins.then_inc(an_spread, 1)
                if v + 1 < NU:
                    scores(v + 1)
                if 2 <= v <= NU + 1:
                    weigh(v - 2)
                if 1 <= v <= NU:
                    turn(v - 1)
                if k == 0:
                    pe.wait_ge(an_sq, j + 1)
                    if j >= 1:
                        pe.wait_ge(an_tmp, j)
                    for i in range(4):
                        ins = nc.tensor.matmul(ps[:, 7, i:i + 1], square[0][:, i * P:(i + 1) * P], ones_d[:, 0:1],
                                               start=True, stop=True)
                    ins.then_inc(an_mm, 1)

            pe.wait_ge(l2_done, 8)
            for i in range(2 * NT):
                if i == 3:
                    pe.wait_ge(an_tmp, 5)
                if i >= 4:
                    pe.wait_ge(kv_copied, i - 3)
                for a in range(4):
                    ins = nc.tensor.transpose(ps[:, 4 + i % 4, a * P:(a + 1) * P],
                                              pre[:, 4 + 4 * (i % 2) + a, (i // 2) * P:(i // 2 + 1) * P], ident[:])
                ins.then_inc(kv_turned, 1)
            pe.wait_ge(an_done, 5)

            def qk(t, g, h, which):
                rows = slice((h % 2) * DK, (h % 2) * DK + DK)
                return pre[rows, which + 2 * g + h // 2, t * P:(t + 1) * P]

            def products(t, g, c, bank, which, e):
                for h in (e, e + 2):
                    ins = nc.tensor.matmul(ps[:, bank, h * P:(h + 1) * P], qk(t, g, h, 4), qk(t, g, h, which),
                                           start=True, stop=True)
                ins.then_inc(t_pe[c], 1)

            def four(c, op):
                for h in range(4):
                    ins = op(ps[:, 2 * c, h * P:(h + 1) * P], h)
                ins.then_inc(t_pe[c], 1)

            for k, c, r, t, g in make_schedule():
                dve0, pool0, bank = r * DVE_T, r * POOL_T, 2 * c
                if k == 0:
                    if r >= 1:
                        pe.wait_ge(t_dve[c], dve0)
                    elif c >= 2:
                        pe.wait_ge(kv_copied, 2 * NT)
                    for d in range(2):
                        for h in range(4):
                            col = g_t[:, t, 8 * d + 4 * g + h:8 * d + 4 * g + h + 1]
                            ins = nc.tensor.matmul(ps[:, bank + d, h * P:(h + 1) * P], col.broadcast_to([P, P]),
                                                   const(("tri_f", "tri_b")[d]), start=True, stop=True)
                        ins.then_inc(t_pe[c], 1)
                if k == 2:
                    pe.wait_ge(t_dve[c], dve0 + 1)
                    products(t, g, c, bank, 4, 0)
                if k == 3:
                    pe.wait_ge(t_pe[c], r * PE_T + 3)
                    products(t, g, c, bank, 4, 1)
                    pe.wait_ge(t_dve[c], dve0 + 2)
                    products(t, g, c, bank + 1, 0, 0)
                if k == 4:
                    pe.wait_ge(t_pe[c], r * PE_T + 5)
                    products(t, g, c, bank + 1, 0, 1)
                if k == 8:
                    pe.wait_ge(t_pool[c], pool0 + 4)
                    four(c, lambda out, h: nc.tensor.transpose(out, t_all[:, t, g, h * P:(h + 1) * P], ident[:]))
                n, part = divmod(k - 6, 3)
                if n >= 1 and part == 0:
                    pe.wait_ge(t_dve[c], dve0 + 6 + 3 * (n - 1))
                    four(c, lambda out, h: nc.tensor.matmul(out, m_t[c][:, h, :], t_cols[c][:, h, :], start=True, stop=True))
                if n >= 1 and part == 1:
                    pe.wait_ge(t_dve[c], dve0 + 7 + 3 * (n - 1))
                    pe.wait_ge(t_pool[c], pool0 + 4 + n)
                    four(c, lambda out, h: nc.tensor.matmul(out, x_w[c][:, h, :], tt_cols[c][:, h, :], start=True, stop=True))
                if n >= 1 and part == 2:
                    pe.wait_ge(t_dve[c], dve0 + 8 + 3 * (n - 1))
                    four(c, lambda out, h: nc.tensor.transpose(out, t_all[:, t, g, h * P:(h + 1) * P], ident[:]))

            def scan_a(s, b):
                d, g = b // 2, b % 2
                t, S = tile_of(s, d), st[0 if s == 0 else 1]
                if s == 0:
                    pe.wait_ge(st_clear, 3)
                    for c in (2, 3):
                        pe.wait_ge(t_dve[c], ROUNDS[c] * DVE_T)
                else:
                    pe.wait_ge(c_dve[b], s * DVE_C[b])
                if s == 1:
                    pe.wait_ge(st_in, 64)
                for which, at in ((4, 0), (0, 256)):
                    for cc in range(2):
                        ins = nc.tensor.matmul(ps[:, 4 + b, at + cc * P:at + cc * P + P],
                                               pre[:, which + 2 * g + cc, t * P:(t + 1) * P], S[:, d, 2 * g + cc, :],
                                               start=True, stop=True)
                ins.then_inc(c_pe[b], 1)

            def scan_b(s, b):
                pe.wait_ge(c_dve[b], s * DVE_C[b] + 2)
                pe.wait_ge(c_act[b], s + 1)
                pe.wait_ge(c_pool[b], s * POOL_C[b] + 1)
                for h in range(4):
                    ins = nc.tensor.matmul(ps[:, 4 + b, h * DK:(h + 1) * DK], t_one[b][:, h, :],
                                           r_s[b][:, h * DK:(h + 1) * DK], start=True, stop=True)
                ins.then_inc(c_pe[b], 1)

            def scan_c(s, b):
                pe.wait_ge(c_dve[b], (s + 1) * DVE_C[b] - 2)
                pe.wait_ge(c_pool[b], (s + 1) * POOL_C[b])
                for cc in range(2):
                    nc.tensor.matmul(ps[:, 4 + b, cc * P:(cc + 1) * P], kg[b][:, cc * P:(cc + 1) * P],
                                     u_s[b][:, cc * P:(cc + 1) * P], start=True, stop=True)
                for h in range(4):
                    ins = nc.tensor.matmul(ps[:, 4 + b, 256 + h * DK:256 + (h + 1) * DK], p_one[b][:, h, :],
                                           u_s[b][:, h * DK:(h + 1) * DK], start=True, stop=True)
                ins.then_inc(c_pe[b], 1)

            for s in range(NT):
                for stage in (scan_a, scan_b, scan_c):
                    for b in range(4):
                        stage(s, b)
            def turn_out(p):
                t = OUT_ORDER[p]
                pe.wait_ge(o_normed, p + 1)
                if p < 4:
                    pe.wait_ge(c_dve[p], NT * DVE_C[p])
                else:
                    pe.wait_ge(o_scaled, p - 3)
                for a in range(4):
                    ins = nc.tensor.transpose(ps[:, 4 + p % 4, a * P:(a + 1) * P], o_acc[:, t, a * P:(a + 1) * P], ident[:])
                ins.then_inc(o_pe, 1)

            for p in range(OUT_EARLY):
                turn_out(p)
            for m in range(2):
                pe.wait_ge(w_lo_ready, TILE_WOUT + m + 1)
                dense(m, 2 * m, ks=range(4, KD), first=4, last=None)
                if m == 0:
                    for p in range(OUT_EARLY, NT):
                        turn_out(p)
            pe.wait_ge(o_lo, NT)
            for m in range(2):
                dense(m, 2 * m, ks=range(4), first=None, last=3).then_inc(tile_done, 1)
            with pe.Fori(0, 3) as i:
                for k in range(2):
                    pe.wait_ge(w_lo_ready, i * 2 + (TILE_WOUT + 3 + k))
                    pe.wait_ge(x_updated, i * 2 + (8 + 1 + k))
                    dense(k, 2 * k).then_inc(tile_done, 1)
            mean(2)
            spread_rs(2)
            ffn(1)
            pe.wait_ge(x_updated, X_BASE[1] + 8)
            for i in range(2 * NT):
                t, q = i % NT, i // NT
                if i == NT:
                    mean(3)
                if q == 0 or i == NT:
                    pe.wait_ge(y_scaled, 4 * q + 4)
                if i >= 7:
                    pe.wait_ge(y_copied[(i - 7) % 2], (i - 7) // 2 + 1)
                for a in range(4):
                    ins = nc.tensor.transpose(ps[:, 1 + i % 7, a * P:(a + 1) * P], x_t[:, 4 * q + a, t * P:(t + 1) * P], ident[:])
                ins.then_inc(y_turned, 1)


_INS = ['x_prompt', 'x_sample', 'cache_diff_k', 'cache_diff_v', 'state_delta', 'c', 'c_ctx', 'w_ada', 'b_ada',
        'norm_ffn1', 'w_ffn1_in', 'w_ffn1_out', 'norm_mix', 'w_in', 'conv_w', 'a_log', 'dt_bias', 'delta_norm',
        'lambda_q1', 'lambda_k1', 'lambda_q2', 'lambda_k2', 'diff_norm', 'w_out', 'norm_ffn2', 'w_ffn2_in',
        'w_ffn2_out', 'norm_final']
_OUTS = [(1, TC, D), (1, TS, D), (TC, HB * P), (TC, HB * P), (2, HA, DK, DK)]


def kernel(**inputs):
    import concourse.bacc as bacc
    from concourse.bass_utils import run_bass_kernel_spmd

    nc = bacc.Bacc("TRN2", target_bir_lowering=False, num_devices=1, dynamic_dma_scratch_size=1024)
    arrays, args = {}, []
    tables = dict(zip(("consts", "rope"), shape_constants()))
    for name in _INS + ["consts", "rope"]:
        a = np.ascontiguousarray(tables[name] if name in tables else inputs[name])
        arrays[f"in_{name}"] = a
        args.append(nc.dram_tensor(f"in_{name}", a.shape, F32, kind="ExternalInput").ap())
    for i, shape in enumerate(_OUTS):
        args.append(nc.dram_tensor(f"out_{i}", shape, F32, kind="ExternalOutput").ap())
    hybrid_step(nc, *args)
    r = run_bass_kernel_spmd(nc, [arrays], core_ids=[0])
    y_p, y_s, nk, nv, ns = (r.results[0][f"out_{i}"] for i in range(len(_OUTS)))
    return (y_p, y_s, nk.reshape(1, 1, TC, HB, 2, DK), nv.reshape(1, 1, TC, HB, P),
            ns.reshape(1, 1, 2, HA, DK, DK))
```
